# Optimizing a Trainium2 kernel written in Bass

```python
import jax, jax.numpy as jnp
from jax import lax
import numpy as np

D_MODEL = 1024
BATCH = 1
SEQ = 128
DEPTH = 2
DEC_BATCH = 1
DEC_SEQ = 512
PAST_LEN = 128

GRID_W = 64
N_MIXERS = 2
RET_HEADS = 4
RET_DK = 256
RET_DV = 512
RET_CHUNK = 128
MLA_HEADS = 8
MLA_Q_RANK = 512
MLA_KV_RANK = 256
MLA_NOPE = 128
MLA_ROPE = 64
MLA_V = 128
ROPE_BASE = 10000.0
ATTN_BLOCK = 128
N_EXPERTS = 16
N_GROUPS = 4
EXPERTS_PER_GROUP = N_EXPERTS // N_GROUPS
TOP_K = 2
GROUP_SCORE_K = 2
EXPERT_FF = 256
EPS = 1e-6

kernel_name = "hybrid_retention_mla_moe_diffusion_step"

F32 = jnp.float32

def rmsnorm(x, g):
    xf = x.astype(F32)
    y = xf * lax.rsqrt(jnp.mean(xf * xf, axis=-1, keepdims=True) + EPS)
    return (y * g.astype(F32)).astype(x.dtype)

def head_layernorm(y, g):
    B, H, T, dv = y.shape
    yf = y.astype(F32)
    mu = jnp.mean(yf, axis=-1, keepdims=True)
    var = jnp.mean(jnp.square(yf - mu), axis=-1, keepdims=True)
    yn = ((yf - mu) * lax.rsqrt(var + EPS)).transpose(0, 2, 1, 3).reshape(B, T, H * dv)
    return (yn * g.astype(F32)).astype(y.dtype)

def ada_params(cond, w_ada, b_ada):
    m = jax.nn.silu(cond) @ w_ada + b_ada
    return jnp.split(m[:, None, :], 6, axis=-1)

def retention_scan(q, k, v, log_gamma, s0):
    B, H, T, dk = q.shape
    dv = v.shape[-1]
    C = RET_CHUNK
    nc = T // C
    lg = log_gamma.astype(F32)[:, None]
    pos = jnp.arange(C, dtype=F32)
    diff = pos[:, None] - pos[None, :]
    intra = jnp.where(diff >= 0, jnp.exp(lg[:, :, None] * jnp.maximum(diff, 0.0)), 0.0).astype(q.dtype)
    q_dec = jnp.exp(lg * (pos + 1.0)).astype(q.dtype)[..., None]
    k_dec = jnp.exp(lg * (C - 1.0 - pos)).astype(q.dtype)[..., None]
    c_dec = jnp.exp(lg * C).astype(q.dtype)[:, :, None]

    def chunks(a):
        return jnp.moveaxis(a.reshape(B, H, nc, C, a.shape[-1]), 2, 0)

    def step(s, xs):
        qc, kc, vc = xs
        att = jnp.einsum('bhnd,bhmd->bhnm', qc, kc) * intra
        o = jnp.einsum('bhnm,bhmv->bhnv', att, vc) + jnp.einsum('bhnd,bhdv->bhnv', qc * q_dec, s)
        s = s * c_dec + jnp.einsum('bhmd,bhmv->bhdv', kc * k_dec, vc)
        return s, o

    s_fin, o = lax.scan(step, s0.astype(q.dtype), (chunks(q), chunks(k), chunks(v)))
    o = jnp.moveaxis(o, 0, 2).reshape(B, H, T, dv)
    return o, s_fin

def retention_mixer(h, w_in, decay_param, gn, w_out, s0_f, s0_b):
    B, T, _ = h.shape
    hk = RET_HEADS * RET_DK
    hv = RET_HEADS * RET_DV
    q, k, v, g_f, g_b = jnp.split(h @ w_in, [hk, 2 * hk, 2 * hk + hv, 2 * hk + 2 * hv], axis=-1)

    def heads(a, d):
        return a.reshape(B, T, RET_HEADS, d).transpose(0, 2, 1, 3)

    q = heads(q, RET_DK)
    k = heads(k, RET_DK) * (RET_DK ** -0.5)
    v = heads(v, RET_DV)
    log_gamma = -jnp.exp(decay_param.astype(F32))
    o_f, s_f = retention_scan(q, k, v, log_gamma[0], s0_f)
    flip = lambda a: jnp.flip(a, axis=2)
    o_b, s_b = retention_scan(flip(q), flip(k), flip(v), log_gamma[1], s0_b)
    o_b = flip(o_b)
    y = jax.nn.silu(g_f) * head_layernorm(o_f, gn[0]) + jax.nn.silu(g_b) * head_layernorm(o_b, gn[1])
    return y @ w_out, s_f, s_b

def axial_rope_tables(rows):
    row = jnp.repeat(jnp.arange(rows), GRID_W).astype(F32)
    col = jnp.tile(jnp.arange(GRID_W), rows).astype(F32)
    half = MLA_ROPE // 2
    inv = ROPE_BASE ** (-jnp.arange(0, half, 2, dtype=F32) / half)
    ang = jnp.stack([row[:, None] * inv, col[:, None] * inv], axis=1)[:, :, None, :]
    return jnp.cos(ang), jnp.sin(ang)

def apply_axial_rope(x, cos, sin):
    shp = x.shape
    xr = x.reshape(shp[:-1] + (2, 2, MLA_ROPE // 4))
    x1, x2 = xr[..., 0:1, :], xr[..., 1:2, :]
    cos = cos.astype(x.dtype)
    sin = sin.astype(x.dtype)
    out = jnp.concatenate([x1 * cos - x2 * sin, x2 * cos + x1 * sin], axis=-2)
    return out.reshape(shp)

def mla_project(h, w_in, q_norm, kv_norm, w_uq):
    B, T, _ = h.shape
    cq, ckv, kpe = jnp.split(h @ w_in, [MLA_Q_RANK, MLA_Q_RANK + MLA_KV_RANK], axis=-1)
    q = (rmsnorm(cq, q_norm) @ w_uq).reshape(B, T, MLA_HEADS, MLA_NOPE + MLA_ROPE)
    return q[..., :MLA_NOPE], q[..., MLA_NOPE:], rmsnorm(ckv, kv_norm), kpe

def mla_attend(q_nope, q_pe, ckv, kpe, w_uk, w_uv, w_o):
    k_nope = jnp.einsum('bkr,rhd->bkhd', ckv, w_uk)
    v = jnp.einsum('bkr,rhd->bkhd', ckv, w_uv)
    B, Tq = q_nope.shape[:2]
    nb = Tq // ATTN_BLOCK
    scale = (MLA_NOPE + MLA_ROPE) ** -0.5

    def blk(a):
        return jnp.moveaxis(a.reshape((B, nb, ATTN_BLOCK) + a.shape[2:]), 1, 0)

    def one(xs):
        qn, qp = xs
        s = jnp.einsum('bqhd,bkhd->bhqk', qn, k_nope) + jnp.einsum('bqhd,bkd->bhqk', qp, kpe)
        p = jax.nn.softmax(s.astype(F32) * scale, axis=-1).astype(v.dtype)
        return jnp.einsum('bhqk,bkhd->bqhd', p, v)

    o = lax.map(one, (blk(q_nope), blk(q_pe)))
    o = jnp.moveaxis(o, 0, 1).reshape(B, Tq, MLA_HEADS * MLA_V)
    return o @ w_o

def grouped_moe(h, w_router, router_bias, w_gate, w_up, w_down):
    B, T, D = h.shape
    x = h.reshape(B * T, D)
    s = jax.nn.sigmoid((x @ w_router).astype(F32))
    sb = s + router_bias.astype(F32)
    sbg = sb.reshape(-1, N_GROUPS, EXPERTS_PER_GROUP)
    gscore = jnp.sum(lax.top_k(sbg, GROUP_SCORE_K)[0], axis=-1)
    g = jnp.argmax(gscore, axis=-1)
    gmask = jnp.arange(N_GROUPS)[None, :] == g[:, None]
    masked = jnp.where(gmask[:, :, None], sbg, -jnp.inf).reshape(-1, N_EXPERTS)
    _, eid = lax.top_k(masked, TOP_K)
    w = jnp.take_along_axis(s, eid, axis=1)
    w = w / jnp.sum(w, axis=-1, keepdims=True)
    gate = jnp.sum(jax.nn.one_hot(eid, N_EXPERTS, dtype=F32) * w[..., None], axis=1)
    a = jnp.einsum('nd,edf->nef', x, w_gate)
    u = jnp.einsum('nd,edf->nef', x, w_up)
    act = jax.nn.silu(a) * u * gate[..., None].astype(x.dtype)
    return jnp.einsum('nef,efd->nd', act, w_down).reshape(B, T, D)

def setup_inputs(seed: int = 0) -> dict:
    key = jax.random.key(seed)
    ks = iter(jax.random.split(key, 40))
    nrm = lambda shape, s: jax.random.normal(next(ks), shape, F32) * s
    gain = lambda shape: 1.0 + nrm(shape, 0.02)
    n_ret = (DEPTH + N_MIXERS - 1) // N_MIXERS
    n_mla = DEPTH // N_MIXERS
    hk = RET_HEADS * RET_DK
    hv = RET_HEADS * RET_DV
    base = jnp.asarray(np.log(-np.log(1.0 - 2.0 ** (-5.0 - np.arange(RET_HEADS)))), F32)
    return {
        "x_prompt": nrm((BATCH, SEQ, D_MODEL), 1.0),
        "x_sample": nrm((DEC_BATCH, DEC_SEQ, D_MODEL), 1.0),
        "state_ret_fwd": nrm((DEC_BATCH, n_ret, RET_HEADS, RET_DK, RET_DV), 0.5),
        "state_ret_bwd": nrm((DEC_BATCH, n_ret, RET_HEADS, RET_DK, RET_DV), 0.5),
        "cache_mla_ckv": nrm((DEC_BATCH, n_mla, PAST_LEN, MLA_KV_RANK), 1.0),
        "cache_mla_kpe": nrm((DEC_BATCH, n_mla, PAST_LEN, MLA_ROPE), 1.0),
        "c": nrm((DEC_BATCH, D_MODEL), 1.0),
        "c_ctx": nrm((D_MODEL,), 1.0),
        "w_ada": nrm((DEPTH, D_MODEL, 6 * D_MODEL), 0.5 * D_MODEL ** -0.5),
        "b_ada": nrm((DEPTH, 6 * D_MODEL), 0.02),
        "norm1": gain((DEPTH, D_MODEL)),
        "norm2": gain((DEPTH, D_MODEL)),
        "norm_final": gain((D_MODEL,)),
        "ret_w_in": nrm((n_ret, D_MODEL, 2 * hk + 3 * hv), D_MODEL ** -0.5),
        "ret_decay": base + nrm((n_ret, 2, RET_HEADS), 0.1),
        "ret_gn": gain((n_ret, 2, hv)),
        "ret_w_out": nrm((n_ret, hv, D_MODEL), hv ** -0.5),
        "mla_w_in": nrm((n_mla, D_MODEL, MLA_Q_RANK + MLA_KV_RANK + MLA_ROPE), D_MODEL ** -0.5),
        "mla_q_norm": gain((n_mla, MLA_Q_RANK)),
        "mla_kv_norm": gain((n_mla, MLA_KV_RANK)),
        "mla_w_uq": nrm((n_mla, MLA_Q_RANK, MLA_HEADS * (MLA_NOPE + MLA_ROPE)), MLA_Q_RANK ** -0.5),
        "mla_w_uk": nrm((n_mla, MLA_KV_RANK, MLA_HEADS, MLA_NOPE), MLA_KV_RANK ** -0.5),
        "mla_w_uv": nrm((n_mla, MLA_KV_RANK, MLA_HEADS, MLA_V), MLA_KV_RANK ** -0.5),
        "mla_w_o": nrm((n_mla, MLA_HEADS * MLA_V, D_MODEL), (MLA_HEADS * MLA_V) ** -0.5),
        "w_router": nrm((D_MODEL, N_EXPERTS), D_MODEL ** -0.5),
        "router_bias": nrm((N_EXPERTS,), 0.01),
        "moe_w_gate": nrm((DEPTH, N_EXPERTS, D_MODEL, EXPERT_FF), D_MODEL ** -0.5),
        "moe_w_up": nrm((DEPTH, N_EXPERTS, D_MODEL, EXPERT_FF), D_MODEL ** -0.5),
        "moe_w_down": nrm((DEPTH, N_EXPERTS, EXPERT_FF, D_MODEL), EXPERT_FF ** -0.5),
    }

def reference(x_prompt, x_sample, state_ret_fwd, state_ret_bwd, cache_mla_ckv, cache_mla_kpe, c, c_ctx,
              w_ada, b_ada, norm1, norm2, norm_final,
              ret_w_in, ret_decay, ret_gn, ret_w_out,
              mla_w_in, mla_q_norm, mla_kv_norm, mla_w_uq, mla_w_uk, mla_w_uv, mla_w_o,
              w_router, router_bias, moe_w_gate, moe_w_up, moe_w_down):
    rows = x_sample.shape[1] // GRID_W
    cos, sin = axial_rope_tables(rows)
    xp, xs = x_prompt, x_sample
    ret_f, ret_b, mla_ckv, mla_kpe = [], [], [], []
    for i in range(DEPTH):
        j = i // N_MIXERS
        sh1p, sc1p, g1p, sh2p, sc2p, g2p = ada_params(c_ctx[None, :], w_ada[i], b_ada[i])
        sh1s, sc1s, g1s, sh2s, sc2s, g2s = ada_params(c, w_ada[i], b_ada[i])
        hp = rmsnorm(xp, norm1[i]) * (1.0 + sc1p) + sh1p
        hs = rmsnorm(xs, norm1[i]) * (1.0 + sc1s) + sh1s
        if i % N_MIXERS == 0:
            z = jnp.zeros((xp.shape[0], RET_HEADS, RET_DK, RET_DV), xp.dtype)
            op, sf, sb = retention_mixer(hp, ret_w_in[j], ret_decay[j], ret_gn[j], ret_w_out[j], z, z)
            ret_f.append(sf)
            ret_b.append(sb)
            os_, _, _ = retention_mixer(hs, ret_w_in[j], ret_decay[j], ret_gn[j], ret_w_out[j],
                                        state_ret_fwd[:, j], state_ret_bwd[:, j])
        else:
            qn, qpe, ckv, kpe = mla_project(hp, mla_w_in[j], mla_q_norm[j], mla_kv_norm[j], mla_w_uq[j])
            op = mla_attend(qn, qpe, ckv, kpe, mla_w_uk[j], mla_w_uv[j], mla_w_o[j])
            mla_ckv.append(ckv)
            mla_kpe.append(kpe)
            qn_s, qpe_s, ckv_s, kpe_s = mla_project(hs, mla_w_in[j], mla_q_norm[j], mla_kv_norm[j], mla_w_uq[j])
            qpe_s = apply_axial_rope(qpe_s, cos[:, None], sin[:, None])
            kpe_s = apply_axial_rope(kpe_s, cos, sin)
            ckv_all = jnp.concatenate([ckv_s, cache_mla_ckv[:, j].astype(ckv_s.dtype)], axis=1)
            kpe_all = jnp.concatenate([kpe_s, cache_mla_kpe[:, j].astype(kpe_s.dtype)], axis=1)
            os_ = mla_attend(qn_s, qpe_s, ckv_all, kpe_all, mla_w_uk[j], mla_w_uv[j], mla_w_o[j])
        xp = xp + g1p * op
        xs = xs + g1s * os_
        xp = xp + g2p * grouped_moe(rmsnorm(xp, norm2[i]) * (1.0 + sc2p) + sh2p,
                                    w_router, router_bias, moe_w_gate[i], moe_w_up[i], moe_w_down[i])
        xs = xs + g2s * grouped_moe(rmsnorm(xs, norm2[i]) * (1.0 + sc2s) + sh2s,
                                    w_router, router_bias, moe_w_gate[i], moe_w_up[i], moe_w_down[i])
    y_prompt = rmsnorm(xp, norm_final)
    y_sample = rmsnorm(xs, norm_final)
    return (y_prompt, y_sample, jnp.stack(ret_f, axis=1), jnp.stack(ret_b, axis=1),
            jnp.stack(mla_ckv, axis=1), jnp.stack(mla_kpe, axis=1))


_drawn_inputs = setup_inputs


def setup_inputs(seed=0):
    import zlib

    import numpy as np

    out = dict(_drawn_inputs(seed))
    spreads = {}
    factors = {'cache_mla_ckv': 3.103,
     'cache_mla_kpe': 4.346,
     'norm_final': 2.881,
     'ret_gn': 2.875,
     'mla_q_norm': 8.0,
     'mla_kv_norm': 2.883}
    for name, (base, spread) in spreads.items():
        noise = np.random.default_rng([zlib.crc32(name.encode()), seed]).standard_normal(out[name].shape)
        drawn = base * np.exp(spread * noise) if base else spread * noise
        out[name] = __import__('jax').numpy.asarray(drawn.astype(out[name].dtype))
    for name, factor in factors.items():
        out[name] = (out[name] * factor).astype(out[name].dtype)
    return out
```

```python
from contextlib import ExitStack

import numpy as np

import concourse.bass as bass
from concourse import mybir

F32 = mybir.dt.float32
I32 = mybir.dt.int32
ALU = mybir.AluOpType
ACT = mybir.ActivationFunctionType
AX = mybir.AxisListType

P = 128
D = 1024
KT = D // P
TS = 512
T = 640
NT = T // P
PT = NT - 1
EPS = 1e-6
RH, DK, DV = 4, 256, 512
MH, NOPE, ROPE, QR, KVR, VD = 8, 128, 64, 512, 256, 128
KEYS = TS + P + P
NE, NG, FF = 16, 4, 256
BIG = 1e30
CAP = T
BLK = P
ARENA = 20480 - 768

STEPS = [(0, 0), (3, 1), (1, 0), (2, 1), (2, 0), (1, 1), (3, 0), (0, 1), (4, 0), (4, 1)]
STATE_STEPS = [0, 1, 2, 3, 4, 5, 8, 9]
NSS = len(STATE_STEPS)

CHUNKS_FIRST = {i: i for i in range(8)}
CHUNKS_LOOP = {1: 0, 3: 1, 5: 2, 7: 3}
SLOTS_FIRST = [4, 0, 1, 4, 0, 1, 4, 0]
SLOTS_LOOP = [4, 1, 4, 0]
PRE_CHUNKS = 4
PRE_ORDER = [(kind, c) for c in range(PRE_CHUNKS) for kind in ("part", "sum")]
PRE_SLOTS = (2, 3, 4, 1)
PRE = len(PRE_ORDER)


def use_plan(chunks):
    gate, chunk, total, n = {}, {}, {}, 13
    for i in range(len(STEPS)):
        gate[i] = n
        n += 1
        if i - 1 in chunks:
            total[chunks[i - 1]] = n
            n += 1
        if i in chunks:
            chunk[chunks[i]] = n
            n += 1
    assert n % 4 in (0, 3)
    return gate, chunk, total, n


GATE_F, CHUNK_F, SUM_F, USES_F = use_plan(CHUNKS_FIRST)
GATE_L, CHUNK_L, SUM_L, USES_L = use_plan(CHUNKS_LOOP)
AFTER_CHUNKS = 3


def use_base(h):
    if isinstance(h, int) and h == 0:
        return PRE
    return h * USES_L + (PRE + USES_F - USES_L)


class Count:

    def __init__(self, step=1):
        self.step, self.base, self.n = step, 0, 0

    def next(self, k=1):
        self.n += k
        return self.base + self.n * self.step

    def now(self):
        return self.base + self.n * self.step

    def enter(self, reg, first, per):
        self.start, self.per, self.first = self.base + self.n * self.step, per, first
        self.base, self.n = reg * (per * self.step) + (self.start - first * per * self.step), 0

    def leave(self, last):
        assert self.n == self.per, (self.n, self.per)
        self.base, self.n = self.start + (last - self.first) * self.per * self.step, 0


class Step:

    def __init__(self, reg, per, u):
        self.reg, self.per, self.u = reg, per, u
        self.par = u % 2
        self.buf = u % 4
        self.n = reg * per + u
        self.half = reg * (per // 2) + u // 2
        self.quarter = reg + u // 4 if per == 4 else None

    def plus(self, k):
        return Step(self.reg, self.per, self.u + k)


def fixed(n, per):
    s = Step(0, per, n)
    return s


class Chain:

    def __init__(self, eng, sem):
        self.eng, self.sem, self.c = eng, sem, Count()

    def link(self, ins):
        ins.then_inc(self.sem, 1)
        self.eng.wait_ge(self.sem, self.c.next())


def build(nc, a, out):
    ctx = ExitStack()
    with ctx:
        def sb(name, shape, dt=F32):
            return ctx.enter_context(nc.sbuf_tensor(name, shape, dt))

        sems = {}

        def S(name):
            if name not in sems:
                sems[name] = ctx.enter_context(nc.semaphore(name))
            return sems[name]

        x = sb("x", [P, NT, D])
        wr = sb("wr", [P, 5 * 4096 + KT * T])
        arena = sb("arena", [P, ARENA])
        ident = sb("ident", [P, P])
        ones = sb("ones", [P, P])
        before = sb("before", [P, P])
        vraw = sb("vraw", [P, P])
        vraw2 = sb("vraw2", [20, P])
        vt1 = sb("vt1", [P, P])
        vt2 = sb("vt2", [P, 20])
        mod = sb("mod", [P, 2, 48, 2])
        mod_rows = sb("mod_rows", [96, P])
        a1 = sb("a1", [P, 2, 8, 2])
        cond = sb("cond", [P, KT * 2 + 30])
        stage = sb("stage", [P, 512])
        pick2 = sb("pick2", [P, 2])
        w_rt = sb("w_rt", [P, KT, NE])
        bias_row = sb("bias_row", [P, NE])
        kv_row = sb("kv_row", [P, KVR])
        idx16 = sb("idx16", [P, NE])
        idx16p = sb("idx16p", [P, NE])
        ebase = sb("ebase", [P, NE])
        tok_id = sb("tok_id", [P, NT], I32)
        zero_id = sb("zero_id", [P, NE * CAP // P], I32)
        epsc = sb("epsc", [P, 1])
        half = sb("half", [P, 1])
        lg = sb("lg", [P, 8])
        lgk = sb("lgk", [P, 8])
        kdec = sb("kdec", [P, 8])
        cdec = sb("cdec", [P, 8])
        pf = sb("pf", [P, 2])
        ss = sb("ss", [P, 8])
        rs = sb("rs", [P, 8])
        st6 = sb("st6", [P, 6])
        mv = sb("mv", [P, 2, 2])
        rv = sb("rv", [P, 2])
        smx = sb("smx", [P, 2])
        nmx = sb("nmx", [P, 2])
        sm_sum = sb("sm_sum", [P, NT])
        sm_inv = sb("sm_inv", [P, NT])
        cntf = sb("cntf", [P, 1])
        cnt = sb("cnt", [P, 1], I32)
        slots = sb("slots", [P, 2, NT], I32)
        ids = sb("ids", [P, NE], I32)
        idc = sb("idc", [P, 2], I32)
        wts = sb("wts", [P, 3, NT])
        PSUM = ctx.enter_context(nc.psum_tensor("banks", [P, 8, 512], F32))
        bank = [PSUM[:, i, :] for i in range(8)]

        def banks(b, n):
            return PSUM[:, b:b + n, :].rearrange("p b n -> p (b n)")

        def ring(s):
            return wr[:, s * 4096:(s + 1) * 4096]

        def ring8(s):
            return ring(s).rearrange("p (k n) -> p k n", k=KT)

        hT = wr[:, 20480:25600].rearrange("p (k t) -> p k t", k=KT)

        def carve(sizes):
            views, at = {}, 0
            for name, n in sizes:
                views[name] = arena[:, at:at + n]
                at += n
            assert at <= ARENA, at
            return views

        R = carve([("mask", 1024), ("qdec", 1024), ("q", 1280), ("k", 1280), ("v", 2560), ("sg", 1024),
                   ("S", 2048), ("attm", 1280), ("qd", 512), ("kd", 512), ("gn", 1024),
                   ("y", 2560), ("t1", 512), ("yT", 1024), ("g1", 2048)])
        mask = R["mask"].rearrange("p (c n) -> p c n", c=8)
        qdec = R["qdec"].rearrange("p (c n) -> p c n", c=8)
        qT = R["q"].rearrange("p (j t) -> p j t", j=2)
        kT = R["k"].rearrange("p (j t) -> p j t", j=2)
        vv = R["v"].rearrange("p (t d) -> p t d", t=NT)
        sg = R["sg"].rearrange("p (b d) -> p b d", b=2)
        yy = R["y"].rearrange("p (t d) -> p t d", t=NT)
        St = R["S"].rearrange("p (r j d) -> p r j d", r=2, j=2)
        attm = R["attm"].rearrange("p (r t n) -> p r t n", r=2, t=NT)
        qd = R["qd"].rearrange("p (b j n) -> p b j n", b=2, j=2)
        kd = R["kd"].rearrange("p (b n) -> p b n", b=2)
        gn = R["gn"].rearrange("p (r d) -> p r d", r=2)
        t1 = R["t1"]
        yT = R["yT"].rearrange("p (b j n) -> p b j n", b=2, j=4)
        g1 = [R["g1"].rearrange("p (c d) -> p c d", c=2)]
        dist = R["S"][:, 0:512].rearrange("p (c n) -> p c n", c=4)

        M = carve([("rows", 6144), ("rt", 1200), ("h2", 2048), ("xg", 2048), ("xgT", 2048),
                   ("act", 512), ("actT", 512), ("ysb", 2048)])
        rows = M["rows"].rearrange("p (g c d) -> p g c d", g=3, c=2)
        rt = [M["rt"][:, 80 * i:80 * i + 80].rearrange("p (t e) -> p t e", t=NT) for i in range(12)]
        rq = [M["rt"][:, 960 + 20 * i:980 + 20 * i] for i in range(12)]
        h2b = M["h2"].rearrange("p (b d) -> p b d", b=2)
        xg = M["xg"].rearrange("p (b d) -> p b d", b=2)
        xgT = M["xgT"].rearrange("p (b k n) -> p b k n", b=2, k=KT)
        gact = M["act"].rearrange("p (b f) -> p b f", b=2)
        gactT = M["actT"].rearrange("p (b j n) -> p b j n", b=2, j=2)
        ysb = M["ysb"].rearrange("p (b d) -> p b d", b=2)
        picked = M["rows"][:, 0:4096].rearrange("p (b j d) -> p b j d", b=2, j=2)
        fin_row = M["xg"][:, 0:D]
        fin = M["xgT"].rearrange("p (b d) -> p b d", b=2)

        def expert_w(b):
            w = wr[:, b * 6144:(b + 1) * 6144]
            return (w[:, 0:4096].rearrange("p (k g f) -> p k g f", k=KT, g=2),
                    w[:, 4096:6144].rearrange("p (j d) -> p j d", j=2))

        A = carve([("wq", 2048), ("wk", 512), ("kT", 1536), ("qT", 1280), ("qpe", 1280), ("P", 1280), ("PT", 1280),
                   ("cqT", 2560), ("CS", 640), ("tab", 640), ("cqn", 1024), ("ckvn", 512), ("kr", 256),
                   ("cache", 384), ("g1", 2048), ("xn", 2048)])
        wq = A["wq"].rearrange("p (b k n) -> p b k n", b=2, k=4)
        wk = A["wk"].rearrange("p (b k n) -> p b k n", b=2, k=2)
        knT = A["kT"].rearrange("p (b t) -> p b t", b=2)
        qnT = A["qT"].rearrange("p (b t) -> p b t", b=2)
        qpT = A["qpe"].rearrange("p (b t) -> p b t", b=2)
        pr = A["P"].rearrange("p (b t) -> p b t", b=2)
        prT = A["PT"].rearrange("p (b k n) -> p b k n", b=2, k=5)
        cqT = A["cqT"].rearrange("p (j t) -> p j t", j=4)
        CS = A["CS"]
        tab = A["tab"].rearrange("p (g t n) -> p g t n", g=2, t=NT)
        cqn = A["cqn"].rearrange("p (b n) -> p b n", b=2)
        ckvn = A["ckvn"].rearrange("p (b n) -> p b n", b=2)
        kr = A["kr"].rearrange("p (b n) -> p b n", b=2)
        c_ckv, c_kpe = A["cache"][:, 0:256], A["cache"][:, 256:384]
        g1.append(A["g1"].rearrange("p (c d) -> p c d", c=2))
        xn = [R["y"][:, 0:2048].rearrange("p (b d) -> p b d", b=2), A["xn"].rearrange("p (b d) -> p b d", b=2)]
        junk = {0: R["v"][:, 0:D], 1: M["xg"][:, 0:D], 2: A["P"][:, 0:D], 3: M["xg"][:, 0:D], 4: M["h2"][:, 0:D]}
        kro = A["PT"][:, 0:128]
        w_in = wr[:, 0:6656].rearrange("p (k n) -> p k n", k=KT)
        V = wr[:, 0:6144].rearrange("p (t n) -> p t n", t=6)
        w_uv = wr[:, 6656:8704].rearrange("p (k n) -> p k n", k=2)
        w_o = wr[:, 8704:16896].rearrange("p (k n) -> p k n", k=MH)
        ckT = wr[:, 16896:18432].rearrange("p (j t) -> p j t", j=2)
        kpT = wr[:, 18432:19200]
        o_all = wr[:, 20480:25600].rearrange("p (t n) -> p t n", t=NT)
        oTb = A["xn"].rearrange("p (b k n) -> p b k n", b=2, k=KT)
        mtmp = A["cqn"][:, 0:512]

        w_ada = a["w_ada"].rearrange("l (k p) n -> l p k n", p=P)
        w_ret = a["ret_w_in"][0].rearrange("(k p) n -> p k n", p=P)
        w_out = a["ret_w_out"][0].rearrange("(j p) n -> p j n", p=P)
        w_g = a["moe_w_gate"].rearrange("l e (k p) f -> l e p k f", p=P)
        w_u = a["moe_w_up"].rearrange("l e (k p) f -> l e p k f", p=P)
        w_d = a["moe_w_down"].rearrange("l e (k p) d -> l e p k d", p=P)
        w_uq = a["mla_w_uq"][0].rearrange("(k p) n -> p k n", p=P)
        w_uk = a["mla_w_uk"][0].rearrange("(k p) h n -> p k (h n)", p=P)
        s_in = [a["state_ret_fwd"][0, 0].rearrange("h (j p) d -> h p j d", p=P),
                a["state_ret_bwd"][0, 0].rearrange("h (j p) d -> h p j d", p=P)]
        s_out = [out[2][0, 0].rearrange("h (j p) d -> h p j d", p=P),
                 out[3][0, 0].rearrange("h (j p) d -> h p j d", p=P)]
        gn_in = a["ret_gn"][0]
        mrow = a["mod_rows_dram"]
        h2d, slot_tok, ybuf = a["h2_dram"], a["slot_tok_dram"], a["y_dram"]

        def alone(eng):
            eng.sem_inc(S("alone"), 1)

        def gate_row(l, j, c):
            return mrow[l, 8 * j:8 * j + 8, c, :].partition_broadcast(P)

        block = ctx.enter_context(nc.Block())

        def tile_cols(t):
            return slice(t * P, (t + 1) * P)

        def key_cols(t):
            return slice(640, 768) if t == PT else tile_cols(t)

        def overflow_guard(eng, l):
            eng.wait_ge(S("cnt_ready"), l + 1)
            r = eng.value_load(cnt[0:1, 0:1], min_val=0, max_val=T)
            with eng.If(r > BLK):
                eng.wait_ge(S(f"ov_out{l}"), 16 * NE * (CAP // BLK - 1))

        def overflow(eng, l):
            eng.wait_ge(S("cnt_ready"), l + 1)
            r = eng.value_load(cnt[0:1, 0:1], min_val=0, max_val=T)
            nb = CAP // BLK - 1
            gu, dn = expert_w(0)
            kind = {nc.gpsimd: "pool", nc.tensor: "pe", nc.scalar: "act", nc.vector: "dve"}
            who = [v for k, v in kind.items() if k is eng][0]
            with eng.If(r > BLK):
                if who == "pool":
                    eng.wait_ge(S("down_done"), l * NE + NE)
                    eng.wait_ge(S("y_out0"), l * 128 + 128)
                    eng.wait_ge(S("y_out1"), l * 128 + 128)
                with eng.Fori(0, NE) as e:
                    with eng.Fori(0, nb) as b:
                        n = e * nb + b
                        row = b * (NE * BLK) + e * BLK + NE * BLK
                        if who == "pool":
                            eng.dma_start(gu[:, :, 0, :], w_g[l][e]).then_inc(S(f"ov_w{l}"), 16)
                            eng.dma_start(gu[:, :, 1, :], w_u[l][e]).then_inc(S(f"ov_w{l}"), 16)
                            eng.dma_start(dn, w_d[l][e]).then_inc(S(f"ov_w{l}"), 16)
                            eng.dma_start(idc[:, 0:1], slot_tok[l][bass.ds(row, BLK), :]).then_inc(S(f"ov_i{l}"), 16)
                            eng.wait_ge(S(f"ov_i{l}"), n * 16 + 16)
                            alone(eng)
                            nc.gpsimd.indirect_dma_start(out=xg[:, 0, :], out_offset=None, in_=h2d[l],
                                                         in_offset=bass.IndirectOffsetOnAxis(ap=idc[:, 0:1], axis=0))\
                                .then_inc(S(f"ov_g{l}"), 16)
                            eng.wait_ge(S(f"ov_out{l}"), n * 16 + 16)
                        if who == "pe":
                            eng.wait_ge(S(f"ov_w{l}"), n * 48 + 48)
                            eng.wait_ge(S(f"ov_g{l}"), n * 16 + 16)
                            for k in range(KT):
                                mm = nc.tensor.transpose(banks(0, 2)[:, tile_cols(k)], xg[:, 0, tile_cols(k)], ident[:])
                            mm.then_inc(S(f"ov_pe{l}"), 1)
                            eng.wait_ge(S(f"ov_ev{l}"), n * 4 + 1)
                            for k in range(KT):
                                mm = nc.tensor.matmul(bank[2], xgT[:, 0, k, :], gu[:, k].rearrange("p g f -> p (g f)"),
                                                      start=(k == 0), stop=(k == KT - 1))
                            mm.then_inc(S(f"ov_pe{l}"), 1)
                            eng.wait_ge(S(f"ov_ev{l}"), n * 4 + 2)
                            for j in range(2):
                                mm = nc.tensor.transpose(bank[3][:, tile_cols(j)], gact[:, 0, tile_cols(j)], ident[:])
                            mm.then_inc(S(f"ov_pe{l}"), 1)
                            eng.wait_ge(S(f"ov_ev{l}"), n * 4 + 3)
                            for hf in range(2):
                                for j in range(2):
                                    mm = nc.tensor.matmul(bank[4 + hf], gactT[:, 0, j, :], dn[:, j, hf * 512:hf * 512 + 512],
                                                          start=(j == 0), stop=(j == 1))
                            mm.then_inc(S(f"ov_pe{l}"), 1)
                        if who == "act":
                            eng.wait_ge(S(f"ov_pe{l}"), n * 4 + 2)
                            nc.scalar.activation(gact[:, 0, :], bank[2][:, 0:FF], ACT.Silu).then_inc(S(f"ov_sig{l}"), 1)
                            eng.wait_ge(S(f"ov_ev{l}"), n * 4 + 4)
                            eng.dma_start(ybuf[l][bass.ds(row, BLK), :], ysb[:, 0, :]).then_inc(S(f"ov_out{l}"), 16)
                        if who == "dve":
                            eng.wait_ge(S(f"ov_pe{l}"), n * 4 + 1)
                            nc.vector.tensor_copy(xgT[:, 0].rearrange("p k n -> p (k n)"), banks(0, 2)).then_inc(S(f"ov_ev{l}"), 1)
                            eng.wait_ge(S(f"ov_sig{l}"), n + 1)
                            nc.vector.tensor_tensor(gact[:, 0, :], bank[2][:, FF:2 * FF], gact[:, 0, :], ALU.mult)\
                                .then_inc(S(f"ov_ev{l}"), 1)
                            eng.wait_ge(S(f"ov_pe{l}"), n * 4 + 3)
                            nc.vector.tensor_copy(gactT[:, 0].rearrange("p j n -> p (j n)"), bank[3][:, 0:256]).then_inc(S(f"ov_ev{l}"), 1)
                            eng.wait_ge(S(f"ov_pe{l}"), n * 4 + 4)
                            nc.vector.tensor_copy(ysb[:, 0, :], banks(4, 2)).then_inc(S(f"ov_ev{l}"), 1)
                if who == "pool":
                    eng.wait_ge(S(f"ov_out{l}"), 16 * NE * nb)
        @block.sync
        def _(sp):
            sp.dma_start(vraw[0:96, :], a["b_ada"].rearrange("l (m p) -> (l m) p", p=P)).then_inc(S("vec_in"), 16)
            sp.dma_start(vraw[96:112, :], a["norm1"].rearrange("l (m p) -> (l m) p", p=P)).then_inc(S("vec_in"), 16)
            sp.dma_start(vraw[112:120, :], a["c"].rearrange("l (m p) -> (l m) p", p=P)).then_inc(S("vec_in"), 16)
            sp.dma_start(vraw[120:128, :], a["c_ctx"].rearrange("(m p) -> m p", p=P)).then_inc(S("vec_in"), 16)
            sp.dma_start(vraw2[0:16, :], a["norm2"].rearrange("l (m p) -> (l m) p", p=P)).then_inc(S("vec_in"), 16)
            sp.dma_start(vraw2[16:20, :], a["mla_q_norm"].rearrange("l (m p) -> (l m) p", p=P)).then_inc(S("vec_in"), 16)
            sp.dma_start(lg[:], a["ret_decay"].rearrange("a r h -> (a r h)").partition_broadcast(P)).then_inc(S("lg_in"), 16)

            def load(s, dst, src):
                sp.dma_start(dst, src).then_inc(S(f"ring_full{s}"), 16)

            def load_chunk(l, c, s):
                if isinstance(c, int):
                    src = w_ada[l][:, :, c * 512:(c + 1) * 512]
                else:
                    src = w_ada[l][:, :, bass.ds(c * 512, 512)]
                load(s, ring8(s), src)

            load_chunk(0, 0, PRE_SLOTS[0])
            load_chunk(0, 1, PRE_SLOTS[1])
            load_chunk(0, 2, PRE_SLOTS[2])
            for t in range(NT):
                src = a["x_prompt"][0] if t == PT else a["x_sample"][0, t * P:(t + 1) * P, :]
                sp.dma_start(x[:, t, :], src).then_inc(S("x_in"), 16)
            load_chunk(0, 3, PRE_SLOTS[3])

            def head_loads(h):
                first = isinstance(h, int)
                chunk = CHUNK_F if first else CHUNK_L
                b = use_base(h)
                if not first:
                    sp.wait_ge(S("proj_done"), b - AFTER_CHUNKS)
                for s, off in ((0, 0), (0, RH * DK)):
                    at = off + h * DK
                    dst = ring8(0)[:, :, 0:DK] if off == 0 else ring8(0)[:, :, DK:2 * DK]
                    src = w_ret[:, :, at:at + DK] if first else w_ret[:, :, bass.ds(at, DK)]
                    load(0, dst, src)
                if not first:
                    load(4, ring(4).rearrange("p (j n) -> p j n", j=4), w_out[:, bass.ds(h * 4 - 4, 4), :])
                for s, off in ((1, 2 * RH * DK), (2, 2 * RH * DK + RH * DV), (3, 2 * RH * DK + 2 * RH * DV)):
                    if s == 1 and first:
                        sp.wait_ge(S("proj_done"), PRE)
                    if s == 2 and not first:
                        sp.wait_ge(S("proj_done"), b - 2)
                    if s == 3 and not first:
                        sp.wait_ge(S("proj_done"), b)
                    at = off + h * DV
                    load(s, ring8(s), w_ret[:, :, at:at + DV] if first else w_ret[:, :, bass.ds(at, DV)])
                if first:
                    last = {0: b + 8, 1: b + 13, 4: PRE}
                    for j, s in enumerate(SLOTS_FIRST):
                        sp.wait_ge(S("proj_done"), last[s])
                        load_chunk(0, 4 + j, s)
                        last[s] = b + chunk[j] + 1
                else:
                    sp.wait_ge(S("op_done"), h * 10)
                    load_chunk(1, h * 4 - 4, 4)
                    sp.wait_ge(S("proj_done"), b + 13)
                    load_chunk(1, h * 4 - 3, 1)
                    sp.wait_ge(S("proj_done"), b + chunk[0] + 1)
                    load_chunk(1, h * 4 - 2, 4)
                    load_chunk(1, h * 4 - 1, 0)

            def mod_rows_out(l):
                sp.wait_ge(S("rows_sb"), l + 1)
                sp.dma_start(mrow[l].rearrange("m c p -> (m c) p"), mod_rows[:]).then_inc(S("rows_out"), 16)
                sp.wait_ge(S("rows_out"), 16 * (l + 1))

            head_loads(0)
            sp.dma_start(w_rt[:], a["w_router"].rearrange("(k p) e -> p k e", p=P)).then_inc(S("misc_in"), 16)
            sp.dma_start(bias_row[:], a["router_bias"].partition_broadcast(P)).then_inc(S("misc_in"), 16)
            sp.dma_start(kv_row[:], a["mla_kv_norm"][0].partition_broadcast(P)).then_inc(S("misc_in"), 16)
            sp.wait_ge(S("zero_set"), 1)
            for l in range(2):
                sp.dma_start(slot_tok[l].rearrange("(p n) o -> p (n o)", p=P), zero_id[:]).then_inc(S("slot_zero"), 16)
            mod_rows_out(0)
            for c in range(2):
                sp.dma_start(g1[0][:, c, :].rearrange("p (m q) -> p m q", m=8), gate_row(0, 2, c)).then_inc(S("g1_in0"), 16)
            with sp.Fori(1, RH) as h:
                head_loads(h)
            sp.wait_ge(S("proj_done"), use_base(RH) - AFTER_CHUNKS)
            load(4, ring(4).rearrange("p (j n) -> p j n", j=4), w_out[:, 12:16, :])

            def moe_loads(l):
                def w_load(e, b):
                    gu, dn = expert_w(b)
                    sp.dma_start(gu[:, :, 0, :], w_g[l][e]).then_inc(S(f"w_full{b}"), 16)
                    sp.dma_start(gu[:, :, 1, :], w_u[l][e]).then_inc(S(f"w_full{b}"), 16)
                    sp.dma_start(dn, w_d[l][e]).then_inc(S(f"w_full{b}"), 16)
                if l == 0:
                    sp.wait_ge(S("proj_done"), use_base(RH))
                    sp.wait_ge(S("ln_done"), 10 * RH)
                    sp.wait_ge(S("S_saved"), 32 * RH)
                else:
                    sp.wait_ge(S("pv_done"), 5 * MH)
                for g, j in ((0, 4), (1, 3), (2, 5)):
                    for c in range(2):
                        sp.dma_start(rows[:, g, c, :].rearrange("p (m q) -> p m q", m=8), gate_row(l, j, c))\
                            .then_inc(S(f"rows_in{l}"), 16)
                if l == 0:
                    w_load(0, 0)
                    w_load(1, 1)
                    sp.wait_ge(S("op_done"), 10 * RH)
                    w_load(2, 2)
                else:
                    sp.wait_ge(S("mo_done"), 10)
                    w_load(0, 0)
                    w_load(1, 1)
                    w_load(2, 2)
                for t in range(NT):
                    sp.wait_ge(S("h2_ready"), l * NT + t + 1)
                    sp.dma_start(h2d[l][t * P:(t + 1) * P, :], h2b[:, t % 2, :]).then_inc(S(f"h2_out{l}"), 16)
                    sp.wait_ge(S(f"h2_out{l}"), 16 * (t + 1))
                sp.wait_ge(S("router_mm"), l * NT + NT)
                w_load(3, 3)
                sp.wait_ge(S(f"scattered{l}"), 160)
                sp.dma_start(ids[:], slot_tok[l][0:NE * BLK, :].rearrange("(e c) o -> c (e o)", c=BLK),
                             allow_slow_non_contiguous=True)\
                    .then_inc(S(f"ids_in{l}"), 16)
                with sp.Fori(0, 3) as i:
                    for b in range(4):
                        sp.wait_ge(S("down_done"), l * NE + i * 4 + b + 1)
                        w_load(i * 4 + b + 4, b)

            moe_loads(0)
            mod_rows_out(1)
            sp.wait_ge(S("down_done"), NE)
            overflow_guard(sp, 0)
            sp.dma_start(w_in, a["mla_w_in"][0].rearrange("(k p) n -> p k n", p=P)).then_inc(S("mw_in"), 16)
            sp.dma_start(w_uv, a["mla_w_uv"][0].rearrange("(k p) h n -> p k (h n)", p=P)).then_inc(S("mw_in"), 16)
            sp.dma_start(w_o, a["mla_w_o"][0].rearrange("(k p) n -> p k n", p=P)).then_inc(S("mw_o"), 16)
            sp.wait_ge(S("y_out0"), 128)
            sp.wait_ge(S("y_out1"), 128)
            sp.wait_ge(S("comb"), NT)
            sp.dma_start(CS, a["rope_cs"]).then_inc(S("tab_in"), 16)
            sp.dma_start(A["tab"], a["rope_tab"]).then_inc(S("tab_in"), 16)
            sp.dma_start(c_ckv, a["cache_mla_ckv"][0, 0]).then_inc(S("tab_in"), 16)
            for j in range(2):
                sp.dma_start(c_kpe[:, j * 64:j * 64 + 64], a["cache_mla_kpe"][0, 0]).then_inc(S("tab_in"), 16)
            for c in range(2):
                sp.dma_start(g1[1][:, c, :].rearrange("p (m q) -> p m q", m=8), gate_row(1, 2, c)).then_inc(S("g1_in1"), 16)

            def head_w(h, b, dyn):
                sq = w_uq[:, :, bass.ds(h * 192, 192)] if dyn else w_uq[:, :, h * 192:h * 192 + 192]
                sk = w_uk[:, :, bass.ds(h * 128, 128)] if dyn else w_uk[:, :, h * 128:h * 128 + 128]
                sp.dma_start(wq[:, b, :, 0:192], sq).then_inc(S(f"wq_full{b}"), 16)
                sp.dma_start(wk[:, b], sk).then_inc(S(f"wq_full{b}"), 16)
            head_w(0, 0, False)
            head_w(1, 1, False)
            with sp.Fori(0, 3) as i:
                for b in range(2):
                    sp.wait_ge(S("hp_done"), i * 8 + 4 * b + 4)
                    head_w(i * 2 + b + 2, b, True)
            sp.wait_ge(S("kr_ready"), NT)
            sp.dma_start(out[4][0, 0], ckvn[:, PT % 2, :]).then_inc(S("cache_out"), 16)
            sp.dma_start(out[5][0, 0], kr[:, PT % 2, 0:64]).then_inc(S("cache_out"), 16)
            moe_loads(1)
            sp.wait_ge(S("y_out0"), 256)
            sp.wait_ge(S("down_done"), 2 * NE)
            overflow_guard(sp, 1)
            sp.dma_start(fin_row, a["norm_final"].partition_broadcast(P)).then_inc(S("fin_in"), 16)
            for t in range(NT):
                sp.wait_ge(S("fin_ready"), t + 1)
                dst = out[0][0] if t == PT else out[1][0, t * P:(t + 1) * P, :]
                sp.dma_start(dst, fin[:, t % 2, :]).then_inc(S(f"fin_out{t % 2}"), 16)
            sp.wait_ge(S("fin_out0"), 48)
            sp.wait_ge(S("fin_out1"), 32)
            sp.wait_ge(S("cache_out"), 32)

        @block.gpsimd
        def _(pool):
            g = nc.gpsimd
            g.memset(ident[:], 0.0).then_inc(S("gset"), 1)
            g.memset(ones[:], 1.0).then_inc(S("gset"), 1)
            g.memset(before[:], 1.0).then_inc(S("gset"), 1)
            g.memset(half[:], -0.5).then_inc(S("gset"), 1)
            g.memset(epsc[:], EPS).then_inc(S("gset"), 1)
            pool.wait_ge(S("gset"), 5)
            g.affine_select(out=ident[:], in_=ident[:], compare_op=ALU.not_equal, fill=1.0, base=0,
                            pattern=[[-1, P]], channel_multiplier=1).then_inc(S("gset"), 1)
            g.affine_select(out=before[:], in_=before[:], compare_op=ALU.is_gt, fill=0.0, base=0,
                            pattern=[[1, P]], channel_multiplier=-1).then_inc(S("gset"), 1)
            for j, (st, base, cm) in enumerate(((1, 0, -1), (-1, 0, 1), (1, 1, 0), (-1, P, 0))):
                g.iota(dist[:, j, :], pattern=[[st, P]], base=base, channel_multiplier=cm,
                       allow_small_or_imprecise_dtypes=True).then_inc(S("gset"), 1)
            g.iota(pf[:, 0:1], pattern=[[1, 1]], base=P - 1, channel_multiplier=-1,
                   allow_small_or_imprecise_dtypes=True).then_inc(S("gset"), 1)
            g.iota(pf[:, 1:2], pattern=[[1, 1]], base=0, channel_multiplier=1,
                   allow_small_or_imprecise_dtypes=True).then_inc(S("gset"), 1)
            g.iota(idx16[:], pattern=[[1, NE]], base=0, channel_multiplier=0,
                   allow_small_or_imprecise_dtypes=True).then_inc(S("gset"), 1)
            g.iota(idx16p[:], pattern=[[1, NE]], base=100, channel_multiplier=0,
                   allow_small_or_imprecise_dtypes=True).then_inc(S("gset"), 1)
            g.iota(ebase[:], pattern=[[BLK, NE]], base=0, channel_multiplier=0,
                   allow_small_or_imprecise_dtypes=True).then_inc(S("gset"), 1)
            g.iota(tok_id[:], pattern=[[P, NT]], base=0, channel_multiplier=1).then_inc(S("gset"), 1)
            g.memset(zero_id[:], 0).then_inc(S("zero_set"), 1)
            pool.wait_ge(S("mask_exp"), 8)
            mf, mb = mask[:, 0:4, :], mask[:, 4:8, :]
            g.affine_select(out=mf, in_=mf, compare_op=ALU.is_ge, fill=0.0, base=0,
                            pattern=[[0, 4], [1, P]], channel_multiplier=-1).then_inc(S("mask_tri"), 1)
            g.affine_select(out=mb, in_=mb, compare_op=ALU.is_ge, fill=0.0, base=0,
                            pattern=[[0, 4], [-1, P]], channel_multiplier=1).then_inc(S("mask_tri"), 1)

            ch = Chain(pool, S("pool_step"))

            def rstd(n):
                for t in range(NT):
                    pool.wait_ge(S("sq"), n * NT + t + 1)
                    if n:
                        pool.wait_ge(S("used"), n * NT - NT + t + 1)
                    ch.link(g.tensor_scalar(rs[:, t:t + 1], ss[:, t:t + 1], 1.0 / D, EPS, ALU.mult, ALU.add))
                    g.tensor_tensor(rs[:, t:t + 1], rs[:, t:t + 1], half[:], ALU.pow).then_inc(S("rstd"), 1)

            rstd(0)

            def head(h, per):
                def qdec_mul(u):
                    t, r = STEPS[u]
                    pool.wait_ge(S("qdec_exp"), 8)
                    if u == 0:
                        pool.wait_ge(S("proj_evac"), use_base(h) + 4)
                    if u < 2:
                        pool.wait_ge(S("o_done"), h * 10)
                    else:
                        pool.wait_ge(S("o_done"), h * 10 + u - 1)
                    c = qdec[:, r * 4 + h, :] if isinstance(h, int) else qdec[:, bass.ds(h + r * 4, 1), :].rearrange("p a n -> p (a n)")
                    g.tensor_tensor(qd[:, u % 2], qT[:, :, tile_cols(t)], c.unsqueeze(1).to_broadcast([P, 2, P]),
                                    ALU.mult).then_inc(S("qd_ready"), 1)
                qdec_mul(0)
                qdec_mul(1)
                for i in range(10):
                    pool.wait_ge(S("stats"), h * 10 + i + 1)
                    ch.link(g.tensor_tensor(rv[:, i % 2:i % 2 + 1], mv[:, i % 2, 1:2], epsc[:], ALU.add))
                    g.tensor_tensor(rv[:, i % 2:i % 2 + 1], rv[:, i % 2:i % 2 + 1], half[:], ALU.pow)\
                        .then_inc(S("head_rstd"), 1)
                    if i + 2 < 8:
                        qdec_mul(i + 2)

            head(0, 10)
            with pool.Fori(1, RH) as h:
                ch.c.enter(h, 1, 10)
                head(h, 10)
            ch.c.leave(RH)

            def moe(l):
                n = 2 * l + 1
                rstd(n)
                pool.wait_ge(S("slot_zero"), 32)
                pool.wait_ge(S("slots_ready"), l + 1)
                for t in range(NT):
                    for j in range(2):
                        g.indirect_dma_start(out=slot_tok[l], out_offset=bass.IndirectOffsetOnAxis(ap=slots[:, j, t:t + 1], axis=0),
                                             in_=tok_id[:, t:t + 1], in_offset=None).then_inc(S(f"scattered{l}"), 16)
                pool.wait_ge(S(f"h2_out{l}"), 16 * NT)
                pool.wait_ge(S(f"ids_in{l}"), 16)
                def gather(e):
                    b = e.par
                    if not (isinstance(e.n, int) and e.n < 2):
                        pool.wait_ge(S("tr_done"), l * NE + e.n - 1)
                    ch.link(g.tensor_copy(idc[:, b:b + 1], ids[:, e.n:e.n + 1] if isinstance(e.n, int)
                                          else ids[:, bass.ds(e.n, 1)]))
                    alone(pool)
                    g.indirect_dma_start(out=xg[:, b, :], out_offset=None, in_=h2d[l],
                                         in_offset=bass.IndirectOffsetOnAxis(ap=idc[:, b:b + 1], axis=0))\
                        .then_inc(S(f"gath{b}"), 16)
                gather(fixed(0, 2))
                gather(fixed(1, 2))
                with pool.Fori(0, NE // 2 - 1) as i:
                    ch.c.enter(i, 0, 2)
                    gather(Step(i, 2, 2))
                    gather(Step(i, 2, 3))
                ch.c.leave(NE // 2 - 1)
                overflow(pool, l)
                pool.wait_ge(S("y_out0"), l * 128 + 128)
                pool.wait_ge(S("y_out1"), l * 128 + 128)
                def pick(table):
                  for t in range(NT):
                    if t >= 2:
                        pool.wait_ge(S("comb"), l * NT + t - 1)
                    for j in range(2):
                        g.indirect_dma_start(out=picked[:, t % 2, j, :], out_offset=None, in_=table,
                                             in_offset=bass.IndirectOffsetOnAxis(ap=slots[:, j, t:t + 1], axis=0))\
                            .then_inc(S(f"pick{t % 2}_{l}"), 16)
                r = pool.value_load(cnt[0:1, 0:1], min_val=0, max_val=T)
                with pool.If(r > BLK):
                    pick(ybuf[l])
                with pool.Else():
                    pick(ybuf[l][0:NE * BLK, :])

            moe(0)
            rstd(2)
            for t in range(NT):
                pool.wait_ge(S("lat_sq"), 2 * t + 2)
                if t:
                    pool.wait_ge(S("lat_used"), t)
                ch.link(g.tensor_scalar(rv[:, 0:1], ss[:, 6:7], 1.0 / QR, EPS, ALU.mult, ALU.add))
                ch.link(g.tensor_scalar(rv[:, 1:2], ss[:, 7:8], 1.0 / KVR, EPS, ALU.mult, ALU.add))
                g.tensor_tensor(rv[:, 0:1], rv[:, 0:1], half[:], ALU.pow).then_inc(S("lat_rstd"), 1)
                g.tensor_tensor(rv[:, 1:2], rv[:, 1:2], half[:], ALU.pow).then_inc(S("lat_rstd"), 1)

            with pool.Fori(0, MH // 2) as i:
                for b in range(2):
                    pool.wait_ge(S(f"wq_full{b}"), i * 32 + 32)
                    alone(pool)
                    w5 = wq[:, b].rearrange("p k (q n) -> p k q n", q=16)
                    for o, s in ((12, 9), (13, 8), (14, 11), (15, 10)):
                        g.tensor_copy(w5[:, :, o, :], w5[:, :, s, :]).then_inc(S("wq_swap"), 1)
            moe(1)
            rstd(4)


        @block.tensor
        def _(pe):
            mmul, tpose = nc.tensor.matmul, nc.tensor.transpose
            full = [Count(16) for _ in range(5)]

            pe.wait_ge(S("vec_in"), 96)
            pe.wait_ge(S("gset"), 17)
            tpose(bank[7][:, 0:P], vraw[:], ident[:])
            tpose(bank[7][:, P:P + 20], vraw2[:], ident[0:20, 0:20]).then_inc(S("vec_T"), 1)

            def bank_free(base, j):
                if not (isinstance(base, int) and base + j < 3):
                    pe.wait_ge(S("proj_evac"), base + j - 2)

            def chunk(base, j, s):
                bank_free(base, j)
                pe.wait_ge(S(f"ring_full{s}"), full[s].next())
                for i in range(2):
                    for g in range(4):
                        k = 2 * g + i
                        mm = mmul(bank[j % 4][32 * g:32 * g + 32, :], cond[:, 2 * k:2 * k + 32], ring8(s)[:, k, :],
                                  start=(i == 0), stop=(i == 1), tile_position=(0, 32 * g))
                mm.then_inc(S("proj_done"), 1)

            def chunk_sum(base, part, j):
                bank_free(base, j)
                pe.wait_ge(S("proj_evac"), base + part + 1)
                for m in range(4):
                    mm = mmul(bank[j % 4][:, 2 * m:2 * m + 2], stage[:, tile_cols(m)], pick2[:], start=True, stop=True)
                mm.then_inc(S("proj_done"), 1)

            def norm_T(n, src):
                for t in range(NT):
                    if n % 2:
                        pe.wait_ge(S("h2_ready"), n // 2 * NT + t + 1)
                    else:
                        pe.wait_ge(S("used"), n * NT + t + 1)
                    if t >= 2:
                        pe.wait_ge(S("hTa"), n * NT + t - 1)
                        pe.wait_ge(S("hTd"), n * NT + t - 1)
                    for k in range(KT):
                        mm = tpose(banks(2 * (t % 2), 2)[:, tile_cols(k)], src[:, t % 2, tile_cols(k)], ident[:])
                    mm.then_inc(S("tr"), 1)
                    yield t

            pe.wait_ge(S("cond_set"), 1)
            pe.wait_ge(S("pick2_set"), 2)
            for j, (kind, c) in enumerate(PRE_ORDER):
                if kind == "part":
                    chunk(0, j, PRE_SLOTS[c])
                else:
                    chunk_sum(0, PRE_ORDER.index(("part", c)), j)
            pe.wait_ge(S("proj_evac"), PRE)
            for _ in norm_T(0, xn[0]):
                pass
            pe.wait_ge(S("hTa"), 1 * NT)
            pe.wait_ge(S("hTd"), 1 * NT)

            def out_proj(h):
                def y_T(t):
                    if t == 0:
                        pe.wait_ge(S("ln_done"), h * 10)
                        pe.wait_ge(S("kd_ready"), h * NSS)
                        pe.wait_ge(S("rows_sb"), 1)
                    elif t == 1:
                        pe.wait_ge(S("o_free"), h * 10)
                    else:
                        pe.wait_ge(S("yt_evac"), h * NT - NT + t - 1)
                    for j in range(4):
                        mm = tpose(bank[4 + t % 2][:, tile_cols(j)], yy[:, t, tile_cols(j)], ident[:])
                    mm.then_inc(S("yt_done"), 1)
                y_T(0)
                for t in range(NT):
                    if t + 1 < NT:
                        y_T(t + 1)
                    pe.wait_ge(S("yt_evac"), h * NT - NT + t + 1)
                    if t == 0:
                        pe.wait_ge(S("ring_full4"), full[4].next())
                        pe.wait_ge(S("S_upd"), h * NSS)
                    for hf in range(2):
                        if t:
                            pe.wait_ge(S("op_evac"), h * 10 - 10 + 2 * t + hf - 1)
                        for j in range(4):
                            mm = mmul(bank[6 + hf][:], yT[:, t % 2, j, :],
                                      ring(4)[:, j * D + hf * 512:j * D + hf * 512 + 512],
                                      start=(j == 0), stop=(j == 3))
                        mm.then_inc(S("op_done"), 1)

            def head(h):
                first = isinstance(h, int)
                gate, chunk_use, sum_use, _ = use_plan(CHUNKS_FIRST if first else CHUNKS_LOOP)
                chunks = CHUNKS_FIRST if first else CHUNKS_LOOP
                slots_of = SLOTS_FIRST if first else SLOTS_LOOP
                b = use_base(h)
                pe.wait_ge(S("ring_full0"), full[0].next(2))
                for j in range(4):
                    for s, cols in enumerate((slice(0, TS), slice(TS, T))):
                        bank_free(b, 2 * j + s)
                        w = cols.stop - cols.start
                        for k in range(KT):
                            mm = mmul(bank[(2 * j + s) % 4][:, 0:w], ring8(0)[:, k, tile_cols(j)], hT[:, k, cols],
                                      start=(k == 0), stop=(k == KT - 1))
                        mm.then_inc(S("proj_done"), 1)
                if not first:
                    out_proj(h)
                pe.wait_ge(S("ring_full1"), full[1].next())
                for t in range(NT):
                    bank_free(b, 8 + t)
                    for k in range(KT):
                        mm = mmul(bank[(8 + t) % 4][:], hT[:, k, tile_cols(t)], ring8(1)[:, k, :],
                                  start=(k == 0), stop=(k == KT - 1))
                    mm.then_inc(S("proj_done"), 1)
                pe.wait_ge(S("proj_evac"), b + 8)
                if not first:
                    pe.wait_ge(S("yt_evac"), h * NT)
                for t in range(NT):
                    dst = bank[4][:, tile_cols(t)] if t < 4 else bank[5][:, 0:P]
                    for j in range(2):
                        mm = mmul(dst, kT[:, j, tile_cols(t)], qT[:, j, tile_cols(t)], start=(j == 0), stop=(j == 1))
                    if t >= 3:
                        mm.then_inc(S("att_done"), 1)
                pe.wait_ge(S("attm"), h * 4 + 4)

                def k_T(u):
                    if u:
                        pe.wait_ge(S("kd_ready"), h * NSS + u)
                    for j in range(2):
                        mm = tpose(bank[4][:, tile_cols(j)], kT[:, j, tile_cols(STEPS[STATE_STEPS[u]][0])], ident[:])
                    mm.then_inc(S("kt_done"), 1)

                k_T(0)
                pe.wait_ge(S("proj_evac"), b + 13)
                if not first:
                    pe.wait_ge(S("op_evac"), h * 10)
                for i, (t, r) in enumerate(STEPS):
                    latent = t != PT
                    if i:
                        pe.wait_ge(S("o_free"), h * 10 + i)
                    mm = mmul(bank[5][:], attm[:, r, t, :], vv[:, t, :], start=True, stop=not latent)
                    if latent:
                        pe.wait_ge(S("qd_ready"), h * 8 + i + 1)
                        before_i = [u for u, s in enumerate(STATE_STEPS) if s < i and STEPS[s][1] == r]
                        if before_i:
                            pe.wait_ge(S("S_upd"), h * NSS + before_i[-1] + 1)
                        else:
                            pe.wait_ge(S("S_in"), h * 32 + 32)
                        for j in range(2):
                            mm = mmul(bank[5][:], qd[:, i % 2, j, :], St[:, r, j, :], start=False, stop=(j == 1))
                    mm.then_inc(S("o_done"), 1)
                    if i in STATE_STEPS:
                        u = STATE_STEPS.index(i)
                        pe.wait_ge(S("kd_ready"), h * NSS + u + 1)
                        if u:
                            pe.wait_ge(S("S_upd"), h * NSS + u)
                        for j in range(2):
                            mm = mmul(bank[6 + j][:], kd[:, u % 2, tile_cols(j)], vv[:, t, :], start=True, stop=True)
                        mm.then_inc(S("S_done"), 1)
                        if u + 1 < NSS:
                            k_T(u + 1)
                    bank_free(b, gate[i])
                    if i < 2:
                        pe.wait_ge(S(f"ring_full{2 + r}"), full[2 + r].next())
                    for k in range(KT):
                        mm = mmul(bank[gate[i] % 4][:], hT[:, k, tile_cols(t)], ring8(2 + r)[:, k, :],
                                  start=(k == 0), stop=(k == KT - 1))
                    mm.then_inc(S("proj_done"), 1)
                    if i - 1 in chunks:
                        c = chunks[i - 1]
                        chunk_sum(b, chunk_use[c], sum_use[c])
                    if i in chunks:
                        c = chunks[i]
                        chunk(b, chunk_use[c], slots_of[c])

            def rows_T(l):
                pe.wait_ge(S("modB"), l + 1)
                tpose(bank[4][0:96, 0:P], mod[:, l].rearrange("p m c -> p (m c)"), ident[:]).then_inc(S("rows_T"), 1)

            head(0)
            pe.wait_ge(S("kd_ready"), NSS)
            rows_T(0)
            per = (3, 2, 1, 1, 3)
            with pe.Fori(1, RH) as h:
                for f, n in zip(full, per):
                    f.enter(h, 1, n)
                head(h)
            for f in full:
                f.leave(RH)
            out_proj(RH)
            pe.wait_ge(S("yt_evac"), NT * RH)
            rows_T(1)

            def moe(l):
                n = 2 * l + 1

                def router(t):
                    pe.wait_ge(S("hTa"), n * NT + t + 1)
                    pe.wait_ge(S("hTd"), n * NT + t + 1)
                    for k in range(KT):
                        mm = mmul(bank[4][:, t * NE:(t + 1) * NE], hT[:, k, tile_cols(t)], w_rt[:, k, :],
                                  start=(k == 0), stop=(k == KT - 1))
                    mm.then_inc(S("router_mm"), 1)

                if l == 0:
                    pe.wait_ge(S("proj_evac"), use_base(RH))
                    pe.wait_ge(S("misc_in"), 48)
                for t in norm_T(n, h2b):
                    if t == 0 and l == 0:
                        pe.wait_ge(S("rows_sb"), 2)
                    if t:
                        router(t - 1)
                router(NT - 1)
                pe.wait_ge(S("sel"), l + 1)
                msk = rt[3]
                for t in range(NT):
                    for j in range(t + 1):
                        mmul(bank[5][:, t * NE:(t + 1) * NE], before[:] if j == t else ones[:], msk[:, j, :],
                             start=(j == 0), stop=(j == t))
                for j in range(NT):
                    mm = mmul(bank[5][:, NT * NE:NT * NE + NE], ones[:], msk[:, j, :], start=(j == 0), stop=(j == NT - 1))
                mm.then_inc(S("rank_done"), 1)

                def gathered_T(e):
                    pe.wait_ge(S(f"gath{e.par}"), l * 128 + e.half * 16 + 16)
                    pe.wait_ge(S("xa"), l * NE + e.n)
                    pe.wait_ge(S("xd"), l * NE + e.n)
                    for k in range(KT):
                        mm = tpose(banks(0, 2)[:, tile_cols(k)], xg[:, e.par, tile_cols(k)], ident[:])
                    mm.then_inc(S("tr_done"), 1)

                def gate_up(e):
                    pe.wait_ge(S(f"w_full{e.buf}"), l * 192 + e.quarter * 48 + 48)
                    pe.wait_ge(S("xa"), l * NE + e.n + 1)
                    pe.wait_ge(S("xd"), l * NE + e.n + 1)
                    pe.wait_ge(S("act"), l * NE + e.n)
                    for k in range(KT):
                        mm = mmul(bank[2][:], xgT[:, e.par, k, :], expert_w(e.buf)[0][:, k].rearrange("p g f -> p (g f)"),
                                  start=(k == 0), stop=(k == KT - 1))
                    mm.then_inc(S("gu_done"), 1)

                def act_T(e):
                    pe.wait_ge(S("act"), l * NE + e.n + 1)
                    pe.wait_ge(S("actT"), l * NE + e.n)
                    for j in range(2):
                        mm = tpose(bank[3][:, tile_cols(j)], gact[:, e.par, tile_cols(j)], ident[:])
                    mm.then_inc(S("at_done"), 1)

                def down(e):
                    pe.wait_ge(S("actT"), l * NE + e.n + 1)
                    if not (isinstance(e.n, int) and e.n < 2):
                        pe.wait_ge(S("ya"), l * NE + e.n - 1)
                        pe.wait_ge(S("yd"), l * NE + e.n - 1)
                    for hf in range(2):
                        for j in range(2):
                            mm = mmul(bank[4 + 2 * e.par + hf][:], gactT[:, e.par, j, :],
                                      expert_w(e.buf)[1][:, j, hf * 512:hf * 512 + 512], start=(j == 0), stop=(j == 1))
                    mm.then_inc(S("down_done"), 1)

                gathered_T(fixed(0, 4))
                pe_step(pe, gate_up, gathered_T, down, act_T)
                down(fixed(NE - 1, 4))
                overflow(pe, l)

            def pe_step(eng, gate_up, gathered_T, down, act_T):
                def one(e):
                    static = isinstance(e.n, int)
                    gate_up(e)
                    if not (static and e.n == NE - 1):
                        gathered_T(e.plus(1))
                    if not (static and e.n == 0):
                        down(e.plus(-1))
                    act_T(e)
                for u in range(3):
                    one(fixed(u, 4))
                with eng.Fori(0, 3) as i:
                    for u in range(3, 7):
                        one(Step(i, 4, u))
                one(fixed(NE - 1, 4))

            moe(0)
            for _ in norm_T(2, xn[1]):
                pass

            def lat_T(t):
                if t < NT:
                    pe.wait_ge(S("kr_ready"), t + 1)
                else:
                    pe.wait_ge(S("tab_in"), 80)
                if t >= 2:
                    pe.wait_ge(S("lat_Ta"), t - 1)
                    pe.wait_ge(S("lat_Td"), t - 1)
                b0 = 2 * (t % 2)
                if t < NT:
                    for j in range(4):
                        tpose(bank[b0][:, tile_cols(j)], cqn[:, t % 2, tile_cols(j)], ident[:])
                ck, kp = (ckvn[:, t % 2, :], kr[:, t % 2, :]) if t < NT else (c_ckv, c_kpe)
                for j in range(2):
                    tpose(bank[b0 + 1][:, tile_cols(j)], ck[:, tile_cols(j)], ident[:])
                tpose(bank[b0 + 1][:, tile_cols(2)], kp, ident[:]).then_inc(S("lat_tr"), 1)

            pe.wait_ge(S("hTa"), 3 * NT)
            pe.wait_ge(S("hTd"), 3 * NT)
            pe.wait_ge(S("mw_in"), 32)
            for t in range(NT):
                if t >= 2:
                    pe.wait_ge(S("lat_used"), t - 1)
                b0 = 4 + 2 * (t % 2)
                for k in range(KT):
                    mmul(bank[b0][:], hT[:, k, tile_cols(t)], w_in[:, k, 0:512], start=(k == 0), stop=(k == KT - 1))
                for k in range(KT):
                    mm = mmul(bank[b0 + 1][:, 0:320], hT[:, k, tile_cols(t)], w_in[:, k, 512:832],
                              start=(k == 0), stop=(k == KT - 1))
                mm.then_inc(S("lat_done"), 1)
                if t:
                    lat_T(t - 1)
            lat_T(NT - 1)
            lat_T(NT)
            pe.wait_ge(S("lat_Ta"), NT)
            pe.wait_ge(S("lat_Td"), NT + 1)
            for kt in range(6):
                for hf in range(2):
                    if kt >= 2:
                        pe.wait_ge(S("va" if hf == 0 else "vd"), kt - 1)
                    for j in range(2):
                        mm = mmul(bank[4 + (2 * kt + hf) % 4][:], ckT[:, j, tile_cols(kt)],
                                  w_uv[:, j, hf * 512:hf * 512 + 512], start=(j == 0), stop=(j == 1))
                    mm.then_inc(S("v_done"), 1)
            pe.wait_ge(S("va"), 6)
            pe.wait_ge(S("vd"), 6)

            def head_proj(h):
                p = h.par
                pe.wait_ge(S(f"wq_full{p}"), h.half * 32 + 32)
                pe.wait_ge(S("wq_swap"), h.n * 4 + 4)
                notfirst = not (isinstance(h.n, int) and h.n == 0)

                def run(dst, lhs, rhs, nk, inc):
                    for k in range(nk):
                        mm = mmul(dst, lhs(k), rhs(k), start=(k == 0), stop=(k == nk - 1))
                    if inc:
                        mm.then_inc(S("hp_done"), 1)
                qn = lambda k: wq[:, p, k, 0:NOPE]
                qp = lambda k: wq[:, p, k, NOPE:NOPE + 128]
                kn = lambda k: wk[:, p, k, :]
                if notfirst:
                    pe.wait_ge(S("ex_done"), h.n * 5 - 2)
                run(bank[1][:], qn, lambda k: cqT[:, k, 0:TS], 4, True)
                if notfirst:
                    pe.wait_ge(S("ex_done"), h.n * 5 - 1)
                run(bank[2][:], qp, lambda k: cqT[:, k, 0:TS], 4, True)
                run(bank[3][:], kn, lambda k: ckT[:, k, 0:512], 2, True)
                if notfirst:
                    pe.wait_ge(S("hp_d"), h.n * 2)
                run(bank[7][:, 0:128], qn, lambda k: cqT[:, k, TS:T], 4, False)
                run(bank[7][:, 128:256], qp, lambda k: cqT[:, k, TS:T], 4, False)
                run(bank[7][:, 256:512], kn, lambda k: ckT[:, k, 512:768], 2, True)

            def score(h, t):
                if t == 0:
                    pe.wait_ge(S("hp_a"), h.n * 2 + 2)
                    pe.wait_ge(S("hp_d"), h.n * 2 + 2)
                    pe.wait_ge(S("ex_done"), h.n * 5)
                elif t >= 2:
                    pe.wait_ge(S("ex_done"), h.n * 5 + t - 1)
                b0 = 2 * (t % 2)
                parts = ((b0, 128, slice(640, 768)),) if t == PT else ((b0, 512, slice(0, 512)), (b0 + 1, 128, slice(512, 640)))
                for b, w, cols in parts:
                    mmul(bank[b][:, 0:w], qnT[:, h.par, tile_cols(t)], knT[:, h.par, cols], start=True, stop=False)
                    mm = mmul(bank[b][:, 0:w], qpT[:, h.par, tile_cols(t)], kpT[:, cols], start=False, stop=True)
                mm.then_inc(S("sc_done"), 1)

            def prob_T(h, t):
                gp = (h.par + t) % 2
                pe.wait_ge(S("ex_done"), h.n * 5 + t + 1)
                pe.wait_ge(S("pt_a"), h.n * 5 + t)
                for k in range(1 if t == PT else 5):
                    mm = tpose(banks(4, 2)[:, tile_cols(k)], pr[:, gp, tile_cols(k)], ident[:])
                mm.then_inc(S("pt_done"), 1)

            def prob_v(h, t):
                gp = (h.par + t) % 2
                pe.wait_ge(S("pt_a"), h.n * 5 + t + 1)
                pe.wait_ge(S("o_ev"), h.n * 5 + t)
                keys = [5] if t == PT else range(5)
                for i, kt in enumerate(keys):
                    rhs = V[:, kt, h.n * VD:h.n * VD + VD] if isinstance(h.n, int) else V[:, kt, bass.ds(h.n * VD, VD)]
                    mm = mmul(bank[6][:, 0:VD], prT[:, gp, i, :], rhs, start=(i == 0), stop=(i == len(keys) - 1))
                mm.then_inc(S("pv_done"), 1)

            def main(h):
                score(h, 0)
                score(h, 1)
                prob_T(h, 0)
                score(h, 2)
                prob_T(h, 1)
                prob_v(h, 0)
                score(h, 3)
                prob_T(h, 2)
                prob_v(h, 1)
                score(h, 4)
                prob_T(h, 3)
                prob_v(h, 2)

            def tail(h):
                prob_T(h, 4)
                prob_v(h, 3)
                prob_v(h, 4)

            head_proj(fixed(0, 2))
            main(fixed(0, 2))
            with pe.Fori(0, 3) as i:
                for u in (1, 2):
                    h = Step(i, 2, u)
                    head_proj(h)
                    tail(h.plus(-1))
                    main(h)
            head_proj(fixed(MH - 1, 2))
            tail(fixed(MH - 2, 2))
            main(fixed(MH - 1, 2))
            tail(fixed(MH - 1, 2))

            pe.wait_ge(S("mw_o"), 16)
            pe.wait_ge(S("o_ev"), 5 * MH)

            def o_T(t):
                if t >= 2:
                    pe.wait_ge(S("oTa"), t - 1)
                    pe.wait_ge(S("oTd"), t - 1)
                for k in range(KT):
                    mm = tpose(banks(2 * (t % 2), 2)[:, tile_cols(k)], o_all[:, t, tile_cols(k)], ident[:])
                mm.then_inc(S("o_tr"), 1)
            o_T(0)
            for t in range(NT):
                if t + 1 < NT:
                    o_T(t + 1)
                pe.wait_ge(S("oTa"), t + 1)
                pe.wait_ge(S("oTd"), t + 1)
                for hf in range(2):
                    if t >= 2:
                        pe.wait_ge(S("mo_evac"), 2 * t + hf - 3)
                    for k in range(KT):
                        mm = mmul(bank[4 + 2 * (t % 2) + hf][:], oTb[:, t % 2, k, :], w_o[:, k, hf * 512:hf * 512 + 512],
                                  start=(k == 0), stop=(k == KT - 1))
                    mm.then_inc(S("mo_done"), 1)
            moe(1)

        @block.scalar
        def _(act):
            A_ = nc.scalar.activation
            ch = Chain(act, S("act_step"))
            act.wait_ge(S("lg_in"), 16)
            ch.link(A_(lg[:], lg[:], ACT.Exp))
            ch.link(A_(lg[:], lg[:], ACT.Copy, scale=-1.0))
            act.wait_ge(S("gset"), 17)
            A_(cdec[:], lg[:], ACT.Exp, scale=float(P)).then_inc(S("cdec_set"), 1)
            for r in range(2):
                ch.link(A_(lgk[:, 4 * r:4 * r + 4], lg[:, 4 * r:4 * r + 4], ACT.Copy, scale=pf[:, r:r + 1]))
            A_(kdec[:], lgk[:], ACT.Exp).then_inc(S("kdec_set"), 1)
            for r in range(2):
                ch.link(A_(dist[:, r, :], dist[:, r, :], ACT.Relu))
            for c in range(8):
                A_(mask[:, c, :], dist[:, c // 4, :], ACT.Exp, scale=lg[:, c:c + 1]).then_inc(S("mask_exp"), 1)
            for c in range(8):
                A_(qdec[:, c, :], dist[:, 2 + c // 4, :], ACT.Exp, scale=lg[:, c:c + 1]).then_inc(S("qdec_exp"), 1)
            act.wait_ge(S("vec_T"), 1)
            A_(cond[:, 0:16].rearrange("p (k c) -> p c k", c=2), bank[7][:, 112:128].rearrange("p (c k) -> p c k", c=2), ACT.Silu)\
                .then_inc(S("cond_set"), 1)
            A_(vt1[:], bank[7][:, 0:P], ACT.Copy).then_inc(S("vt_set"), 1)
            A_(vt2[:], bank[7][:, P:P + 20], ACT.Copy).then_inc(S("vt_set"), 1)

            def squares(n, ready):
                for t in range(NT):
                    ready(t)
                    if t:
                        act.wait_ge(S("sq"), n * NT + t)
                    A_(junk[n], x[:, t, :], ACT.Square, accum_out=ss[:, t:t + 1]).then_inc(S("sq"), 1)

            def chunk_stage(n, b):
                act.wait_ge(S("proj_done"), n + 1)
                A_(stage[:], bank[b], ACT.Copy).then_inc(S("proj_evac"), 1)

            def chunk_evac(l, c, n, b):
                act.wait_ge(S("proj_done"), n + 1)
                dst = mod[:, l, 4 * c:4 * c + 4, :] if isinstance(c, int) else mod[:, l, bass.ds(c * 4, 4), :]
                A_(dst, bank[b][:, 0:8].rearrange("p (m c) -> p m c", c=2), ACT.Copy).then_inc(S("proj_evac"), 1)

            squares(0, lambda t: act.wait_ge(S("x_in"), 80))
            for j, (kind, c) in enumerate(PRE_ORDER):
                if kind == "part":
                    chunk_stage(j, j % 4)
                else:
                    chunk_evac(0, c, j, j % 4)

            def norm_evac(n, l, modulated):
                for t in range(NT):
                    c = 1 if t == PT else 0
                    act.wait_ge(S("tr"), n * NT + t + 1)
                    if t == 0 and modulated:
                        act.wait_ge(S("modA"), l + 1)
                    src = bank[2 * (t % 2)]
                    if modulated:
                        for k in range(4):
                            ins = A_(hT[:, k, tile_cols(t)], src[:, tile_cols(k)], ACT.Identity,
                                     scale=a1[:, l, k, c:c + 1], bias=mod[:, l, k, c:c + 1])
                    else:
                        ins = A_(hT[:, 0:4, tile_cols(t)], src.rearrange("p (k n) -> p k n", k=4), ACT.Copy)
                    ins.then_inc(S("hTa"), 1)

            norm_evac(0, 0, True)

            def y_evac(h):
                for t in range(NT):
                    act.wait_ge(S("yt_done"), h * NT - NT + t + 1)
                    if t >= 2:
                        act.wait_ge(S("op_done"), h * 10 - 10 + 2 * t - 2)
                    A_(yT[:, t % 2].rearrange("p j n -> p (j n)"), bank[4 + t % 2], ACT.Copy).then_inc(S("yt_evac"), 1)

            def head(h):
                first = isinstance(h, int)
                chunks = CHUNKS_FIRST if first else CHUNKS_LOOP
                gate, chunk_use, sum_use, _ = use_plan(chunks)
                b = use_base(h)
                if first:
                    act.wait_ge(S("mask_exp"), 8)
                    act.wait_ge(S("qdec_exp"), 8)
                else:
                    act.wait_ge(S("S_saved"), h * 32)
                    act.wait_ge(S("ln_done"), h * 10)
                for r in range(2):
                    act.dma_start(St[:, r], s_in[r][h]).then_inc(S("S_in"), 16)
                gsrc = gn_in[:, h * DV:h * DV + DV] if first else gn_in[:, bass.ds(h * DV, DV)]
                act.dma_start(gn, gsrc.partition_broadcast(P)).then_inc(S("gn_in"), 16)
                for j in range(4):
                    for s, cols in enumerate((slice(0, TS), slice(TS, T))):
                        act.wait_ge(S("proj_done"), b + 2 * j + s + 1)
                        dst = (qT if j < 2 else kT)[:, j % 2, cols]
                        A_(dst, bank[(2 * j + s) % 4][:, 0:cols.stop - cols.start], ACT.Copy,
                           scale=1.0 if j < 2 else DK ** -0.5).then_inc(S("proj_evac"), 1)
                if not first:
                    y_evac(h)
                for t in range(NT):
                    act.wait_ge(S("proj_done"), b + 8 + t + 1)
                    A_(vv[:, t, :], bank[(8 + t) % 4], ACT.Copy).then_inc(S("proj_evac"), 1)
                for i in range(10):
                    act.wait_ge(S("proj_done"), b + gate[i] + 1)
                    if not (first and i < 2):
                        act.wait_ge(S("ln_done"), h * 10 + i - 1)
                    A_(sg[:, i % 2, :], bank[gate[i] % 4], ACT.Silu).then_inc(S("proj_evac"), 1)
                    if i - 1 in chunks:
                        c = chunks[i - 1]
                        chunk_evac(0 if first else 1, PRE_CHUNKS + c if first else h * 4 + (c - 4), b + sum_use[c], sum_use[c] % 4)
                    if i in chunks:
                        n = chunk_use[chunks[i]]
                        chunk_stage(b + n, n % 4)
                act.wait_ge(S("S_upd"), h * NSS + NSS)
                for r in range(2):
                    act.dma_start(s_out[r][h], St[:, r]).then_inc(S("S_saved"), 16)

            def rows_evac(l):
                act.wait_ge(S("rows_T"), l + 1)
                if l:
                    act.wait_ge(S("rows_out"), 16 * l)
                A_(mod_rows[:], bank[4][0:96, 0:P], ACT.Copy).then_inc(S("rows_sb"), 1)

            head(0)
            rows_evac(0)
            with act.Fori(1, RH) as h:
                head(h)
            y_evac(RH)
            rows_evac(1)

            def moe(l):
                n = 2 * l + 1
                if l == 0:
                    act.wait_ge(S("S_saved"), 32 * RH)
                    squares(n, lambda t: act.wait_ge(S("x_add"), 10 * RH - 10 + 2 * t + 2))
                else:
                    act.wait_ge(S("cache_out"), 32)
                    squares(n, lambda t: act.wait_ge(S("mx_add"), 2 * t + 2))
                norm_evac(n, l, False)
                act.wait_ge(S("router_mm"), l * NT + NT)
                A_(rt[0].rearrange("p t e -> p (t e)"), bank[4][:, 0:NT * NE], ACT.Sigmoid).then_inc(S("sig_s"), 1)

                def x_evac(e):
                    act.wait_ge(S("tr_done"), l * NE + e.n + 1)
                    if not (isinstance(e.n, int) and e.n < 2):
                        act.wait_ge(S("gu_done"), l * NE + e.n - 1)
                    A_(xgT[:, e.par, 0:4, :].rearrange("p k n -> p (k n)"), bank[0], ACT.Copy).then_inc(S("xa"), 1)

                def silu(e):
                    act.wait_ge(S("gu_done"), l * NE + e.n + 1)
                    A_(gact[:, e.par, :], bank[2][:, 0:FF], ACT.Silu).then_inc(S("silu"), 1)

                def actT_evac(e):
                    act.wait_ge(S("at_done"), l * NE + e.n + 1)
                    A_(gactT[:, e.par].rearrange("p j n -> p (j n)"), bank[3][:, 0:FF], ACT.Copy).then_inc(S("actT"), 1)

                def y_store(e):
                    act.wait_ge(S("down_done"), l * NE + e.n + 1)
                    if not (isinstance(e.n, int) and e.n < 2):
                        act.wait_ge(S(f"y_out{e.par}"), l * 128 + e.half * 16)
                    A_(ysb[:, e.par, 0:512], bank[4 + 2 * e.par], ACT.Copy).then_inc(S("ya"), 1)
                    act.wait_ge(S("ya"), l * NE + e.n + 1)
                    act.wait_ge(S("yd"), l * NE + e.n + 1)
                    dst = ybuf[l][e.n * BLK:e.n * BLK + BLK, :] if isinstance(e.n, int) else ybuf[l][bass.ds(e.n * BLK, BLK), :]
                    act.dma_start(dst, ysb[:, e.par, :]).then_inc(S(f"y_out{e.par}"), 16)

                def one(e):
                    static = isinstance(e.n, int)
                    silu(e)
                    if not (static and e.n == NE - 1):
                        x_evac(e.plus(1))
                    if not (static and e.n == 0):
                        y_store(e.plus(-1))
                    actT_evac(e)

                x_evac(fixed(0, 4))
                for u in range(3):
                    one(fixed(u, 4))
                with act.Fori(0, 3) as i:
                    for u in range(3, 7):
                        one(Step(i, 4, u))
                one(fixed(NE - 1, 4))
                y_store(fixed(NE - 1, 4))
                overflow(act, l)

            moe(0)
            squares(2, lambda t: act.wait_ge(S("comb"), t + 1))
            norm_evac(2, 1, True)

            def lat_evac(t):
                act.wait_ge(S("lat_tr"), t + 1)
                for j in range(4):
                    ins = A_(cqT[:, j, tile_cols(t)], bank[2 * (t % 2)][:, tile_cols(j)], ACT.Copy,
                             scale=vt2[:, 16 + j:17 + j])
                ins.then_inc(S("lat_Ta"), 1)

            for t in range(NT):
                b0 = 4 + 2 * (t % 2)
                act.wait_ge(S("lat_done"), t + 1)
                if t:
                    act.wait_ge(S("lat_rstd"), 2 * t)
                    act.wait_ge(S("lat_sq"), 2 * t)
                A_(junk[2][:, 0:512], bank[b0], ACT.Square, accum_out=ss[:, 6:7]).then_inc(S("lat_sq"), 1)
                A_(junk[2][:, 512:768], bank[b0 + 1][:, 0:256], ACT.Square, accum_out=ss[:, 7:8]).then_inc(S("lat_sq"), 1)
                if t:
                    lat_evac(t - 1)
            lat_evac(NT - 1)
            for kt in range(6):
                act.wait_ge(S("v_done"), 2 * kt + 1)
                A_(V[:, kt, 0:512], bank[4 + (2 * kt) % 4], ACT.Copy).then_inc(S("va"), 1)
            SCALE = (NOPE + ROPE) ** -0.5

            def head_evac(h):
                act.wait_ge(S("hp_done"), h.n * 4 + 1)
                A_(qnT[:, h.par, 0:TS], bank[1], ACT.Copy).then_inc(S("hp_a"), 1)
                act.wait_ge(S("hp_done"), h.n * 4 + 3)
                A_(knT[:, h.par, 0:512], bank[3], ACT.Copy).then_inc(S("hp_a"), 1)

            def expo(h, t):
                g, gp = h.n * 5 + t, (h.par + t) % 2
                w = P if t == PT else 640
                act.wait_ge(S("mx"), g + 1)
                if not (isinstance(g, int) and g < 2):
                    act.wait_ge(S("pt_done"), g - 1)
                A_(pr[:, gp, 0:w], banks(2 * (t % 2), 2)[:, 0:w], ACT.Exp, bias=nmx[:, gp:gp + 1], scale=SCALE,
                   accum_out=sm_sum[:, t:t + 1]).then_inc(S("ex_done"), 1)

            def probT_evac(h, t):
                g, gp = h.n * 5 + t, (h.par + t) % 2
                act.wait_ge(S("pt_done"), g + 1)
                if not (isinstance(g, int) and g < 2):
                    act.wait_ge(S("pv_done"), g - 1)
                w = P if t == PT else 640
                A_(prT[:, gp].rearrange("p k n -> p (k n)")[:, 0:w], banks(4, 2)[:, 0:w], ACT.Copy).then_inc(S("pt_a"), 1)

            def main(h):
                expo(h, 0)
                expo(h, 1)
                probT_evac(h, 0)
                expo(h, 2)
                probT_evac(h, 1)
                expo(h, 3)
                probT_evac(h, 2)
                expo(h, 4)
                probT_evac(h, 3)

            head_evac(fixed(0, 2))
            main(fixed(0, 2))
            with act.Fori(0, 3) as i:
                for u in (1, 2):
                    h = Step(i, 2, u)
                    head_evac(h)
                    probT_evac(h.plus(-1), 4)
                    main(h)
            head_evac(fixed(MH - 1, 2))
            probT_evac(fixed(MH - 2, 2), 4)
            main(fixed(MH - 1, 2))
            probT_evac(fixed(MH - 1, 2), 4)
            for t in range(NT):
                act.wait_ge(S("o_tr"), t + 1)
                if t >= 2:
                    act.wait_ge(S("mo_done"), 2 * t - 2)
                A_(oTb[:, t % 2, 0:4, :].rearrange("p k n -> p (k n)"), bank[2 * (t % 2)], ACT.Copy).then_inc(S("oTa"), 1)
            moe(1)
            squares(4, lambda t: act.wait_ge(S("comb"), NT + t + 1))

        @block.vector
        def _(dve):
            v = nc.vector
            ch = Chain(dve, S("dve_step"))

            def cols2(ap, n):
                return ap.unsqueeze(2).to_broadcast([P, n, 2])

            def mod_first(l, hi):
                m = mod[:, l, 0:hi, :]
                ch.link(v.tensor_tensor(m, m, cols2(vt1[:, 48 * l:48 * l + hi], hi), ALU.add))
                v.scalar_tensor_tensor(out=a1[:, l], in0=mod[:, l, 8:16, :], scalar=1.0,
                                       in1=cols2(vt1[:, 96 + 8 * l:104 + 8 * l], 8), op0=ALU.add, op1=ALU.mult)\
                    .then_inc(S("modA"), 1)

            def mod_rest(l, lo):
                if lo < 48:
                    m = mod[:, l, lo:48, :]
                    ch.link(v.tensor_tensor(m, m, cols2(vt1[:, 48 * l + lo:48 * l + 48], 48 - lo), ALU.add))
                m = mod[:, l, 32:40, :]
                v.scalar_tensor_tensor(out=m, in0=m, scalar=1.0, in1=cols2(vt2[:, 8 * l:8 * l + 8], 8),
                                       op0=ALU.add, op1=ALU.mult).then_inc(S("modB"), 1)

            def norm(n, l):
                def evac(t):
                    c = 1 if t == PT else 0
                    dve.wait_ge(S("tr"), n * NT + t + 1)
                    src = bank[2 * (t % 2) + 1]
                    for k in range(4):
                        ins = v.tensor_scalar(hT[:, 4 + k, tile_cols(t)], src[:, tile_cols(k)], a1[:, l, 4 + k, c:c + 1],
                                              mod[:, l, 4 + k, c:c + 1], ALU.mult, ALU.add)
                    ins.then_inc(S("hTd"), 1)
                for t in range(NT):
                    dve.wait_ge(S("rstd"), n * NT + t + 1)
                    if t >= 2:
                        dve.wait_ge(S("tr"), n * NT + t - 1)
                    v.tensor_scalar(xn[l][:, t % 2, :], x[:, t, :], rs[:, t:t + 1], None, ALU.mult).then_inc(S("used"), 1)
                    if t == 1:
                        dve.wait_ge(S("modA"), l + 1)
                    if t:
                        evac(t - 1)
                evac(NT - 1)

            dve.wait_ge(S("gset"), 17)
            v.memset(cond[:, 16:46], 0.0).then_inc(S("pick2_set"), 1)
            v.tensor_reduce(pick2[:], ident[:].rearrange("p (g c) -> p c g", g=4)[:, 0:2, :], AX.X, ALU.add)\
                .then_inc(S("pick2_set"), 1)
            dve.wait_ge(S("vt_set"), 2)
            dve.wait_ge(S("proj_evac"), PRE)
            mod_first(0, 16)
            norm(0, 0)

            def op_evac(h):
                for t in range(NT):
                    c = 1 if t == PT else 0
                    for hf in range(2):
                        n = h * 10 + (2 * t + hf - 10)
                        dve.wait_ge(S("op_done"), n + 1)
                        if t or hf:
                            dve.wait_ge(S("x_add"), n)
                        v.tensor_tensor(t1, bank[6 + hf], g1[0][:, c, hf * 512:hf * 512 + 512], ALU.mult).then_inc(S("op_evac"), 1)
                        dve.wait_ge(S("op_evac"), n + 1)
                        xs = x[:, t, hf * 512:hf * 512 + 512]
                        v.tensor_tensor(xs, xs, t1, ALU.add).then_inc(S("x_add"), 1)

            def head(h):
                first = isinstance(h, int)
                chunks = CHUNKS_FIRST if first else CHUNKS_LOOP
                gate = use_plan(chunks)[0]
                b = use_base(h)

                def col(tile, r):
                    return tile[:, r * 4 + h:r * 4 + h + 1] if first else tile[:, bass.ds(h + r * 4, 1)]

                if not first:
                    op_evac(h)
                    dve.wait_ge(S("x_add"), h * 10)
                dve.wait_ge(S("att_done"), h * 2 + 1)
                for r in range(2):
                    m = mask[:, r * 4 + h:r * 4 + h + 1, :] if first else mask[:, bass.ds(h + r * 4, 1), :]
                    v.tensor_tensor(attm[:, r, 0:4, :], bank[4].rearrange("p (t n) -> p t n", t=4),
                                    m.to_broadcast([P, 4, P]), ALU.mult).then_inc(S("attm"), 1)
                dve.wait_ge(S("att_done"), h * 2 + 2)
                for r in range(2):
                    m = mask[:, r * 4 + h, :] if first else mask[:, bass.ds(h + r * 4, 1), :].rearrange("p a n -> p (a n)")
                    v.tensor_tensor(attm[:, r, 4, :], bank[5][:, 0:P], m, ALU.mult).then_inc(S("attm"), 1)

                def k_decay(u):
                    dve.wait_ge(S("kt_done"), h * NSS + u + 1)
                    if u >= 2:
                        dve.wait_ge(S("S_done"), h * NSS + u - 1)
                    v.tensor_scalar(kd[:, u % 2, :], bank[4][:, 0:DK], col(kdec, STEPS[STATE_STEPS[u]][1]), None,
                                    ALU.mult).then_inc(S("kd_ready"), 1)

                k_decay(0)
                dve.wait_ge(S("S_in"), h * 32 + 32)
                dve.wait_ge(S("gn_in"), h * 16 + 16)
                seen = set()
                for i, (t, r) in enumerate(STEPS):
                    if i in STATE_STEPS:
                        u = STATE_STEPS.index(i)
                        dve.wait_ge(S("S_done"), h * NSS + u + 1)
                        s = St[:, r].rearrange("p j d -> p (j d)")
                        if t == PT:
                            ins = v.tensor_copy(s, banks(6, 2))
                        else:
                            ins = v.scalar_tensor_tensor(out=s, in0=s, scalar=col(cdec, r), in1=banks(6, 2),
                                                         op0=ALU.mult, op1=ALU.add)
                        ins.then_inc(S("S_upd"), 1)
                        if u + 1 < NSS:
                            k_decay(u + 1)
                    dve.wait_ge(S("o_done"), h * 10 + i + 1)
                    ch.link(v.bn_stats(st6[:], bank[5]))
                    alone(dve)
                    v.bn_aggr(mv[:, i % 2, :], st6[:]).then_inc(S("stats"), 1)
                    dve.wait_ge(S("head_rstd"), h * 10 + i + 1)
                    v.tensor_scalar(t1, bank[5], mv[:, i % 2, 0:1], rv[:, i % 2:i % 2 + 1], ALU.subtract, ALU.mult)\
                        .then_inc(S("o_free"), 1)
                    dve.wait_ge(S("o_free"), h * 10 + i + 1)
                    ch.link(v.tensor_tensor(t1, t1, gn[:, r, :], ALU.mult))
                    dve.wait_ge(S("proj_evac"), b + gate[i] + 1)
                    if t not in seen:
                        seen.add(t)
                        v.tensor_tensor(yy[:, t, :], t1, sg[:, i % 2, :], ALU.mult).then_inc(S("ln_done"), 1)
                    else:
                        ch.link(v.tensor_tensor(t1, t1, sg[:, i % 2, :], ALU.mult))
                        v.tensor_tensor(yy[:, t, :], yy[:, t, :], t1, ALU.add).then_inc(S("ln_done"), 1)
                    dve.wait_ge(S("ln_done"), h * 10 + i + 1)

            dve.wait_ge(S("mask_tri"), 2)
            dve.wait_ge(S("cdec_set"), 1)
            dve.wait_ge(S("kdec_set"), 1)
            head(0)
            mod_rest(0, 16)
            dve.wait_ge(S("g1_in0"), 32)
            with dve.Fori(1, RH) as h:
                ch.c.enter(h, 1, 25)
                head(h)
            ch.c.leave(RH)
            mod_first(1, 48)
            mod_rest(1, 48)
            op_evac(RH)

            def moe(l):
                n = 2 * l + 1
                dve.wait_ge(S(f"rows_in{l}"), 96)
                if l:
                    dve.wait_ge(S("mx_add"), 10)

                def evac(t):
                    dve.wait_ge(S("tr"), n * NT + t + 1)
                    v.tensor_copy(hT[:, 4:8, tile_cols(t)], bank[2 * (t % 2) + 1].rearrange("p (k n) -> p k n", k=4))\
                        .then_inc(S("hTd"), 1)
                for t in range(NT):
                    c = 1 if t == PT else 0
                    dve.wait_ge(S("rstd"), n * NT + t + 1)
                    if t >= 2:
                        dve.wait_ge(S("tr"), n * NT + t - 1)
                        dve.wait_ge(S(f"h2_out{l}"), 16 * t - 16)
                    hb = h2b[:, t % 2, :]
                    v.scalar_tensor_tensor(out=hb, in0=x[:, t, :], scalar=rs[:, t:t + 1], in1=rows[:, 0, c, :],
                                           op0=ALU.mult, op1=ALU.mult).then_inc(S("used"), 1)
                    dve.wait_ge(S("used"), n * NT + t + 1)
                    v.tensor_tensor(hb, hb, rows[:, 1, c, :], ALU.add).then_inc(S("h2_ready"), 1)
                    if t:
                        evac(t - 1)
                evac(NT - 1)
                dve.wait_ge(S("misc_in"), 48)
                dve.wait_ge(S("sig_s"), l + 1)
                s, sbias, msk, chosen, oh1, oh2, tmp, tmp2 = rt[:8]
                grp = lambda ap: ap.rearrange("p t (g e) -> p (t g) e", g=NG)
                bc5 = lambda ap: ap.unsqueeze(1).to_broadcast([P, NT, NE])
                bce = lambda ap: ap.unsqueeze(2).to_broadcast([P, NT, NE])
                L = ch.link
                L(v.tensor_tensor(sbias, s, bc5(bias_row[:]), ALU.add))
                sgp = grp(sbias)
                pairs = M["rt"][:, 640:760].rearrange("p (q e) -> p q e", e=6)
                L(v.tensor_tensor(pairs[:, :, 0:3], sgp[:, :, 0:3], sgp[:, :, 1:4], ALU.add))
                L(v.tensor_tensor(pairs[:, :, 3:5], sgp[:, :, 0:2], sgp[:, :, 2:4], ALU.add))
                L(v.tensor_tensor(pairs[:, :, 5:6], sgp[:, :, 0:1], sgp[:, :, 3:4], ALU.add))
                gsc, geq, gkey, gpen = rq[0], rq[1], rq[2], rq[3]
                gmx, gidx = rq[4][:, 0:NT], rq[5][:, 0:NT]
                t4 = lambda ap: ap.rearrange("p (t g) -> p t g", g=NG)
                b4 = lambda ap: ap.unsqueeze(2).to_broadcast([P, NT, NG])
                L(v.tensor_reduce(gsc, pairs, AX.X, ALU.max))
                L(v.tensor_reduce(gmx, t4(gsc), AX.X, ALU.max))
                L(v.tensor_tensor(t4(geq), t4(gsc), b4(gmx), ALU.is_equal))
                g5 = lambda ap: ap.unsqueeze(1).to_broadcast([P, NT, NG])
                L(v.scalar_tensor_tensor(out=t4(gkey), in0=t4(geq), scalar=-100.0, in1=g5(idx16p[:, 0:NG]),
                                         op0=ALU.mult, op1=ALU.add))
                L(v.tensor_reduce(gidx, t4(gkey), AX.X, ALU.min))
                L(v.tensor_tensor(t4(geq), g5(idx16[:, 0:NG]), b4(gidx), ALU.is_equal))
                L(v.tensor_scalar(gpen, geq, BIG, -BIG, ALU.mult, ALU.add))
                L(v.tensor_tensor(grp(msk), sgp, gpen.unsqueeze(2).to_broadcast([P, NT * NG, 4]), ALU.add))

                def top(src, oh):
                    mx, ix = rq[6][:, 0:NT], rq[7][:, 0:NT]
                    L(v.tensor_reduce(mx, src, AX.X, ALU.max))
                    L(v.tensor_tensor(tmp, src, bce(mx), ALU.is_equal))
                    L(v.scalar_tensor_tensor(out=tmp2, in0=tmp, scalar=-100.0, in1=bc5(idx16p[:]), op0=ALU.mult, op1=ALU.add))
                    L(v.tensor_reduce(ix, tmp2, AX.X, ALU.min))
                    L(v.tensor_tensor(oh, bc5(idx16[:]), bce(ix), ALU.is_equal))
                top(msk, oh1)
                L(v.scalar_tensor_tensor(out=msk, in0=oh1, scalar=-BIG, in1=msk, op0=ALU.mult, op1=ALU.add))
                top(msk, oh2)
                v.tensor_tensor(chosen, oh1, oh2, ALU.add).then_inc(S("sel"), 1)
                for j, oh in enumerate((oh1, oh2)):
                    L(v.tensor_tensor(tmp, s, oh, ALU.mult))
                    L(v.tensor_reduce(wts[:, j, :], tmp, AX.X, ALU.add))
                L(v.tensor_tensor(wts[:, 2, :], wts[:, 0, :], wts[:, 1, :], ALU.add))
                L(v.reciprocal(wts[:, 2, :], wts[:, 2, :]))
                for j in range(2):
                    L(v.tensor_tensor(wts[:, j, :], wts[:, j, :], wts[:, 2, :], ALU.mult))
                dve.wait_ge(S("rank_done"), l + 1)
                L(v.tensor_copy(tmp.rearrange("p t e -> p (t e)"), bank[5][:, 0:NT * NE]))
                rank, slot, blk = rq[8][:, 0:10], rq[9][:, 0:10], rq[10][:, 0:10]
                for j, oh in enumerate((oh1, oh2)):
                    L(v.tensor_tensor(tmp2, tmp, oh, ALU.mult))
                    L(v.tensor_reduce(rank[:, 5 * j:5 * j + 5], tmp2, AX.X, ALU.add))
                    L(v.tensor_tensor(tmp2, bc5(ebase[:]), oh, ALU.mult))
                    L(v.tensor_reduce(slot[:, 5 * j:5 * j + 5], tmp2, AX.X, ALU.add))
                L(v.tensor_tensor(slot, slot, rank, ALU.add))
                L(v.tensor_scalar(blk, rank, float(BLK), None, ALU.is_ge))
                for n_ in range(2, CAP // BLK):
                    L(v.scalar_tensor_tensor(out=blk, in0=rank, scalar=float(n_ * BLK), in1=blk, op0=ALU.is_ge, op1=ALU.add))
                L(v.scalar_tensor_tensor(out=slot, in0=blk, scalar=float(NE * BLK - BLK), in1=slot,
                                         op0=ALU.mult, op1=ALU.add))
                v.tensor_copy(slots[:].rearrange("p j t -> p (j t)"), slot).then_inc(S("slots_ready"), 1)
                L(v.tensor_reduce(cntf[:], bank[5][:, NT * NE:NT * NE + NE], AX.X, ALU.max))
                v.tensor_copy(cnt[:], cntf[:]).then_inc(S("cnt_ready"), 1)

                def x_evac(e):
                    dve.wait_ge(S("tr_done"), l * NE + e.n + 1)
                    if not (isinstance(e.n, int) and e.n < 2):
                        dve.wait_ge(S("gu_done"), l * NE + e.n - 1)
                    v.tensor_copy(xgT[:, e.par, 4:8, :].rearrange("p k n -> p (k n)"), bank[1]).then_inc(S("xd"), 1)

                def act_mul(e):
                    dve.wait_ge(S("silu"), l * NE + e.n + 1)
                    v.tensor_tensor(gact[:, e.par, :], bank[2][:, FF:2 * FF], gact[:, e.par, :], ALU.mult).then_inc(S("act"), 1)

                def y_evac(e):
                    dve.wait_ge(S("down_done"), l * NE + e.n + 1)
                    if not (isinstance(e.n, int) and e.n < 2):
                        dve.wait_ge(S(f"y_out{e.par}"), l * 128 + e.half * 16)
                    v.tensor_copy(ysb[:, e.par, 512:1024], bank[5 + 2 * e.par]).then_inc(S("yd"), 1)

                def one(e):
                    static = isinstance(e.n, int)
                    act_mul(e)
                    if not (static and e.n == NE - 1):
                        x_evac(e.plus(1))
                    if not (static and e.n == 0):
                        y_evac(e.plus(-1))

                x_evac(fixed(0, 4))
                for u in range(3):
                    one(fixed(u, 4))
                with dve.Fori(0, 3) as i:
                    for u in range(3, 7):
                        one(Step(i, 4, u))
                one(fixed(NE - 1, 4))
                y_evac(fixed(NE - 1, 4))
                overflow(dve, l)
                for t in range(NT):
                    c = 1 if t == PT else 0
                    dve.wait_ge(S(f"pick{t % 2}_{l}"), 32 * (t // 2 + 1))
                    p0, p1 = picked[:, t % 2, 0, :], picked[:, t % 2, 1, :]
                    L(v.tensor_scalar(p0, p0, wts[:, 0, t:t + 1], None, ALU.mult))
                    L(v.scalar_tensor_tensor(out=p0, in0=p1, scalar=wts[:, 1, t:t + 1], in1=p0, op0=ALU.mult, op1=ALU.add))
                    L(v.tensor_tensor(p0, p0, rows[:, 2, c, :], ALU.mult))
                    v.tensor_tensor(x[:, t, :], x[:, t, :], p0, ALU.add).then_inc(S("comb"), 1)

            moe(0)
            dve.wait_ge(S("comb"), NT)
            norm(2, 1)

            dve.wait_ge(S("tab_in"), 80)
            dve.wait_ge(S("misc_in"), 48)

            def latent(t):
                b0 = 4 + 2 * (t % 2)
                dve.wait_ge(S("lat_rstd"), 2 * t + 2)
                if t >= 2:
                    dve.wait_ge(S("lat_tr"), t - 1)
                v.tensor_scalar(cqn[:, t % 2, :], bank[b0], rv[:, 0:1], None, ALU.mult)
                kv = bank[b0 + 1]
                v.scalar_tensor_tensor(out=ckvn[:, t % 2, :], in0=kv[:, 0:KVR], scalar=rv[:, 1:2], in1=kv_row[:],
                                       op0=ALU.mult, op1=ALU.mult)
                ax = lambda ap: ap.rearrange("p (a o n) -> p a o n", a=2, o=2)
                kp, sn, m = ax(kv[:, KVR:KVR + 64]), ax(tab[:, 1, t, :]), ax(kro[:, 64:128])
                v.tensor_tensor(kro[:, 0:64], kv[:, KVR:KVR + 64], tab[:, 0, t, :], ALU.mult)
                for o in range(2):
                    ins = v.tensor_tensor(m[:, :, o, :], kp[:, :, 1 - o, :], sn[:, :, o, :], ALU.mult)
                ins.then_inc(S("lat_used"), 1)
                dve.wait_ge(S("lat_used"), t + 1)
                for o in range(2):
                    ins = v.tensor_tensor(kr[:, t % 2, o * 64:o * 64 + 64], kro[:, 0:64], kro[:, 64:128], ALU.add)
                ins.then_inc(S("kr_ready"), 1)
                dve.wait_ge(S("kr_ready"), t + 1)

            def lat_evac_d(t):
                b1 = 2 * (t % 2) + 1
                cols = key_cols(t) if t < NT else slice(512, 640)
                dve.wait_ge(S("lat_tr"), t + 1)
                v.tensor_copy(ckT[:, :, cols], bank[b1][:, 0:256].rearrange("p (j n) -> p j n", j=2))
                v.tensor_copy(kpT[:, cols], bank[b1][:, 256:384]).then_inc(S("lat_Td"), 1)

            for t in range(NT):
                latent(t)
                if t:
                    lat_evac_d(t - 1)
            lat_evac_d(NT - 1)
            lat_evac_d(NT)
            for kt in range(6):
                dve.wait_ge(S("v_done"), 2 * kt + 2)
                v.tensor_copy(V[:, kt, 512:1024], bank[4 + (2 * kt + 1) % 4]).then_inc(S("vd"), 1)
            SCALE = (NOPE + ROPE) ** -0.5

            def head_evac(h):
                p = h.par
                dve.wait_ge(S("hp_done"), h.n * 4 + 2)
                v.tensor_tensor(qpT[:, p, 0:TS], bank[2], CS[:, 0:TS], ALU.mult).then_inc(S("hp_d"), 1)
                dve.wait_ge(S("hp_done"), h.n * 4 + 4)
                v.tensor_copy(qnT[:, p, TS:T], bank[7][:, 0:128])
                v.tensor_tensor(qpT[:, p, TS:T], bank[7][:, 128:256], CS[:, TS:T], ALU.mult)
                v.tensor_copy(knT[:, p, 512:768], bank[7][:, 256:512]).then_inc(S("hp_d"), 1)

            def row_max(h, t):
                g, gp = h.n * 5 + t, (h.par + t) % 2
                w = P if t == PT else 640
                dve.wait_ge(S("sc_done"), g + 1)
                ch.link(v.tensor_reduce(smx[:, gp:gp + 1], banks(2 * (t % 2), 2)[:, 0:w], AX.X, ALU.max))
                if not (isinstance(g, int) and g < 2):
                    dve.wait_ge(S("ex_done"), g - 1)
                v.tensor_scalar(nmx[:, gp:gp + 1], smx[:, gp:gp + 1], -SCALE, None, ALU.mult).then_inc(S("mx"), 1)

            def recip(h, t):
                dve.wait_ge(S("ex_done"), h.n * 5 + t + 1)
                ch.link(v.reciprocal(sm_inv[:, t:t + 1], sm_sum[:, t:t + 1]))

            def o_evac(h, t):
                dve.wait_ge(S("pv_done"), h.n * 5 + t + 1)
                dst = o_all[:, t, h.n * VD:h.n * VD + VD] if isinstance(h.n, int) else o_all[:, t, bass.ds(h.n * VD, VD)]
                v.tensor_scalar(dst, bank[6][:, 0:VD], sm_inv[:, t:t + 1], None, ALU.mult).then_inc(S("o_ev"), 1)

            def main(h):
                row_max(h, 0)
                row_max(h, 1)
                recip(h, 0)
                row_max(h, 2)
                recip(h, 1)
                o_evac(h, 0)
                row_max(h, 3)
                recip(h, 2)
                o_evac(h, 1)
                row_max(h, 4)
                recip(h, 3)
                o_evac(h, 2)

            def tail(h):
                recip(h, 4)
                o_evac(h, 3)
                o_evac(h, 4)

            head_evac(fixed(0, 2))
            main(fixed(0, 2))
            with dve.Fori(0, 3) as i:
                ch.c.enter(i, 0, 20)
                for u in (1, 2):
                    h = Step(i, 2, u)
                    head_evac(h)
                    tail(h.plus(-1))
                    main(h)
            ch.c.leave(3)
            head_evac(fixed(MH - 1, 2))
            tail(fixed(MH - 2, 2))
            main(fixed(MH - 1, 2))
            tail(fixed(MH - 1, 2))
            dve.wait_ge(S("g1_in1"), 32)

            def oT_evac(t):
                dve.wait_ge(S("o_tr"), t + 1)
                if t >= 2:
                    dve.wait_ge(S("mo_done"), 2 * t - 2)
                v.tensor_copy(oTb[:, t % 2, 4:8, :].rearrange("p k n -> p (k n)"), bank[2 * (t % 2) + 1]).then_inc(S("oTd"), 1)
            oT_evac(0)
            for t in range(NT):
                c = 1 if t == PT else 0
                if t + 1 < NT:
                    oT_evac(t + 1)
                for hf in range(2):
                    n = 2 * t + hf
                    dve.wait_ge(S("mo_done"), n + 1)
                    dve.wait_ge(S("mx_add"), n)
                    v.tensor_tensor(mtmp, bank[4 + 2 * (t % 2) + hf], g1[1][:, c, hf * 512:hf * 512 + 512], ALU.mult)\
                        .then_inc(S("mo_evac"), 1)
                    dve.wait_ge(S("mo_evac"), n + 1)
                    xs = x[:, t, hf * 512:hf * 512 + 512]
                    v.tensor_tensor(xs, xs, mtmp, ALU.add).then_inc(S("mx_add"), 1)
            moe(1)
            dve.wait_ge(S("comb"), 2 * NT)
            dve.wait_ge(S("fin_in"), 16)
            for t in range(NT):
                dve.wait_ge(S("rstd"), 4 * NT + t + 1)
                if t >= 2:
                    dve.wait_ge(S(f"fin_out{t % 2}"), 16 * (t // 2))
                v.scalar_tensor_tensor(out=fin[:, t % 2, :], in0=x[:, t, :], scalar=rs[:, t:t + 1], in1=fin_row,
                                       op0=ALU.mult, op1=ALU.mult).then_inc(S("fin_ready"), 1)


_INS = ["x_prompt", "x_sample", "state_ret_fwd", "state_ret_bwd", "cache_mla_ckv", "cache_mla_kpe", "c", "c_ctx",
        "w_ada", "b_ada", "norm1", "norm2", "norm_final", "ret_w_in", "ret_decay", "ret_gn", "ret_w_out",
        "mla_w_in", "mla_q_norm", "mla_kv_norm", "mla_w_uq", "mla_w_uk", "mla_w_uv", "mla_w_o",
        "w_router", "router_bias", "moe_w_gate", "moe_w_up", "moe_w_down"]
_OUTS = [(1, P, D), (1, TS, D), (1, 1, RH, DK, DV), (1, 1, RH, DK, DV), (1, 1, P, KVR), (1, 1, P, ROPE)]


def rope_tables():
    f = np.float32
    pos = np.arange(TS)
    row, col = (pos // 64).astype(f), (pos % 64).astype(f)
    half_w = ROPE // 2
    inv = (f(10000.0) ** (-np.arange(0, half_w, 2, dtype=f) / f(half_w))).astype(f)
    ang = np.stack([row[:, None] * inv, col[:, None] * inv], axis=1)
    cos = np.stack([np.cos(ang), np.cos(ang)], axis=2).reshape(TS, 64)
    sin = np.stack([-np.sin(ang), np.sin(ang)], axis=2).reshape(TS, 64)
    cos = np.concatenate([cos, np.ones((P, 64))]).astype(f)
    sin = np.concatenate([sin, np.zeros((P, 64))]).astype(f)
    cs = np.concatenate([cos, sin], axis=1).T
    tabs = np.stack([cos.reshape(NT, P, 64), sin.reshape(NT, P, 64)])
    return np.ascontiguousarray(cs), np.ascontiguousarray(tabs.transpose(2, 0, 1, 3).reshape(P, 2 * NT * 64))


def kernel(**inputs):
    import concourse.bacc as bacc
    from concourse.bass_utils import run_bass_kernel_spmd as run

    nc = bacc.Bacc("TRN2", target_bir_lowering=False, num_devices=1)
    arrays, a = {}, {}
    for name in _INS:
        arr = np.ascontiguousarray(inputs[name])
        arrays[f"in_{name}"] = arr
        a[name] = nc.dram_tensor(f"in_{name}", arr.shape, F32, kind="ExternalInput").ap()
    for name, arr in zip(("rope_cs", "rope_tab"), rope_tables()):
        arrays[f"in_{name}"] = arr
        a[name] = nc.dram_tensor(f"in_{name}", arr.shape, F32, kind="ExternalInput").ap()
    a["mod_rows_dram"] = nc.dram_tensor("mod_rows_dram", (2, 48, 2, P), F32, kind="Internal").ap()
    for key, shape, dt in (("h2_dram", (T, D), F32), ("slot_tok_dram", (NE * CAP, 1), I32), ("y_dram", (NE * CAP, D), F32)):
        a[key] = [nc.dram_tensor(f"{key}{l}", shape, dt, kind="Internal").ap() for l in range(2)]
    out = [nc.dram_tensor(f"out_{i}", s, F32, kind="ExternalOutput").ap() for i, s in enumerate(_OUTS)]
    build(nc, a, out)
    r = run(nc, [arrays], core_ids=[0])
    return tuple(r.results[0][f"out_{i}"] for i in range(len(_OUTS)))
```

```python
from contextlib import ExitStack

import numpy as np

import concourse.bass as bass
from concourse import mybir

F32 = mybir.dt.float32
I32 = mybir.dt.int32
ALU = mybir.AluOpType
ACT = mybir.ActivationFunctionType
AX = mybir.AxisListType

P = 128
D = 1024
KT = D // P
TS = 512
T = 640
NT = T // P
PT = NT - 1
EPS = 1e-6
RH, DK, DV = 4, 256, 512
MH, NOPE, ROPE, QR, KVR, VD = 8, 128, 64, 512, 256, 128
NE, NG, FF = 16, 4, 256
BIG = 1e30
CAP = T
BLK = P
ARENA = 19712

STEPS = [(0, 0), (3, 1), (1, 0), (2, 1), (2, 0), (1, 1), (3, 0), (0, 1), (4, 0), (4, 1)]
STATE_STEPS = [0, 1, 2, 3, 4, 5, 8, 9]
NSS = len(STATE_STEPS)

CHUNKS_FIRST = {i: i for i in range(8)}
CHUNKS_LOOP = {1: 0, 3: 1, 5: 2, 7: 3}
SLOTS_FIRST = [4, 0, 1, 4, 0, 1, 4, 1]
SLOTS_LOOP = [0, 4, 1, 4]
PRE_CHUNKS = 4
PRE_ORDER = [(kind, c) for c in range(PRE_CHUNKS) for kind in ("part", "sum")]
PRE_SLOTS = (2, 3, 4, 1)
PRE = len(PRE_ORDER)


def use_plan(chunks):
    gate, chunk, total, n = {}, {}, {}, 13
    for i in range(len(STEPS)):
        gate[i] = n
        n += 1
        if i - 1 in chunks:
            total[chunks[i - 1]] = n
            n += 1
        if i in chunks:
            chunk[chunks[i]] = n
            n += 1
    assert n % 4 in (0, 3)
    return gate, chunk, total, n


_, CHUNK_F, _, USES_F = use_plan(CHUNKS_FIRST)
_, CHUNK_L, _, USES_L = use_plan(CHUNKS_LOOP)
AFTER_CHUNKS = USES_L - 1 - CHUNK_L[3]
assert AFTER_CHUNKS == USES_F - 1 - CHUNK_F[7]
AFTER_SLOT0 = min(USES_F - CHUNK_F[4] - 1, USES_L - CHUNK_L[0] - 1)


T_BANK = {0: (4, 6, 0, 2, 4), 2: (0, 0, 0, 0, 0)}
R_BANK = (2, 6)


def use_base(h):
    if isinstance(h, int) and h == 0:
        return PRE
    return h * USES_L + (PRE + USES_F - USES_L)


class Count:

    def __init__(self, step=1):
        self.step, self.base, self.n = step, 0, 0

    def next(self, k=1):
        self.n += k
        return self.base + self.n * self.step

    def now(self):
        return self.base + self.n * self.step

    def enter(self, reg, first, per):
        self.start, self.per, self.first = self.base + self.n * self.step, per, first
        self.base, self.n = reg * (per * self.step) + (self.start - first * per * self.step), 0

    def leave(self, last):
        assert self.n == self.per, (self.n, self.per)
        self.base, self.n = self.start + (last - self.first) * self.per * self.step, 0


class Step:

    def __init__(self, reg, per, u):
        self.reg, self.per, self.u = reg, per, u
        self.par = u % 2
        self.buf = u % 4
        self.n = reg * per + u
        self.half = reg * (per // 2) + u // 2
        self.quarter = reg + u // 4 if per == 4 else None

    def plus(self, k):
        return Step(self.reg, self.per, self.u + k)


def fixed(n, per):
    return Step(0, per, n)


class Chain:

    def __init__(self, eng, sem):
        self.eng, self.sem, self.c = eng, sem, Count()

    def link(self, ins):
        ins.then_inc(self.sem, 1)
        self.eng.wait_ge(self.sem, self.c.next())


def build(nc, a, out):
    ctx = ExitStack()
    with ctx:
        def sb(name, shape, dt=F32):
            return ctx.enter_context(nc.sbuf_tensor(name, shape, dt))

        sems = {}

        def S(name):
            if name not in sems:
                sems[name] = ctx.enter_context(nc.semaphore(name))
            return sems[name]

        x = sb("x", [P, NT, D])
        wr = sb("wr", [P, 5 * 4096 + KT * T])
        arena = sb("arena", [P, ARENA])
        ident = sb("ident", [P, P])
        ones = sb("ones", [P, P])
        before = sb("before", [P, P])
        vraw = sb("vraw", [P, P])
        vraw2 = sb("vraw2", [20, P])
        vt1 = sb("vt1", [P, P])
        vt2 = sb("vt2", [P, 20])
        mod = sb("mod", [P, 2, 48, 2])
        mod_rows = sb("mod_rows", [96, P])
        a1 = sb("a1", [P, 2, 8, 2])
        cond = sb("cond", [P, KT * 2 + 30])
        stage = sb("stage", [P, 512])
        pick2 = sb("pick2", [P, 2])
        w_rt = sb("w_rt", [P, KT, NE])
        bias_row = sb("bias_row", [P, NE])
        kv_row = sb("kv_row", [P, KVR])
        idx16 = sb("idx16", [P, NE])
        idx16p = sb("idx16p", [P, NE])
        ebase = sb("ebase", [P, NE])
        tok_id = sb("tok_id", [P, NT], I32)
        zero_id = sb("zero_id", [P, NE * CAP // P], I32)
        epsc = sb("epsc", [P, 1])
        half = sb("half", [P, 1])
        lg = sb("lg", [P, 8])
        lgk = sb("lgk", [P, 8])
        kdec = sb("kdec", [P, 8])
        cdec = sb("cdec", [P, 8])
        pf = sb("pf", [P, 2])
        ss = sb("ss", [P, 8])
        rs = sb("rs", [P, 8])
        st6 = sb("st6", [P, 6])
        mv = sb("mv", [P, 2, 2])
        rv = sb("rv", [P, 2])
        smx = sb("smx", [P, 2])
        nmx = sb("nmx", [P, 2])
        sm_sum = sb("sm_sum", [P, NT])
        sm_inv = sb("sm_inv", [P, NT])
        cntf = sb("cntf", [P, 1])
        cnt = sb("cnt", [P, 1], I32)
        slots = sb("slots", [P, 2, NT], I32)
        ids = sb("ids", [P, NE], I32)
        idc = sb("idc", [P, 2], I32)
        wts = sb("wts", [P, 3, NT])
        slot_w = sb("slot_w", [P, NE])
        gate_rows = sb("gate_rows", [P, NE])
        row_no = sb("row_no", [P, P])
        tok_f = sb("tok_f", [P, NT])
        PSUM = ctx.enter_context(nc.psum_tensor("banks", [P, 8, 512], F32))
        bank = [PSUM[:, i, :] for i in range(8)]

        def banks(b, n):
            return PSUM[:, b:b + n, :].rearrange("p b n -> p (b n)")

        def ring(s):
            return wr[:, s * 4096:(s + 1) * 4096]

        def ring8(s):
            return ring(s).rearrange("p (k n) -> p k n", k=KT)

        hT = wr[:, 20480:25600].rearrange("p (k t) -> p k t", k=KT)

        def carve(sizes):
            views, at = {}, 0
            for name, n in sizes:
                views[name] = arena[:, at:at + n]
                at += n
            assert at <= ARENA, at
            return views

        R = carve([("mask", 1024), ("qdec", 1024), ("q", 1280), ("k", 1280), ("v", 2560), ("sg", 1024),
                   ("S", 2048), ("attm", 1280), ("qd", 512), ("kd", 512), ("gn", 1024),
                   ("y", 2560), ("t1", 512), ("yT", 1024), ("g1", 2048)])
        mask = R["mask"].rearrange("p (c n) -> p c n", c=8)
        qdec = R["qdec"].rearrange("p (c n) -> p c n", c=8)
        qT = R["q"].rearrange("p (j t) -> p j t", j=2)
        kT = R["k"].rearrange("p (j t) -> p j t", j=2)
        vv = R["v"].rearrange("p (t d) -> p t d", t=NT)
        sg = R["sg"].rearrange("p (b d) -> p b d", b=2)
        yy = R["y"].rearrange("p (t d) -> p t d", t=NT)
        St = R["S"].rearrange("p (r j d) -> p r j d", r=2, j=2)
        attm = R["attm"].rearrange("p (r t n) -> p r t n", r=2, t=NT)
        qd = R["qd"].rearrange("p (b j n) -> p b j n", b=2, j=2)
        kd = R["kd"].rearrange("p (b n) -> p b n", b=2)
        gn = R["gn"].rearrange("p (r d) -> p r d", r=2)
        t1 = R["t1"]
        yT = R["yT"].rearrange("p (b j n) -> p b j n", b=2, j=4)
        g1 = [R["g1"].rearrange("p (c d) -> p c d", c=2)]
        dist = R["S"][:, 0:512].rearrange("p (c n) -> p c n", c=4)

        M = carve([("rows", 6144), ("rt", 1200), ("h2", 2048), ("xg", 2048), ("xgT", 2048),
                   ("act", 512), ("actT", 512), ("ysb", 2048)])
        rows = M["rows"].rearrange("p (g c d) -> p g c d", g=3, c=2)
        rt = [M["rt"][:, 80 * i:80 * i + 80].rearrange("p (t e) -> p t e", t=NT) for i in range(12)]
        rq = [M["rt"][:, 960 + 20 * i:980 + 20 * i] for i in range(12)]
        h2b = arena[:, 6144 + 1200:6144 + 1200 + 4 * D].rearrange("p (b d) -> p b d", b=4)
        onehot = M["xgT"][:, 0:10 * P].rearrange("p (q n) -> p q n", n=P)
        pairs = M["rt"][:, 640:760].rearrange("p (q e) -> p q e", e=6)
        sent = M["rt"][:, 640:960].rearrange("p (q o e) -> p q o e", o=2, e=NE)
        gate_dense = M["rt"][:, 480:560].rearrange("p (t e) -> p t e", t=NT)
        xg = M["xg"].rearrange("p (b d) -> p b d", b=2)
        xgT = M["xgT"].rearrange("p (b k n) -> p b k n", b=2, k=KT)
        h2T = xgT
        gact = M["act"].rearrange("p (b f) -> p b f", b=2)
        gactT = M["actT"].rearrange("p (b j n) -> p b j n", b=2, j=2)
        ysb = M["ysb"].rearrange("p (b d) -> p b d", b=2)
        picked = [M["rows"][:, i * D:(i + 1) * D] for i in range(4)] + [M["h2"][:, 0:D]]
        fin_row = M["xg"][:, 0:D]
        fin = M["xgT"].rearrange("p (b d) -> p b d", b=2)

        def expert_w(b):
            w = wr[:, b * 6144:(b + 1) * 6144]
            return (w[:, 0:4096].rearrange("p (k g f) -> p k g f", k=KT, g=2),
                    w[:, 4096:6144].rearrange("p (j d) -> p j d", j=2))

        A = carve([("wq", 2048), ("wk", 512), ("kT", 1536), ("qT", 1280), ("qpe", 1280), ("P", 1280), ("PT", 1280),
                   ("cqT", 2560), ("CS", 640), ("tab", 640), ("cqn", 1024), ("ckvn", 512), ("kr", 256),
                   ("cache", 384), ("g1", 2048), ("xn", 2048)])
        wq = A["wq"].rearrange("p (b k n) -> p b k n", b=2, k=4)
        wk = A["wk"].rearrange("p (b k n) -> p b k n", b=2, k=2)
        knT = A["kT"].rearrange("p (b t) -> p b t", b=2)
        qnT = A["qT"].rearrange("p (b t) -> p b t", b=2)
        qpT = A["qpe"].rearrange("p (b t) -> p b t", b=2)
        pr = A["P"].rearrange("p (b t) -> p b t", b=2)
        prT = A["PT"].rearrange("p (b k n) -> p b k n", b=2, k=5)
        cqT = A["cqT"].rearrange("p (j t) -> p j t", j=4)
        CS = A["CS"]
        tab = A["tab"].rearrange("p (g t n) -> p g t n", g=2, t=NT)
        cqn = A["cqn"].rearrange("p (b n) -> p b n", b=2)
        ckvn = A["ckvn"].rearrange("p (b n) -> p b n", b=2)
        kr = A["kr"].rearrange("p (b n) -> p b n", b=2)
        c_ckv, c_kpe = A["cache"][:, 0:256], A["cache"][:, 256:384]
        g1.append(A["g1"].rearrange("p (c d) -> p c d", c=2))
        xn = [R["y"][:, 0:2048].rearrange("p (b d) -> p b d", b=2), A["xn"].rearrange("p (b d) -> p b d", b=2)]
        junk = {0: R["v"][:, 0:D], 1: wr[:, 12288:12288 + D], 2: A["cqT"][:, 0:D], 3: wr[:, 16896:16896 + D], 4: M["h2"][:, D:2 * D]}
        lat_junk = A["P"][:, 0:768]
        kro = A["PT"][:, 0:128]
        w_in = wr[:, 0:6656].rearrange("p (k n) -> p k n", k=KT)
        V = wr[:, 0:6144].rearrange("p (t n) -> p t n", t=6)
        w_uv = wr[:, 6656:8704].rearrange("p (k n) -> p k n", k=2)
        w_o = wr[:, 8704:16896].rearrange("p (k n) -> p k n", k=MH)
        ckT = wr[:, 16896:18432].rearrange("p (j t) -> p j t", j=2)
        kpT = wr[:, 18432:19200]
        o_all = wr[:, 20480:25600].rearrange("p (t n) -> p t n", t=NT)
        oTb = A["xn"].rearrange("p (b k n) -> p b k n", b=2, k=KT)
        mtmp = A["cqn"][:, 512:1024]

        w_ada = a["w_ada"].rearrange("l (k p) n -> l p k n", p=P)
        w_ret = a["ret_w_in"][0].rearrange("(k p) n -> p k n", p=P)
        w_out = a["ret_w_out"][0].rearrange("(j p) n -> p j n", p=P)
        w_g = a["moe_w_gate"].rearrange("l e (k p) f -> l e p k f", p=P)
        w_u = a["moe_w_up"].rearrange("l e (k p) f -> l e p k f", p=P)
        w_d = a["moe_w_down"].rearrange("l e (k p) d -> l e p k d", p=P)
        w_uq = a["mla_w_uq"][0].rearrange("(k p) n -> p k n", p=P)
        w_uk = a["mla_w_uk"][0].rearrange("(k p) h n -> p k (h n)", p=P)
        s_in = [a["state_ret_fwd"][0, 0].rearrange("h (j p) d -> h p j d", p=P),
                a["state_ret_bwd"][0, 0].rearrange("h (j p) d -> h p j d", p=P)]
        s_out = [out[2][0, 0].rearrange("h (j p) d -> h p j d", p=P),
                 out[3][0, 0].rearrange("h (j p) d -> h p j d", p=P)]
        gn_in = a["ret_gn"][0]
        mrow = a["mod_rows_dram"]
        gate_d = a["gate_dram"]
        h2d, slot_tok, ybuf = a["h2_dram"], a["slot_tok_dram"], a["y_dram"]

        def alone(eng):
            eng.sem_inc(S("alone"), 1)

        def gate_row(l, j, c):
            return mrow[l, 8 * j:8 * j + 8, c, :].partition_broadcast(P)

        block = ctx.enter_context(nc.Block())

        def mod_rows_out(eng, l):
            eng.wait_ge(S("rows_sb"), l + 1)
            eng.dma_start(mrow[l].rearrange("m c p -> (m c) p"), mod_rows[:]).then_inc(S(f"rows_out{l}"), 16)
            eng.wait_ge(S(f"rows_out{l}"), 16)

        def tile_cols(t):
            return slice(t * P, (t + 1) * P)

        def key_cols(t):
            return slice(640, 768) if t == PT else tile_cols(t)

        def overflow_guard(eng, l):
            eng.wait_ge(S("cnt_ready"), l + 1)
            r = eng.value_load(cnt[0:1, 0:1], min_val=0, max_val=T)
            with eng.If(r > BLK):
                eng.wait_ge(S(f"ov_out{l}"), 16 * NE * (CAP // BLK - 1))

        def overflow(eng, l):
            eng.wait_ge(S("cnt_ready"), l + 1)
            r = eng.value_load(cnt[0:1, 0:1], min_val=0, max_val=T)
            nb = CAP // BLK - 1
            gu, dn = expert_w(3)
            kind = {nc.gpsimd: "pool", nc.tensor: "pe", nc.scalar: "act", nc.vector: "dve"}
            who = [v for k, v in kind.items() if k is eng][0]
            with eng.If(r > BLK):
                if who == "pool":
                    eng.wait_ge(S("down_done"), l * NE + NE)
                    eng.wait_ge(S("y_out0"), l * 128 + 128)
                    eng.wait_ge(S("y_out1"), l * 128 + 128)
                    eng.wait_ge(S("slot_zero"), 32)
                    eng.wait_ge(S(f"ov_gate{l}"), 1)
                    eng.dma_start(gate_d[l].rearrange("(t p) e -> p t e", p=P), gate_dense).then_inc(S(f"ov_set{l}"), 16)
                    for t in range(NT):
                        for j in range(2):
                            nc.gpsimd.indirect_dma_start(
                                out=slot_tok[l], out_offset=bass.IndirectOffsetOnAxis(ap=slots[:, j, t:t + 1], axis=0),
                                in_=tok_id[:, t:t + 1], in_offset=None).then_inc(S(f"ov_set{l}"), 16)
                    eng.wait_ge(S(f"ov_set{l}"), 176)
                if who == "dve":
                    nc.vector.tensor_tensor(gate_dense, sent[:, 0:NT, 1, :], sent[:, NT:2 * NT, 1, :], ALU.add)\
                        .then_inc(S(f"ov_gate{l}"), 1)
                with eng.Fori(0, NE) as e:
                    with eng.Fori(0, nb) as b:
                        n = e * nb + b
                        row = b * (NE * BLK) + e * BLK + NE * BLK
                        if who == "pool":
                            eng.dma_start(gu[:, :, 0, :], w_g[l][e]).then_inc(S(f"ov_w{l}"), 16)
                            eng.dma_start(gu[:, :, 1, :], w_u[l][e]).then_inc(S(f"ov_w{l}"), 16)
                            eng.dma_start(dn, w_d[l][e]).then_inc(S(f"ov_w{l}"), 16)
                            eng.dma_start(idc[:, 0:1], slot_tok[l][bass.ds(row, BLK), :]).then_inc(S(f"ov_i{l}"), 16)
                            eng.wait_ge(S(f"ov_i{l}"), n * 16 + 16)
                            alone(eng)
                            nc.gpsimd.indirect_dma_start(out=xg[:, 0, :], out_offset=None, in_=h2d[l],
                                                         in_offset=bass.IndirectOffsetOnAxis(ap=idc[:, 0:1], axis=0))\
                                .then_inc(S(f"ov_g{l}"), 16)
                            nc.gpsimd.indirect_dma_start(out=gate_rows[:], out_offset=None, in_=gate_d[l],
                                                         in_offset=bass.IndirectOffsetOnAxis(ap=idc[:, 0:1], axis=0))\
                                .then_inc(S(f"ov_g{l}"), 16)
                            eng.wait_ge(S(f"ov_out{l}"), n * 16 + 16)
                        if who == "pe":
                            eng.wait_ge(S(f"ov_w{l}"), n * 48 + 48)
                            eng.wait_ge(S(f"ov_g{l}"), n * 32 + 32)
                            for k in range(KT):
                                mm = nc.tensor.transpose(banks(0, 2)[:, tile_cols(k)], xg[:, 0, tile_cols(k)], ident[:])
                            mm.then_inc(S(f"ov_pe{l}"), 1)
                            eng.wait_ge(S(f"ov_ev{l}"), n * 4 + 1)
                            for k in range(KT):
                                mm = nc.tensor.matmul(bank[2], xgT[:, 0, k, :], gu[:, k].rearrange("p g f -> p (g f)"),
                                                      start=(k == 0), stop=(k == KT - 1))
                            mm.then_inc(S(f"ov_pe{l}"), 1)
                            eng.wait_ge(S(f"ov_ev{l}"), n * 4 + 2)
                            for j in range(2):
                                mm = nc.tensor.transpose(bank[3][:, tile_cols(j)], gact[:, 0, tile_cols(j)], ident[:])
                            mm.then_inc(S(f"ov_pe{l}"), 1)
                            eng.wait_ge(S(f"ov_ev{l}"), n * 4 + 3)
                            for hf in range(2):
                                for j in range(2):
                                    mm = nc.tensor.matmul(bank[4 + hf], gactT[:, 0, j, :], dn[:, j, hf * 512:hf * 512 + 512],
                                                          start=(j == 0), stop=(j == 1))
                            mm.then_inc(S(f"ov_pe{l}"), 1)
                        if who == "act":
                            eng.wait_ge(S(f"ov_pe{l}"), n * 4 + 2)
                            nc.scalar.activation(gact[:, 0, :], bank[2][:, 0:FF], ACT.Silu).then_inc(S(f"ov_sig{l}"), 1)
                            eng.wait_ge(S(f"ov_ev{l}"), n * 4 + 4)
                            eng.dma_start(ybuf[l][bass.ds(row, BLK), :], ysb[:, 0, :]).then_inc(S(f"ov_out{l}"), 16)
                        if who == "dve":
                            eng.wait_ge(S(f"ov_pe{l}"), n * 4 + 1)
                            nc.vector.tensor_copy(xgT[:, 0].rearrange("p k n -> p (k n)"), banks(0, 2)).then_inc(S(f"ov_ev{l}"), 1)
                            eng.wait_ge(S(f"ov_sig{l}"), n + 1)
                            eng.wait_ge(S(f"ov_g{l}"), n * 32 + 32)
                            alone(eng)
                            nc.vector.scalar_tensor_tensor(out=gact[:, 0, :], in0=bank[2][:, FF:2 * FF],
                                                           scalar=gate_rows[:, bass.ds(e, 1)], in1=gact[:, 0, :],
                                                           op0=ALU.mult, op1=ALU.mult).then_inc(S(f"ov_ev{l}"), 1)
                            eng.wait_ge(S(f"ov_pe{l}"), n * 4 + 3)
                            nc.vector.tensor_copy(gactT[:, 0].rearrange("p j n -> p (j n)"), bank[3][:, 0:256]).then_inc(S(f"ov_ev{l}"), 1)
                            eng.wait_ge(S(f"ov_pe{l}"), n * 4 + 4)
                            nc.vector.tensor_copy(ysb[:, 0, :], banks(4, 2)).then_inc(S(f"ov_ev{l}"), 1)
                if who == "pool":
                    eng.wait_ge(S(f"ov_out{l}"), 16 * NE * nb)
        @block.sync
        def _(sp):
            sp.dma_start(vraw[0:96, :], a["b_ada"].rearrange("l (m p) -> (l m) p", p=P)).then_inc(S("vec_in"), 16)
            sp.dma_start(vraw[96:112, :], a["norm1"].rearrange("l (m p) -> (l m) p", p=P)).then_inc(S("vec_in"), 16)
            sp.dma_start(vraw[112:120, :], a["c"].rearrange("l (m p) -> (l m) p", p=P)).then_inc(S("vec_in"), 16)
            sp.dma_start(vraw[120:128, :], a["c_ctx"].rearrange("(m p) -> m p", p=P)).then_inc(S("vec_in"), 16)
            sp.dma_start(vraw2[0:16, :], a["norm2"].rearrange("l (m p) -> (l m) p", p=P)).then_inc(S("vec_in"), 16)
            sp.dma_start(vraw2[16:20, :], a["mla_q_norm"].rearrange("l (m p) -> (l m) p", p=P)).then_inc(S("vec_in"), 16)
            sp.dma_start(lg[:], a["ret_decay"].rearrange("a r h -> (a r h)").partition_broadcast(P)).then_inc(S("lg_in"), 16)

            def load(s, dst, src):
                sp.dma_start(dst, src).then_inc(S(f"ring_full{s}"), 16)

            def load_chunk(l, c, s):
                if isinstance(c, int):
                    src = w_ada[l][:, :, c * 512:(c + 1) * 512]
                else:
                    src = w_ada[l][:, :, bass.ds(c * 512, 512)]
                load(s, ring8(s), src)

            load_chunk(0, 0, PRE_SLOTS[0])
            load_chunk(0, 1, PRE_SLOTS[1])
            load_chunk(0, 2, PRE_SLOTS[2])
            load_chunk(0, 3, PRE_SLOTS[3])
            for t in range(NT):
                src = a["x_prompt"][0] if t == PT else a["x_sample"][0, t * P:(t + 1) * P, :]
                sp.dma_start(x[:, t, :], src).then_inc(S(f"x_in{(t + 1) // 2}"), 16)

            def head_loads(h):
                first = isinstance(h, int)
                chunk = CHUNK_F if first else CHUNK_L
                b = use_base(h)
                if not first:
                    sp.wait_ge(S("proj_done"), b - AFTER_SLOT0)
                for off in (0, RH * DK):
                    at = off + h * DK
                    dst = ring8(0)[:, :, 0:DK] if off == 0 else ring8(0)[:, :, DK:2 * DK]
                    src = w_ret[:, :, at:at + DK] if first else w_ret[:, :, bass.ds(at, DK)]
                    load(0, dst, src)
                if not first:
                    sp.wait_ge(S("proj_done"), b - AFTER_CHUNKS)
                    load(4, ring(4).rearrange("p (j n) -> p j n", j=4), w_out[:, bass.ds(h * 4 - 4, 4), :])
                for s, off in ((1, 2 * RH * DK), (2, 2 * RH * DK + RH * DV), (3, 2 * RH * DK + 2 * RH * DV)):
                    if s == 1 and first:
                        sp.wait_ge(S("proj_done"), PRE)
                    if s == 2 and not first:
                        sp.wait_ge(S("proj_done"), b - 2)
                    if s == 3 and not first:
                        sp.wait_ge(S("proj_done"), b)
                    at = off + h * DV
                    load(s, ring8(s), w_ret[:, :, at:at + DV] if first else w_ret[:, :, bass.ds(at, DV)])
                if first:
                    last = {0: b + 8, 1: b + 13, 4: PRE}
                    for j, s in enumerate(SLOTS_FIRST):
                        sp.wait_ge(S("proj_done"), last[s])
                        load_chunk(0, 4 + j, s)
                        last[s] = b + chunk[j] + 1
                else:
                    sp.wait_ge(S("proj_done"), b + 8)
                    load_chunk(1, h * 4 - 4, 0)
                    sp.wait_ge(S("op_done"), h * 10)
                    load_chunk(1, h * 4 - 3, 4)
                    sp.wait_ge(S("proj_done"), b + 13)
                    load_chunk(1, h * 4 - 2, 1)
                    sp.wait_ge(S("proj_done"), b + chunk[1] + 1)
                    load_chunk(1, h * 4 - 1, 4)

            head_loads(0)
            sp.dma_start(w_rt[:], a["w_router"].rearrange("(k p) e -> p k e", p=P)).then_inc(S("misc_in"), 16)
            sp.dma_start(bias_row[:], a["router_bias"].partition_broadcast(P)).then_inc(S("misc_in"), 16)
            sp.dma_start(kv_row[:], a["mla_kv_norm"][0].partition_broadcast(P)).then_inc(S("misc_in"), 16)
            sp.wait_ge(S("gset"), 20)
            for l in range(2):
                sp.dma_start(slot_tok[l].rearrange("(p n) o -> p (n o)", p=P), zero_id[:]).then_inc(S("slot_zero"), 16)
            with sp.Fori(1, RH) as h:
                head_loads(h)
            sp.wait_ge(S("proj_done"), use_base(RH) - AFTER_CHUNKS)
            load(4, ring(4).rearrange("p (j n) -> p j n", j=4), w_out[:, 12:16, :])

            def moe_loads(l):
                def w_load(e, b):
                    gu, dn = expert_w(b)
                    sp.dma_start(gu[:, :, 0, :], w_g[l][e]).then_inc(S(f"w_full{b}"), 16)
                    sp.dma_start(gu[:, :, 1, :], w_u[l][e]).then_inc(S(f"w_full{b}"), 16)
                    sp.dma_start(dn, w_d[l][e]).then_inc(S(f"w_full{b}"), 16)
                if l == 0:
                    sp.wait_ge(S("proj_done"), use_base(RH))
                    sp.wait_ge(S("ln_done"), 10 * RH)
                    sp.wait_ge(S("S_saved"), 32 * RH)
                else:
                    sp.wait_ge(S("pv_done"), 5 * MH)
                if l == 0:
                    sp.wait_ge(S("rows_out0"), 16)
                for g, j in ((0, 4), (1, 3), (2, 5)):
                    for c in range(2):
                        sp.dma_start(rows[:, g, c, :].rearrange("p (m q) -> p m q", m=8), gate_row(l, j, c))\
                            .then_inc(S(f"rows_in{l}"), 16)
                w_load(0, 0)
                if l == 0:
                    w_load(1, 1)
                for t in range(NT):
                    if l and t == NT - 1:
                        sp.wait_ge(S("o_tr"), NT)
                        w_load(3, 3)
                    sp.wait_ge(S("h2_ready"), l * NT + t + 1)
                    sp.dma_start(h2d[l][t * P:(t + 1) * P, :], h2b[:, t % 4, :])\
                        .then_inc(S(f"h2_out{l}" if t else "h2_first"), 16)
                if l == 0:
                    sp.wait_ge(S("op_done"), 10 * RH)
                else:
                    sp.wait_ge(S("mo_done"), 10)
                    w_load(1, 1)
                w_load(2, 2)
                if l == 0:
                    w_load(3, 3)
                with sp.Fori(0, 3) as i:
                    for b in range(4):
                        sp.wait_ge(S("down_done"), l * NE + i * 4 + b + 1)
                        w_load(i * 4 + b + 4, b)

            moe_loads(0)
            mod_rows_out(sp, 1)
            sp.wait_ge(S("down_done"), NE - 2)
            sp.dma_start(w_in, a["mla_w_in"][0].rearrange("(k p) n -> p k n", p=P)).then_inc(S("mw_in"), 16)
            sp.dma_start(w_uv, a["mla_w_uv"][0].rearrange("(k p) h n -> p k (h n)", p=P)).then_inc(S("mw_in"), 16)
            sp.wait_ge(S("down_done"), NE)
            overflow_guard(sp, 0)
            sp.wait_ge(S("y_out0"), 128)
            sp.wait_ge(S("y_out1"), 128)
            sp.wait_ge(S("comb"), NT)
            sp.dma_start(CS, a["rope_cs"]).then_inc(S("tab_in"), 16)
            sp.dma_start(A["tab"], a["rope_tab"]).then_inc(S("tab_in"), 16)
            sp.dma_start(c_ckv, a["cache_mla_ckv"][0, 0]).then_inc(S("tab_in"), 16)
            for j in range(2):
                sp.dma_start(c_kpe[:, j * 64:j * 64 + 64], a["cache_mla_kpe"][0, 0]).then_inc(S("tab_in"), 16)
            for c in range(2):
                sp.dma_start(g1[1][:, c, :].rearrange("p (m q) -> p m q", m=8), gate_row(1, 2, c)).then_inc(S("g1_in1"), 16)

            def head_w(h, b, dyn):
                sq = w_uq[:, :, bass.ds(h * 192, 192)] if dyn else w_uq[:, :, h * 192:h * 192 + 192]
                sk = w_uk[:, :, bass.ds(h * 128, 128)] if dyn else w_uk[:, :, h * 128:h * 128 + 128]
                sp.dma_start(wq[:, b, :, 0:192], sq).then_inc(S(f"wq_full{b}"), 16)
                sp.dma_start(wk[:, b], sk).then_inc(S(f"wq_full{b}"), 16)
            head_w(0, 0, False)
            head_w(1, 1, False)
            sp.dma_start(w_o, a["mla_w_o"][0].rearrange("(k p) n -> p k n", p=P)).then_inc(S("mw_o"), 16)
            with sp.Fori(0, 3) as i:
                for b in range(2):
                    sp.wait_ge(S("hp_done"), i * 8 + 4 * b + 4)
                    head_w(i * 2 + b + 2, b, True)
            sp.wait_ge(S("kr_ready"), NT)
            sp.dma_start(out[4][0, 0], ckvn[:, PT % 2, :]).then_inc(S("cache_out"), 16)
            sp.dma_start(out[5][0, 0], kr[:, PT % 2, 0:64]).then_inc(S("cache_out"), 16)
            moe_loads(1)
            sp.wait_ge(S("y_out0"), 256)
            sp.wait_ge(S("down_done"), 2 * NE)
            overflow_guard(sp, 1)
            sp.dma_start(fin_row, a["norm_final"].partition_broadcast(P)).then_inc(S("misc_in"), 16)
            for t in range(NT):
                sp.wait_ge(S("fin_ready"), t + 1)
                dst = out[0][0] if t == PT else out[1][0, t * P:(t + 1) * P, :]
                sp.dma_start(dst, fin[:, t % 2, :]).then_inc(S(f"fin_out{t % 2}"), 16)
            sp.wait_ge(S("fin_out0"), 48)
            sp.wait_ge(S("fin_out1"), 32)
            sp.wait_ge(S("cache_out"), 32)

        @block.gpsimd
        def _(pool):
            g = nc.gpsimd
            g.memset(ident[:], 0.0).then_inc(S("gset"), 1)
            g.memset(ones[:], 1.0).then_inc(S("gset"), 1)
            g.memset(before[:], 1.0).then_inc(S("gset"), 1)
            g.memset(half[:], -0.5).then_inc(S("gset"), 1)
            g.memset(epsc[:], EPS).then_inc(S("gset"), 1)
            pool.wait_ge(S("gset"), 5)
            g.affine_select(out=ident[:], in_=ident[:], compare_op=ALU.not_equal, fill=1.0, base=0,
                            pattern=[[-1, P]], channel_multiplier=1).then_inc(S("gset"), 1)
            g.affine_select(out=before[:], in_=before[:], compare_op=ALU.is_gt, fill=0.0, base=0,
                            pattern=[[1, P]], channel_multiplier=-1).then_inc(S("gset"), 1)
            for j, (st, base, cm) in enumerate(((1, 0, -1), (-1, 0, 1), (1, 1, 0), (-1, P, 0))):
                g.iota(dist[:, j, :], pattern=[[st, P]], base=base, channel_multiplier=cm,
                       allow_small_or_imprecise_dtypes=True).then_inc(S("gset"), 1)
            g.iota(pf[:, 0:1], pattern=[[1, 1]], base=P - 1, channel_multiplier=-1,
                   allow_small_or_imprecise_dtypes=True).then_inc(S("gset"), 1)
            g.iota(pf[:, 1:2], pattern=[[1, 1]], base=0, channel_multiplier=1,
                   allow_small_or_imprecise_dtypes=True).then_inc(S("gset"), 1)
            g.iota(idx16[:], pattern=[[1, NE]], base=0, channel_multiplier=0,
                   allow_small_or_imprecise_dtypes=True).then_inc(S("gset"), 1)
            g.iota(idx16p[:], pattern=[[1, NE]], base=100, channel_multiplier=0,
                   allow_small_or_imprecise_dtypes=True).then_inc(S("gset"), 1)
            g.iota(ebase[:], pattern=[[BLK, NE]], base=0, channel_multiplier=0,
                   allow_small_or_imprecise_dtypes=True).then_inc(S("gset"), 1)
            g.iota(tok_id[:], pattern=[[P, NT]], base=0, channel_multiplier=1).then_inc(S("gset"), 1)
            g.iota(tok_f[:], pattern=[[P, NT]], base=0, channel_multiplier=1,
                   allow_small_or_imprecise_dtypes=True).then_inc(S("gset"), 1)
            g.iota(row_no[:], pattern=[[1, P]], base=0, channel_multiplier=0,
                   allow_small_or_imprecise_dtypes=True).then_inc(S("gset"), 1)
            g.memset(zero_id[:], 0).then_inc(S("gset"), 1)
            pool.wait_ge(S("mask_exp"), 8)
            mf, mb = mask[:, 0:4, :], mask[:, 4:8, :]
            g.affine_select(out=mf, in_=mf, compare_op=ALU.is_ge, fill=0.0, base=0,
                            pattern=[[0, 4], [1, P]], channel_multiplier=-1).then_inc(S("mask_tri"), 1)
            g.affine_select(out=mb, in_=mb, compare_op=ALU.is_ge, fill=0.0, base=0,
                            pattern=[[0, 4], [-1, P]], channel_multiplier=1).then_inc(S("mask_tri"), 1)

            ch = Chain(pool, S("pool_step"))

            def rstd(n):
                for t in range(NT):
                    pool.wait_ge(S("sq"), n * NT + t + 1)
                    if n:
                        pool.wait_ge(S("used"), n * NT - NT + t + 1)
                    ch.link(g.tensor_scalar(rs[:, t:t + 1], ss[:, t:t + 1], 1.0 / D, EPS, ALU.mult, ALU.add))
                    g.tensor_tensor(rs[:, t:t + 1], rs[:, t:t + 1], half[:], ALU.pow).then_inc(S("rstd"), 1)

            rstd(0)

            def head(h, per):
                def qdec_mul(u):
                    t, r = STEPS[u]
                    pool.wait_ge(S("qdec_exp"), 8)
                    if u == 0:
                        pool.wait_ge(S("proj_evac"), use_base(h) + 4)
                    if u < 2:
                        pool.wait_ge(S("o_done"), h * 10)
                    else:
                        pool.wait_ge(S("o_done"), h * 10 + u - 1)
                    c = qdec[:, r * 4 + h, :] if isinstance(h, int) else qdec[:, bass.ds(h + r * 4, 1), :].rearrange("p a n -> p (a n)")
                    g.tensor_tensor(qd[:, u % 2], qT[:, :, tile_cols(t)], c.unsqueeze(1).to_broadcast([P, 2, P]),
                                    ALU.mult).then_inc(S("qd_ready"), 1)
                qdec_mul(0)
                qdec_mul(1)
                for i in range(10):
                    pool.wait_ge(S("stats"), h * 10 + i + 1)
                    ch.link(g.tensor_tensor(rv[:, i % 2:i % 2 + 1], mv[:, i % 2, 1:2], epsc[:], ALU.add))
                    g.tensor_tensor(rv[:, i % 2:i % 2 + 1], rv[:, i % 2:i % 2 + 1], half[:], ALU.pow)\
                        .then_inc(S("head_rstd"), 1)
                    if i + 2 < 8:
                        qdec_mul(i + 2)

            head(0, 10)
            mod_rows_out(pool, 0)
            for c in range(2):
                pool.dma_start(g1[0][:, c, :].rearrange("p (m q) -> p m q", m=8), gate_row(0, 2, c)).then_inc(S("g1_in0"), 16)
            with pool.Fori(1, RH) as h:
                ch.c.enter(h, 1, 10)
                head(h, 10)
            ch.c.leave(RH)

            def moe(l):
                n = 2 * l + 1
                rstd(n)
                pool.wait_ge(S("h2_first"), 16 * l + 16)
                pool.wait_ge(S(f"h2_out{l}"), 16 * NT - 16)
                pool.wait_ge(S("ids_ready"), l + 1)
                def gather(e):
                    b = e.par
                    if not (isinstance(e.n, int) and e.n < 2):
                        pool.wait_ge(S("tr_done"), l * NE + e.n - 1)
                    ch.link(g.tensor_copy(idc[:, b:b + 1], ids[:, e.n:e.n + 1] if isinstance(e.n, int)
                                          else ids[:, bass.ds(e.n, 1)]))
                    alone(pool)
                    g.indirect_dma_start(out=xg[:, b, :], out_offset=None, in_=h2d[l],
                                         in_offset=bass.IndirectOffsetOnAxis(ap=idc[:, b:b + 1], axis=0))\
                        .then_inc(S(f"gath{b}"), 16)
                gather(fixed(0, 2))
                gather(fixed(1, 2))
                with pool.Fori(0, NE // 2 - 1) as i:
                    ch.c.enter(i, 0, 2)
                    gather(Step(i, 2, 2))
                    gather(Step(i, 2, 3))
                ch.c.leave(NE // 2 - 1)
                overflow(pool, l)
                pool.wait_ge(S("y_out0"), l * 128 + 128)
                pool.wait_ge(S("y_out1"), l * 128 + 128)
                def pick(table):
                    for t, j in ((0, 0), (1, 0), (2, 0), (0, 1), (3, 0), (1, 1), (4, 0), (2, 1), (3, 1), (4, 1)):
                        if j:
                            pool.wait_ge(S(f"pick{t}"), 32 * l + 16)
                        g.indirect_dma_start(out=picked[t], out_offset=None, in_=table,
                                             in_offset=bass.IndirectOffsetOnAxis(ap=slots[:, j, t:t + 1], axis=0),
                                             **({"compute_op": ALU.add} if j else {})).then_inc(S(f"pick{t}"), 16)
                r = pool.value_load(cnt[0:1, 0:1], min_val=0, max_val=T)
                with pool.If(r > BLK):
                    pick(ybuf[l])
                with pool.Else():
                    pick(ybuf[l][0:NE * BLK, :])

            moe(0)
            rstd(2)
            for t in range(NT):
                pool.wait_ge(S("lat_sq"), 2 * t + 2)
                if t:
                    pool.wait_ge(S("lat_used"), t)
                ch.link(g.tensor_scalar(rv[:, 0:1], ss[:, 6:7], 1.0 / QR, EPS, ALU.mult, ALU.add))
                ch.link(g.tensor_scalar(rv[:, 1:2], ss[:, 7:8], 1.0 / KVR, EPS, ALU.mult, ALU.add))
                g.tensor_tensor(rv[:, 0:1], rv[:, 0:1], half[:], ALU.pow).then_inc(S("lat_rstd"), 1)
                g.tensor_tensor(rv[:, 1:2], rv[:, 1:2], half[:], ALU.pow).then_inc(S("lat_rstd"), 1)

            with pool.Fori(0, MH // 2) as i:
                for b in range(2):
                    pool.wait_ge(S(f"wq_full{b}"), i * 32 + 32)
                    alone(pool)
                    w5 = wq[:, b].rearrange("p k (q n) -> p k q n", q=16)
                    for o, s in ((12, 9), (13, 8), (14, 11), (15, 10)):
                        g.tensor_copy(w5[:, :, o, :], w5[:, :, s, :]).then_inc(S("wq_swap"), 1)
            moe(1)
            rstd(4)


        @block.tensor
        def _(pe):
            mmul, tpose = nc.tensor.matmul, nc.tensor.transpose
            full = [Count(16) for _ in range(5)]

            pe.wait_ge(S("vec_in"), 96)
            pe.wait_ge(S("gset"), 19)
            tpose(bank[7][:, 0:P], vraw[:], ident[:])
            tpose(bank[7][:, P:P + 20], vraw2[:], ident[0:20, 0:20]).then_inc(S("vec_T"), 1)

            def bank_free(base, j):
                if not (isinstance(base, int) and base + j < 3):
                    pe.wait_ge(S("proj_evac"), base + j - 2)

            def chunk(base, j, s):
                bank_free(base, j)
                pe.wait_ge(S(f"ring_full{s}"), full[s].next())
                for i in range(2):
                    for g in range(4):
                        k = 2 * g + i
                        mm = mmul(bank[j % 4][32 * g:32 * g + 32, :], cond[:, 2 * k:2 * k + 32], ring8(s)[:, k, :],
                                  start=(i == 0), stop=(i == 1), tile_position=(0, 32 * g))
                mm.then_inc(S("proj_done"), 1)

            def chunk_sum(base, part, j):
                bank_free(base, j)
                pe.wait_ge(S("proj_evac"), base + part + 1)
                for m in range(4):
                    mm = mmul(bank[j % 4][:, 2 * m:2 * m + 2], stage[:, tile_cols(m)], pick2[:], start=True, stop=True)
                mm.then_inc(S("proj_done"), 1)

            def norm_T(n, src, tiles=range(NT)):
                reuse = 4 if n == 0 else 1
                for t in tiles:
                    pe.wait_ge(S("used"), n * NT + t + 1)
                    if t >= reuse:
                        pe.wait_ge(S("hTa"), n * NT + t - reuse + 1)
                        pe.wait_ge(S("hTd"), n * NT + t - reuse + 1)
                    for k in range(KT):
                        mm = tpose(banks(T_BANK[n][t], 2)[:, tile_cols(k)], src[:, t % 2, tile_cols(k)], ident[:])
                    mm.then_inc(S("tr"), 1)

            def h2_T(l, t):
                n = 2 * l + 1
                pe.wait_ge(S("h2_ready"), l * NT + t + 1)
                if t:
                    pe.wait_ge(S("hTa"), n * NT + t)
                    pe.wait_ge(S("hTd"), n * NT + t)
                for k in range(KT):
                    mm = tpose(banks(0, 2)[:, tile_cols(k)], h2b[:, t % 4, tile_cols(k)], ident[:])
                mm.then_inc(S("tr"), 1)

            def router(l, t):
                n = 2 * l + 1
                pe.wait_ge(S("hTa"), n * NT + t + 1)
                pe.wait_ge(S("hTd"), n * NT + t + 1)
                for k in range(KT):
                    mm = mmul(bank[R_BANK[l]][:, t * NE:(t + 1) * NE], h2T[:, t % 2, k, :], w_rt[:, k, :],
                              start=(k == 0), stop=(k == KT - 1))
                mm.then_inc(S("router_mm"), 1)

            pe.wait_ge(S("cond_set"), 1)
            pe.wait_ge(S("pick2_set"), 2)
            for j, (kind, c) in enumerate(PRE_ORDER):
                if kind == "part":
                    chunk(0, j, PRE_SLOTS[c])
                else:
                    chunk_sum(0, PRE_ORDER.index(("part", c)), j)
            pe.wait_ge(S("proj_evac"), PRE)
            pe.wait_ge(S("vt_set"), 2)
            norm_T(0, xn[0])
            pe.wait_ge(S("hTa"), NT)
            pe.wait_ge(S("hTd"), NT)

            def out_proj(h):
                def y_T(t):
                    if t == 0:
                        pe.wait_ge(S("ln_done"), h * 10)
                        pe.wait_ge(S("kd_ready"), h * NSS)
                        pe.wait_ge(S("rows_sb"), 1)
                    elif t == 1:
                        pe.wait_ge(S("o_free"), h * 10)
                    else:
                        pe.wait_ge(S("yt_evac"), h * NT - NT + t - 1)
                    for j in range(4):
                        mm = tpose(bank[4 + t % 2][:, tile_cols(j)], yy[:, t, tile_cols(j)], ident[:])
                    mm.then_inc(S("yt_done"), 1)
                y_T(0)
                for t in range(NT):
                    if t + 1 < NT:
                        y_T(t + 1)
                    pe.wait_ge(S("yt_evac"), h * NT - NT + t + 1)
                    if t == 0:
                        pe.wait_ge(S("ring_full4"), full[4].next())
                        pe.wait_ge(S("S_upd"), h * NSS)
                    for hf in range(2):
                        if t:
                            pe.wait_ge(S("op_evac"), h * 10 - 10 + 2 * t + hf - 1)
                        for j in range(4):
                            mm = mmul(bank[6 + hf][:], yT[:, t % 2, j, :],
                                      ring(4)[:, j * D + hf * 512:j * D + hf * 512 + 512],
                                      start=(j == 0), stop=(j == 3))
                        mm.then_inc(S("op_done"), 1)
                    if isinstance(h, int):
                        if t == 1:
                            pe.wait_ge(S("proj_evac"), use_base(RH))
                            pe.wait_ge(S("misc_in"), 48)
                        if t:
                            h2_T(0, t - 1)
                        if t >= 2:
                            router(0, t - 2)

            def head(h):
                first = isinstance(h, int)
                gate, chunk_use, sum_use, _ = use_plan(CHUNKS_FIRST if first else CHUNKS_LOOP)
                chunks = CHUNKS_FIRST if first else CHUNKS_LOOP
                slots_of = SLOTS_FIRST if first else SLOTS_LOOP
                b = use_base(h)
                pe.wait_ge(S("ring_full0"), full[0].next(2))
                for j in range(4):
                    for s, cols in enumerate((slice(0, TS), slice(TS, T))):
                        bank_free(b, 2 * j + s)
                        w = cols.stop - cols.start
                        for k in range(KT):
                            mm = mmul(bank[(2 * j + s) % 4][:, 0:w], ring8(0)[:, k, tile_cols(j)], hT[:, k, cols],
                                      start=(k == 0), stop=(k == KT - 1))
                        mm.then_inc(S("proj_done"), 1)
                if not first:
                    out_proj(h)
                pe.wait_ge(S("ring_full1"), full[1].next())
                for t in range(NT):
                    bank_free(b, 8 + t)
                    for k in range(KT):
                        mm = mmul(bank[(8 + t) % 4][:], hT[:, k, tile_cols(t)], ring8(1)[:, k, :],
                                  start=(k == 0), stop=(k == KT - 1))
                    mm.then_inc(S("proj_done"), 1)
                pe.wait_ge(S("proj_evac"), b + 8)
                if not first:
                    pe.wait_ge(S("yt_evac"), h * NT)
                for t in range(NT):
                    dst = bank[4][:, tile_cols(t)] if t < 4 else bank[5][:, 0:P]
                    for j in range(2):
                        mm = mmul(dst, kT[:, j, tile_cols(t)], qT[:, j, tile_cols(t)], start=(j == 0), stop=(j == 1))
                    if t >= 3:
                        mm.then_inc(S("att_done"), 1)
                pe.wait_ge(S("attm"), h * 4 + 4)

                def k_T(u):
                    if u:
                        pe.wait_ge(S("kd_ready"), h * NSS + u)
                    for j in range(2):
                        mm = tpose(bank[4][:, tile_cols(j)], kT[:, j, tile_cols(STEPS[STATE_STEPS[u]][0])], ident[:])
                    mm.then_inc(S("kt_done"), 1)

                k_T(0)
                pe.wait_ge(S("proj_evac"), b + 13)
                if not first:
                    pe.wait_ge(S("op_evac"), h * 10)
                for i, (t, r) in enumerate(STEPS):
                    latent = t != PT
                    if i:
                        pe.wait_ge(S("o_free"), h * 10 + i)
                    mm = mmul(bank[5][:], attm[:, r, t, :], vv[:, t, :], start=True, stop=not latent)
                    if latent:
                        pe.wait_ge(S("qd_ready"), h * 8 + i + 1)
                        before_i = [u for u, s in enumerate(STATE_STEPS) if s < i and STEPS[s][1] == r]
                        if before_i:
                            pe.wait_ge(S("S_upd"), h * NSS + before_i[-1] + 1)
                        else:
                            pe.wait_ge(S("S_in"), h * 32 + 32)
                        for j in range(2):
                            mm = mmul(bank[5][:], qd[:, i % 2, j, :], St[:, r, j, :], start=False, stop=(j == 1))
                    mm.then_inc(S("o_done"), 1)
                    if i in STATE_STEPS:
                        u = STATE_STEPS.index(i)
                        pe.wait_ge(S("kd_ready"), h * NSS + u + 1)
                        if u:
                            pe.wait_ge(S("S_upd"), h * NSS + u)
                        for j in range(2):
                            mm = mmul(bank[6 + j][:], kd[:, u % 2, tile_cols(j)], vv[:, t, :], start=True, stop=True)
                        mm.then_inc(S("S_done"), 1)
                        if u + 1 < NSS:
                            k_T(u + 1)
                    bank_free(b, gate[i])
                    if i < 2:
                        pe.wait_ge(S(f"ring_full{2 + r}"), full[2 + r].next())
                    for k in range(KT):
                        mm = mmul(bank[gate[i] % 4][:], hT[:, k, tile_cols(t)], ring8(2 + r)[:, k, :],
                                  start=(k == 0), stop=(k == KT - 1))
                    mm.then_inc(S("proj_done"), 1)
                    if i - 1 in chunks:
                        c = chunks[i - 1]
                        chunk_sum(b, chunk_use[c], sum_use[c])
                    if i in chunks:
                        c = chunks[i]
                        chunk(b, chunk_use[c], slots_of[c])

            def rows_T(l):
                pe.wait_ge(S("modB"), l + 1)
                tpose(bank[4][0:96, 0:P], mod[:, l].rearrange("p m c -> p (m c)"), ident[:]).then_inc(S("rows_T"), 1)

            head(0)
            pe.wait_ge(S("kd_ready"), NSS)
            rows_T(0)
            per = (3, 2, 1, 1, 3)
            with pe.Fori(1, RH) as h:
                for f, n in zip(full, per):
                    f.enter(h, 1, n)
                head(h)
            for f in full:
                f.leave(RH)
            out_proj(RH)
            pe.wait_ge(S("yt_evac"), NT * RH)
            rows_T(1)

            def moe(l):
                router(l, NT - 2)
                h2_T(l, NT - 1)
                router(l, NT - 1)
                pe.wait_ge(S("sel"), l + 1)
                msk = rt[3]
                flat = msk.rearrange("p t e -> p (t e)")
                mmul(bank[5][:, 0:NT * NE], before[:], flat, start=True, stop=False)
                for j in range(NT - 1):
                    mmul(bank[5][:, (j + 1) * NE:NT * NE], ones[:],
                         msk[:, j:j + 1, :].to_broadcast([P, NT - 1 - j, NE]), start=False, stop=(j == NT - 2))
                mmul(bank[5][:, NT * NE:2 * NT * NE], ones[:], flat, start=True, stop=True).then_inc(S("rank_done"), 1)
                pe.wait_ge(S("onehot"), l + 1)
                for q in range(2 * NT):
                    mm = mmul(bank[6][:, 0:32], onehot[:, q, :], sent[:, q].rearrange("p o e -> p (o e)"),
                              start=(q == 0), stop=(q == 2 * NT - 1))
                mm.then_inc(S("ids_mm"), 1)

                def gathered_T(e):
                    pe.wait_ge(S(f"gath{e.par}"), l * 128 + e.half * 16 + 16)
                    pe.wait_ge(S("xa"), l * NE + e.n)
                    pe.wait_ge(S("xd"), l * NE + e.n)
                    for k in range(KT):
                        mm = tpose(banks(0, 2)[:, tile_cols(k)], xg[:, e.par, tile_cols(k)], ident[:])
                    mm.then_inc(S("tr_done"), 1)

                def gate_up(e):
                    pe.wait_ge(S(f"w_full{e.buf}"), l * 192 + e.quarter * 48 + 48)
                    pe.wait_ge(S("xa"), l * NE + e.n + 1)
                    pe.wait_ge(S("xd"), l * NE + e.n + 1)
                    pe.wait_ge(S("act"), l * NE + e.n)
                    for k in range(KT):
                        mm = mmul(bank[2][:], xgT[:, e.par, k, :], expert_w(e.buf)[0][:, k].rearrange("p g f -> p (g f)"),
                                  start=(k == 0), stop=(k == KT - 1))
                    mm.then_inc(S("gu_done"), 1)

                def act_T(e):
                    pe.wait_ge(S("act"), l * NE + e.n + 1)
                    pe.wait_ge(S("actT"), l * NE + e.n)
                    for j in range(2):
                        mm = tpose(bank[3][:, tile_cols(j)], gact[:, e.par, tile_cols(j)], ident[:])
                    mm.then_inc(S("at_done"), 1)

                def down(e):
                    pe.wait_ge(S("actT"), l * NE + e.n + 1)
                    if not (isinstance(e.n, int) and e.n < 2):
                        pe.wait_ge(S("ya"), l * NE + e.n - 1)
                        pe.wait_ge(S("yd"), l * NE + e.n - 1)
                    for hf in range(2):
                        for j in range(2):
                            mm = mmul(bank[4 + 2 * e.par + hf][:], gactT[:, e.par, j, :],
                                      expert_w(e.buf)[1][:, j, hf * 512:hf * 512 + 512], start=(j == 0), stop=(j == 1))
                    mm.then_inc(S("down_done"), 1)

                gathered_T(fixed(0, 4))
                pe_step(pe, gate_up, gathered_T, down, act_T)
                down(fixed(NE - 1, 4))
                overflow(pe, l)

            def pe_step(eng, gate_up, gathered_T, down, act_T):
                def one(e):
                    static = isinstance(e.n, int)
                    gate_up(e)
                    if not (static and e.n == NE - 1):
                        gathered_T(e.plus(1))
                    if not (static and e.n == 0):
                        down(e.plus(-1))
                    act_T(e)
                for u in range(3):
                    one(fixed(u, 4))
                with eng.Fori(0, 3) as i:
                    for u in range(3, 7):
                        one(Step(i, 4, u))
                one(fixed(NE - 1, 4))

            moe(0)

            def lat_T(t):
                if t < NT:
                    pe.wait_ge(S("kr_ready"), t + 1)
                else:
                    pe.wait_ge(S("tab_in"), 80)
                if t:
                    pe.wait_ge(S("lat_Ta"), t)
                    pe.wait_ge(S("lat_Td"), t)
                b0 = 2
                if t < NT:
                    for j in range(4):
                        tpose(bank[b0][:, tile_cols(j)], cqn[:, t % 2, tile_cols(j)], ident[:])
                ck, kp = (ckvn[:, t % 2, :], kr[:, t % 2, :]) if t < NT else (c_ckv, c_kpe)
                for j in range(2):
                    tpose(bank[b0 + 1][:, tile_cols(j)], ck[:, tile_cols(j)], ident[:])
                tpose(bank[b0 + 1][:, tile_cols(2)], kp, ident[:]).then_inc(S("lat_tr"), 1)

            def latent(t):
                pe.wait_ge(S("hTa"), 2 * NT + t + 1)
                pe.wait_ge(S("hTd"), 2 * NT + t + 1)
                if t == 0:
                    pe.wait_ge(S("mw_in"), 32)
                if t >= 2:
                    pe.wait_ge(S("lat_used"), t - 1)
                b0 = 4 + 2 * (t % 2)
                for k in range(KT):
                    mmul(bank[b0][:], hT[:, k, tile_cols(t)], w_in[:, k, 0:512], start=(k == 0), stop=(k == KT - 1))
                for k in range(KT):
                    mm = mmul(bank[b0 + 1][:, 0:320], hT[:, k, tile_cols(t)], w_in[:, k, 512:832],
                              start=(k == 0), stop=(k == KT - 1))
                mm.then_inc(S("lat_done"), 1)

            norm_T(2, xn[1], (0, 1))
            for t in range(NT):
                latent(t)
                if t:
                    lat_T(t - 1)
                if t + 2 < NT:
                    norm_T(2, xn[1], (t + 2,))
            lat_T(NT - 1)
            lat_T(NT)
            pe.wait_ge(S("lat_Ta"), NT)
            pe.wait_ge(S("lat_Td"), NT + 1)
            for kt in range(6):
                for hf in range(2):
                    if kt >= 2:
                        pe.wait_ge(S("va" if hf == 0 else "vd"), kt - 1)
                    for j in range(2):
                        mm = mmul(bank[4 + (2 * kt + hf) % 4][:], ckT[:, j, tile_cols(kt)],
                                  w_uv[:, j, hf * 512:hf * 512 + 512], start=(j == 0), stop=(j == 1))
                    mm.then_inc(S("v_done"), 1)
            pe.wait_ge(S("va"), 6)
            pe.wait_ge(S("vd"), 6)

            def head_proj(h):
                p = h.par
                pe.wait_ge(S(f"wq_full{p}"), h.half * 32 + 32)
                pe.wait_ge(S("wq_swap"), h.n * 4 + 4)
                notfirst = not (isinstance(h.n, int) and h.n == 0)

                def run(dst, lhs, rhs, nk, inc):
                    for k in range(nk):
                        mm = mmul(dst, lhs(k), rhs(k), start=(k == 0), stop=(k == nk - 1))
                    if inc:
                        mm.then_inc(S("hp_done"), 1)
                qn = lambda k: wq[:, p, k, 0:NOPE]
                qp = lambda k: wq[:, p, k, NOPE:NOPE + 128]
                kn = lambda k: wk[:, p, k, :]
                if notfirst:
                    pe.wait_ge(S("ex_done"), h.n * 5 - 2)
                run(bank[1][:], qn, lambda k: cqT[:, k, 0:TS], 4, True)
                if notfirst:
                    pe.wait_ge(S("ex_done"), h.n * 5 - 1)
                run(bank[2][:], qp, lambda k: cqT[:, k, 0:TS], 4, True)
                run(bank[3][:], kn, lambda k: ckT[:, k, 0:512], 2, True)
                if notfirst:
                    pe.wait_ge(S("hp_d"), h.n * 2)
                run(bank[7][:, 0:128], qn, lambda k: cqT[:, k, TS:T], 4, False)
                run(bank[7][:, 128:256], qp, lambda k: cqT[:, k, TS:T], 4, False)
                run(bank[7][:, 256:512], kn, lambda k: ckT[:, k, 512:768], 2, True)

            def score(h, t):
                if t == 0:
                    pe.wait_ge(S("hp_a"), h.n * 2 + 2)
                    pe.wait_ge(S("hp_d"), h.n * 2 + 2)
                    pe.wait_ge(S("ex_done"), h.n * 5)
                elif t >= 2:
                    pe.wait_ge(S("ex_done"), h.n * 5 + t - 1)
                b0 = 2 * (t % 2)
                parts = ((b0, 128, slice(640, 768)),) if t == PT else ((b0, 512, slice(0, 512)), (b0 + 1, 128, slice(512, 640)))
                for b, w, cols in parts:
                    mmul(bank[b][:, 0:w], qnT[:, h.par, tile_cols(t)], knT[:, h.par, cols], start=True, stop=False)
                    mm = mmul(bank[b][:, 0:w], qpT[:, h.par, tile_cols(t)], kpT[:, cols], start=False, stop=True)
                mm.then_inc(S("sc_done"), 1)

            def prob_T(h, t):
                gp = (h.par + t) % 2
                pe.wait_ge(S("ex_done"), h.n * 5 + t + 1)
                pe.wait_ge(S("pt_a"), h.n * 5 + t)
                for k in range(1 if t == PT else 5):
                    mm = tpose(banks(4, 2)[:, tile_cols(k)], pr[:, gp, tile_cols(k)], ident[:])
                mm.then_inc(S("pt_done"), 1)

            def prob_v(h, t):
                gp = (h.par + t) % 2
                pe.wait_ge(S("pt_a"), h.n * 5 + t + 1)
                pe.wait_ge(S("o_ev"), h.n * 5 + t)
                keys = [5] if t == PT else range(5)
                for i, kt in enumerate(keys):
                    rhs = V[:, kt, h.n * VD:h.n * VD + VD] if isinstance(h.n, int) else V[:, kt, bass.ds(h.n * VD, VD)]
                    mm = mmul(bank[6][:, 0:VD], prT[:, gp, i, :], rhs, start=(i == 0), stop=(i == len(keys) - 1))
                mm.then_inc(S("pv_done"), 1)

            def main(h):
                score(h, 0)
                score(h, 1)
                prob_T(h, 0)
                score(h, 2)
                prob_T(h, 1)
                prob_v(h, 0)
                score(h, 3)
                prob_T(h, 2)
                prob_v(h, 1)
                score(h, 4)
                prob_T(h, 3)
                prob_v(h, 2)

            def tail(h):
                prob_T(h, 4)
                prob_v(h, 3)
                prob_v(h, 4)

            head_proj(fixed(0, 2))
            main(fixed(0, 2))
            with pe.Fori(0, 3) as i:
                for u in (1, 2):
                    h = Step(i, 2, u)
                    head_proj(h)
                    tail(h.plus(-1))
                    main(h)
            head_proj(fixed(MH - 1, 2))
            tail(fixed(MH - 2, 2))
            main(fixed(MH - 1, 2))
            tail(fixed(MH - 1, 2))

            pe.wait_ge(S("mw_o"), 16)
            pe.wait_ge(S("o_ev"), 5 * MH)

            def o_T(t):
                if t:
                    pe.wait_ge(S("oTa"), t)
                    pe.wait_ge(S("oTd"), t)
                for k in range(KT):
                    mm = tpose(banks(2, 2)[:, tile_cols(k)], o_all[:, t, tile_cols(k)], ident[:])
                mm.then_inc(S("o_tr"), 1)
            o_T(0)
            for t in range(NT):
                if t + 1 < NT:
                    o_T(t + 1)
                pe.wait_ge(S("oTa"), t + 1)
                pe.wait_ge(S("oTd"), t + 1)
                for hf in range(2):
                    if t:
                        pe.wait_ge(S("mo_evac"), 2 * t + hf - 1)
                    for k in range(KT):
                        mm = mmul(bank[4 + hf][:], oTb[:, t % 2, k, :], w_o[:, k, hf * 512:hf * 512 + 512],
                                  start=(k == 0), stop=(k == KT - 1))
                    mm.then_inc(S("mo_done"), 1)
                if t:
                    h2_T(1, t - 1)
                if t >= 2:
                    router(1, t - 2)
            moe(1)

        @block.scalar
        def _(act):
            A_ = nc.scalar.activation
            ch = Chain(act, S("act_step"))
            act.wait_ge(S("lg_in"), 16)
            ch.link(A_(lg[:], lg[:], ACT.Exp))
            ch.link(A_(lg[:], lg[:], ACT.Copy, scale=-1.0))
            act.wait_ge(S("gset"), 19)
            A_(cdec[:], lg[:], ACT.Exp, scale=float(P)).then_inc(S("decay_set"), 1)
            for r in range(2):
                ch.link(A_(lgk[:, 4 * r:4 * r + 4], lg[:, 4 * r:4 * r + 4], ACT.Copy, scale=pf[:, r:r + 1]))
            A_(kdec[:], lgk[:], ACT.Exp).then_inc(S("decay_set"), 1)
            for r in range(2):
                ch.link(A_(dist[:, r, :], dist[:, r, :], ACT.Relu))
            for c in range(8):
                A_(mask[:, c, :], dist[:, c // 4, :], ACT.Exp, scale=lg[:, c:c + 1]).then_inc(S("mask_exp"), 1)
            for c in range(8):
                A_(qdec[:, c, :], dist[:, 2 + c // 4, :], ACT.Exp, scale=lg[:, c:c + 1]).then_inc(S("qdec_exp"), 1)
            act.wait_ge(S("vec_T"), 1)
            A_(cond[:, 0:16].rearrange("p (k c) -> p c k", c=2), bank[7][:, 112:128].rearrange("p (c k) -> p c k", c=2), ACT.Silu)\
                .then_inc(S("cond_set"), 1)
            A_(vt1[:], bank[7][:, 0:P], ACT.Copy).then_inc(S("vt_set"), 1)
            A_(vt2[:], bank[7][:, P:P + 20], ACT.Copy).then_inc(S("vt_set"), 1)

            def square(n, t):
                if n == 0:
                    act.wait_ge(S(f"x_in{(t + 1) // 2}"), 32 if t else 16)
                elif n == 1:
                    act.wait_ge(S("x_add"), 10 * RH - 10 + 2 * t + 2)
                elif n == 3:
                    act.wait_ge(S("mx_add"), 2 * t + 2)
                else:
                    act.wait_ge(S("comb"), (n // 2 - 1) * NT + t + 1)
                if t:
                    act.wait_ge(S("sq"), n * NT + t)
                A_(junk[n], x[:, t, :], ACT.Square, accum_out=ss[:, t:t + 1]).then_inc(S("sq"), 1)

            def chunk_stage(n, b):
                act.wait_ge(S("proj_done"), n + 1)
                A_(stage[:], bank[b], ACT.Copy).then_inc(S("proj_evac"), 1)

            def chunk_evac(l, c, n, b):
                act.wait_ge(S("proj_done"), n + 1)
                dst = mod[:, l, 4 * c:4 * c + 4, :] if isinstance(c, int) else mod[:, l, bass.ds(c * 4, 4), :]
                A_(dst, bank[b][:, 0:8].rearrange("p (m c) -> p m c", c=2), ACT.Copy).then_inc(S("proj_evac"), 1)

            for j, (kind, c) in enumerate(PRE_ORDER):
                if kind == "part":
                    chunk_stage(j, j % 4)
                else:
                    chunk_evac(0, c, j, j % 4)

            def norm_evac(n, l, t):
                c = 1 if t == PT else 0
                act.wait_ge(S("tr"), n * NT + t + 1)
                if t == 0:
                    act.wait_ge(S("modA"), l + 1)
                src = bank[T_BANK[n][t]]
                for k in range(4):
                    ins = A_(hT[:, k, tile_cols(t)], src[:, tile_cols(k)], ACT.Identity,
                             scale=a1[:, l, k, c:c + 1], bias=mod[:, l, k, c:c + 1])
                ins.then_inc(S("hTa"), 1)

            def h2_evac(l, t):
                act.wait_ge(S("tr"), (2 * l + 1) * NT + t + 1)
                if t >= 2:
                    act.wait_ge(S("router_mm"), l * NT + t - 1)
                A_(h2T[:, t % 2, 0:4, :].rearrange("p k n -> p (k n)"), bank[0], ACT.Copy).then_inc(S("hTa"), 1)

            for i in range(NT + 2):
                if i < NT:
                    square(0, i)
                if i >= 2:
                    norm_evac(0, 0, i - 2)

            def y_evac(h, t):
                act.wait_ge(S("yt_done"), h * NT - NT + t + 1)
                if t >= 2:
                    act.wait_ge(S("op_done"), h * 10 - 10 + 2 * t - 2)
                A_(yT[:, t % 2].rearrange("p j n -> p (j n)"), bank[4 + t % 2], ACT.Copy).then_inc(S("yt_evac"), 1)

            def head(h):
                first = isinstance(h, int)
                chunks = CHUNKS_FIRST if first else CHUNKS_LOOP
                gate, chunk_use, sum_use, _ = use_plan(chunks)
                b = use_base(h)
                if first:
                    act.wait_ge(S("mask_exp"), 8)
                    act.wait_ge(S("qdec_exp"), 8)
                else:
                    act.wait_ge(S("S_saved"), h * 32)
                    act.wait_ge(S("ln_done"), h * 10)
                for r in range(2):
                    act.dma_start(St[:, r], s_in[r][h]).then_inc(S("S_in"), 16)
                gsrc = gn_in[:, h * DV:h * DV + DV] if first else gn_in[:, bass.ds(h * DV, DV)]
                act.dma_start(gn, gsrc.partition_broadcast(P)).then_inc(S("gn_in"), 16)
                for j in range(4):
                    for s, cols in enumerate((slice(0, TS), slice(TS, T))):
                        act.wait_ge(S("proj_done"), b + 2 * j + s + 1)
                        dst = (qT if j < 2 else kT)[:, j % 2, cols]
                        A_(dst, bank[(2 * j + s) % 4][:, 0:cols.stop - cols.start], ACT.Copy,
                           scale=1.0 if j < 2 else DK ** -0.5).then_inc(S("proj_evac"), 1)
                if not first:
                    for t in range(NT):
                        y_evac(h, t)
                for t in range(NT):
                    act.wait_ge(S("proj_done"), b + 8 + t + 1)
                    A_(vv[:, t, :], bank[(8 + t) % 4], ACT.Copy).then_inc(S("proj_evac"), 1)
                for i in range(10):
                    act.wait_ge(S("proj_done"), b + gate[i] + 1)
                    if not (first and i < 2):
                        act.wait_ge(S("ln_done"), h * 10 + i - 1)
                    A_(sg[:, i % 2, :], bank[gate[i] % 4], ACT.Silu).then_inc(S("proj_evac"), 1)
                    if i - 1 in chunks:
                        c = chunks[i - 1]
                        chunk_evac(0 if first else 1, PRE_CHUNKS + c if first else h * 4 + (c - 4), b + sum_use[c], sum_use[c] % 4)
                    if i in chunks:
                        n = chunk_use[chunks[i]]
                        chunk_stage(b + n, n % 4)
                act.wait_ge(S("S_upd"), h * NSS + NSS)
                for r in range(2):
                    act.dma_start(s_out[r][h], St[:, r]).then_inc(S("S_saved"), 16)

            def rows_evac(l):
                act.wait_ge(S("rows_T"), l + 1)
                if l:
                    act.wait_ge(S("rows_out0"), 16)
                A_(mod_rows[:], bank[4][0:96, 0:P], ACT.Copy).then_inc(S("rows_sb"), 1)

            head(0)
            rows_evac(0)
            with act.Fori(1, RH) as h:
                head(h)
            act.wait_ge(S("S_saved"), 32 * RH)
            y_evac(RH, 0)
            y_evac(RH, 1)
            for t in range(NT):
                square(1, t)
                if t:
                    h2_evac(0, t - 1)
                if t + 2 < NT:
                    y_evac(RH, t + 2)
            rows_evac(1)

            def moe(l):
                h2_evac(l, NT - 1)
                act.wait_ge(S("router_mm"), l * NT + NT)
                A_(rt[0].rearrange("p t e -> p (t e)"), bank[R_BANK[l]][:, 0:NT * NE], ACT.Sigmoid).then_inc(S("sig_s"), 1)

                def x_evac(e):
                    act.wait_ge(S("tr_done"), l * NE + e.n + 1)
                    if not (isinstance(e.n, int) and e.n < 2):
                        act.wait_ge(S("gu_done"), l * NE + e.n - 1)
                    A_(xgT[:, e.par, 0:4, :].rearrange("p k n -> p (k n)"), bank[0], ACT.Copy).then_inc(S("xa"), 1)

                def silu(e):
                    act.wait_ge(S("gu_done"), l * NE + e.n + 1)
                    A_(gact[:, e.par, :], bank[2][:, 0:FF], ACT.Silu).then_inc(S("silu"), 1)

                def actT_evac(e):
                    act.wait_ge(S("at_done"), l * NE + e.n + 1)
                    A_(gactT[:, e.par].rearrange("p j n -> p (j n)"), bank[3][:, 0:FF], ACT.Copy).then_inc(S("actT"), 1)

                def y_store(e):
                    act.wait_ge(S("down_done"), l * NE + e.n + 1)
                    if not (isinstance(e.n, int) and e.n < 2):
                        act.wait_ge(S(f"y_out{e.par}"), l * 128 + e.half * 16)
                    A_(ysb[:, e.par, 0:512], bank[4 + 2 * e.par], ACT.Copy).then_inc(S("ya"), 1)
                    act.wait_ge(S("ya"), l * NE + e.n + 1)
                    act.wait_ge(S("yd"), l * NE + e.n + 1)
                    dst = ybuf[l][e.n * BLK:e.n * BLK + BLK, :] if isinstance(e.n, int) else ybuf[l][bass.ds(e.n * BLK, BLK), :]
                    act.dma_start(dst, ysb[:, e.par, :]).then_inc(S(f"y_out{e.par}"), 16)

                def one(e):
                    static = isinstance(e.n, int)
                    silu(e)
                    if not (static and e.n == NE - 1):
                        x_evac(e.plus(1))
                    if not (static and e.n == 0):
                        y_store(e.plus(-1))
                    actT_evac(e)

                x_evac(fixed(0, 4))
                for u in range(3):
                    one(fixed(u, 4))
                with act.Fori(0, 3) as i:
                    for u in range(3, 7):
                        one(Step(i, 4, u))
                one(fixed(NE - 1, 4))
                y_store(fixed(NE - 1, 4))
                overflow(act, l)

            moe(0)

            def normalise(t):
                act.wait_ge(S("rstd"), 2 * NT + t + 1)
                if t >= 2:
                    act.wait_ge(S("tr"), 2 * NT + t - 1)
                A_(xn[1][:, t % 2, :], x[:, t, :], ACT.Copy, scale=rs[:, t:t + 1]).then_inc(S("used"), 1)

            def lat_evac(t):
                act.wait_ge(S("lat_tr"), t + 1)
                for j in range(4):
                    ins = A_(cqT[:, j, tile_cols(t)], bank[2][:, tile_cols(j)], ACT.Copy, scale=vt2[:, 16 + j:17 + j])
                ins.then_inc(S("lat_Ta"), 1)

            def lat_squares(t):
                b0 = 4 + 2 * (t % 2)
                act.wait_ge(S("lat_done"), t + 1)
                if t:
                    act.wait_ge(S("lat_rstd"), 2 * t)
                    act.wait_ge(S("lat_sq"), 2 * t)
                A_(lat_junk[:, 0:512], bank[b0], ACT.Square, accum_out=ss[:, 6:7]).then_inc(S("lat_sq"), 1)
                A_(lat_junk[:, 512:768], bank[b0 + 1][:, 0:256], ACT.Square, accum_out=ss[:, 7:8]).then_inc(S("lat_sq"), 1)

            square(2, 0)
            for i in range(1, NT):
                square(2, i)
                normalise(i - 1)
                if 2 <= i < 4:
                    norm_evac(2, 1, i - 2)
            for t in range(NT):
                lat_squares(t)
                if t:
                    lat_evac(t - 1)
                if t + 2 < NT:
                    norm_evac(2, 1, t + 2)
                if t == 0:
                    normalise(NT - 1)
            lat_evac(NT - 1)
            for kt in range(6):
                act.wait_ge(S("v_done"), 2 * kt + 1)
                A_(V[:, kt, 0:512], bank[4 + (2 * kt) % 4], ACT.Copy).then_inc(S("va"), 1)
            SCALE = (NOPE + ROPE) ** -0.5

            def head_evac(h):
                act.wait_ge(S("hp_done"), h.n * 4 + 1)
                A_(qnT[:, h.par, 0:TS], bank[1], ACT.Copy).then_inc(S("hp_a"), 1)
                act.wait_ge(S("hp_done"), h.n * 4 + 3)
                A_(knT[:, h.par, 0:512], bank[3], ACT.Copy).then_inc(S("hp_a"), 1)

            def expo(h, t):
                g, gp = h.n * 5 + t, (h.par + t) % 2
                w = P if t == PT else 640
                act.wait_ge(S("mx"), g + 1)
                if not (isinstance(g, int) and g < 2):
                    act.wait_ge(S("pt_done"), g - 1)
                A_(pr[:, gp, 0:w], banks(2 * (t % 2), 2)[:, 0:w], ACT.Exp, bias=nmx[:, gp:gp + 1], scale=SCALE,
                   accum_out=sm_sum[:, t:t + 1]).then_inc(S("ex_done"), 1)

            def probT_evac(h, t):
                g, gp = h.n * 5 + t, (h.par + t) % 2
                act.wait_ge(S("pt_done"), g + 1)
                if not (isinstance(g, int) and g < 2):
                    act.wait_ge(S("pv_done"), g - 1)
                w = P if t == PT else 640
                A_(prT[:, gp].rearrange("p k n -> p (k n)")[:, 0:w], banks(4, 2)[:, 0:w], ACT.Copy).then_inc(S("pt_a"), 1)

            def main(h):
                expo(h, 0)
                expo(h, 1)
                probT_evac(h, 0)
                expo(h, 2)
                probT_evac(h, 1)
                expo(h, 3)
                probT_evac(h, 2)
                expo(h, 4)
                probT_evac(h, 3)

            head_evac(fixed(0, 2))
            main(fixed(0, 2))
            with act.Fori(0, 3) as i:
                for u in (1, 2):
                    h = Step(i, 2, u)
                    head_evac(h)
                    probT_evac(h.plus(-1), 4)
                    main(h)
            head_evac(fixed(MH - 1, 2))
            probT_evac(fixed(MH - 2, 2), 4)
            main(fixed(MH - 1, 2))
            probT_evac(fixed(MH - 1, 2), 4)
            act.wait_ge(S("cache_out"), 32)

            def oT_evac(t):
                act.wait_ge(S("o_tr"), t + 1)
                if t >= 2:
                    act.wait_ge(S("mo_done"), 2 * t - 2)
                A_(oTb[:, t % 2, 0:4, :].rearrange("p k n -> p (k n)"), bank[2], ACT.Copy).then_inc(S("oTa"), 1)

            oT_evac(0)
            oT_evac(1)
            for t in range(NT):
                square(3, t)
                if t:
                    h2_evac(1, t - 1)
                if t + 2 < NT:
                    oT_evac(t + 2)
            moe(1)
            for t in range(NT):
                square(4, t)

        @block.vector
        def _(dve):
            v = nc.vector
            ch = Chain(dve, S("dve_step"))

            def cols2(ap, n):
                return ap.unsqueeze(2).to_broadcast([P, n, 2])

            def mod_first(l, hi):
                m = mod[:, l, 0:hi, :]
                ch.link(v.tensor_tensor(m, m, cols2(vt1[:, 48 * l:48 * l + hi], hi), ALU.add))
                v.scalar_tensor_tensor(out=a1[:, l], in0=mod[:, l, 8:16, :], scalar=1.0,
                                       in1=cols2(vt1[:, 96 + 8 * l:104 + 8 * l], 8), op0=ALU.add, op1=ALU.mult)\
                    .then_inc(S("modA"), 1)

            def mod_rest(l, lo):
                if lo < 48:
                    m = mod[:, l, lo:48, :]
                    ch.link(v.tensor_tensor(m, m, cols2(vt1[:, 48 * l + lo:48 * l + 48], 48 - lo), ALU.add))
                m = mod[:, l, 32:40, :]
                v.scalar_tensor_tensor(out=m, in0=m, scalar=1.0, in1=cols2(vt2[:, 8 * l:8 * l + 8], 8),
                                       op0=ALU.add, op1=ALU.mult).then_inc(S("modB"), 1)

            def h_evac(n, l, t):
                c = 1 if t == PT else 0
                dve.wait_ge(S("tr"), n * NT + t + 1)
                dve.wait_ge(S("modA"), l + 1)
                src = bank[T_BANK[n][t] + 1]
                for k in range(4):
                    ins = v.tensor_scalar(hT[:, 4 + k, tile_cols(t)], src[:, tile_cols(k)], a1[:, l, 4 + k, c:c + 1],
                                          mod[:, l, 4 + k, c:c + 1], ALU.mult, ALU.add)
                ins.then_inc(S("hTd"), 1)

            def normalise(t):
                dve.wait_ge(S("rstd"), t + 1)
                if t >= 2:
                    dve.wait_ge(S("tr"), t - 1)
                v.tensor_scalar(xn[0][:, t % 2, :], x[:, t, :], rs[:, t:t + 1], None, ALU.mult).then_inc(S("used"), 1)

            def h2_rows(l, t):
                n, c = 2 * l + 1, 1 if t == PT else 0
                if t == 0:
                    dve.wait_ge(S(f"rows_in{l}"), 96)
                dve.wait_ge(S("rstd"), n * NT + t + 1)
                if t >= 4:
                    dve.wait_ge(S("tr"), n * NT + t - 3)
                    dve.wait_ge(S("h2_first"), 16 * l + 16)
                hb = h2b[:, t % 4, :]
                v.scalar_tensor_tensor(out=hb, in0=x[:, t, :], scalar=rs[:, t:t + 1], in1=rows[:, 0, c, :],
                                       op0=ALU.mult, op1=ALU.mult).then_inc(S("used"), 1)
                dve.wait_ge(S("used"), n * NT + t + 1)
                v.tensor_tensor(hb, hb, rows[:, 1, c, :], ALU.add).then_inc(S("h2_ready"), 1)

            def h2_evac(l, t):
                dve.wait_ge(S("tr"), (2 * l + 1) * NT + t + 1)
                if t >= 2:
                    dve.wait_ge(S("router_mm"), l * NT + t - 1)
                v.tensor_copy(h2T[:, t % 2, 4:8, :].rearrange("p k n -> p (k n)"), bank[1]).then_inc(S("hTd"), 1)

            dve.wait_ge(S("gset"), 19)
            v.memset(cond[:, 16:46], 0.0).then_inc(S("pick2_set"), 1)
            v.tensor_reduce(pick2[:], ident[:].rearrange("p (g c) -> p c g", g=4)[:, 0:2, :], AX.X, ALU.add)\
                .then_inc(S("pick2_set"), 1)
            dve.wait_ge(S("vt_set"), 2)
            dve.wait_ge(S("proj_evac"), PRE)
            mod_first(0, 16)
            normalise(0)
            normalise(1)
            for t in range(NT):
                h_evac(0, 0, t)
                if t + 2 < NT:
                    normalise(t + 2)

            def op_evac(h):
                for t in range(NT):
                    c = 1 if t == PT else 0
                    for hf in range(2):
                        n = h * 10 + (2 * t + hf - 10)
                        dve.wait_ge(S("op_done"), n + 1)
                        if t or hf:
                            dve.wait_ge(S("x_add"), n)
                        v.tensor_tensor(t1, bank[6 + hf], g1[0][:, c, hf * 512:hf * 512 + 512], ALU.mult).then_inc(S("op_evac"), 1)
                        dve.wait_ge(S("op_evac"), n + 1)
                        xs = x[:, t, hf * 512:hf * 512 + 512]
                        v.tensor_tensor(xs, xs, t1, ALU.add).then_inc(S("x_add"), 1)
                    if isinstance(h, int):
                        if t:
                            h2_evac(0, t - 1)
                        h2_rows(0, t)

            def head(h):
                first = isinstance(h, int)
                chunks = CHUNKS_FIRST if first else CHUNKS_LOOP
                gate = use_plan(chunks)[0]
                b = use_base(h)

                def col(tile, r):
                    return tile[:, r * 4 + h:r * 4 + h + 1] if first else tile[:, bass.ds(h + r * 4, 1)]

                if not first:
                    op_evac(h)
                    dve.wait_ge(S("x_add"), h * 10)
                dve.wait_ge(S("att_done"), h * 2 + 1)
                for r in range(2):
                    m = mask[:, r * 4 + h:r * 4 + h + 1, :] if first else mask[:, bass.ds(h + r * 4, 1), :]
                    v.tensor_tensor(attm[:, r, 0:4, :], bank[4].rearrange("p (t n) -> p t n", t=4),
                                    m.to_broadcast([P, 4, P]), ALU.mult).then_inc(S("attm"), 1)
                dve.wait_ge(S("att_done"), h * 2 + 2)
                for r in range(2):
                    m = mask[:, r * 4 + h, :] if first else mask[:, bass.ds(h + r * 4, 1), :].rearrange("p a n -> p (a n)")
                    v.tensor_tensor(attm[:, r, 4, :], bank[5][:, 0:P], m, ALU.mult).then_inc(S("attm"), 1)

                def k_decay(u):
                    dve.wait_ge(S("kt_done"), h * NSS + u + 1)
                    if u >= 2:
                        dve.wait_ge(S("S_done"), h * NSS + u - 1)
                    v.tensor_scalar(kd[:, u % 2, :], bank[4][:, 0:DK], col(kdec, STEPS[STATE_STEPS[u]][1]), None,
                                    ALU.mult).then_inc(S("kd_ready"), 1)

                k_decay(0)
                dve.wait_ge(S("S_in"), h * 32 + 32)
                dve.wait_ge(S("gn_in"), h * 16 + 16)
                seen = set()
                for i, (t, r) in enumerate(STEPS):
                    if i in STATE_STEPS:
                        u = STATE_STEPS.index(i)
                        dve.wait_ge(S("S_done"), h * NSS + u + 1)
                        s = St[:, r].rearrange("p j d -> p (j d)")
                        if t == PT:
                            ins = v.tensor_copy(s, banks(6, 2))
                        else:
                            ins = v.scalar_tensor_tensor(out=s, in0=s, scalar=col(cdec, r), in1=banks(6, 2),
                                                         op0=ALU.mult, op1=ALU.add)
                        ins.then_inc(S("S_upd"), 1)
                        if u + 1 < NSS:
                            k_decay(u + 1)
                    dve.wait_ge(S("o_done"), h * 10 + i + 1)
                    ch.link(v.bn_stats(st6[:], bank[5]))
                    alone(dve)
                    v.bn_aggr(mv[:, i % 2, :], st6[:]).then_inc(S("stats"), 1)
                    dve.wait_ge(S("head_rstd"), h * 10 + i + 1)
                    v.tensor_scalar(t1, bank[5], mv[:, i % 2, 0:1], rv[:, i % 2:i % 2 + 1], ALU.subtract, ALU.mult)\
                        .then_inc(S("o_free"), 1)
                    dve.wait_ge(S("o_free"), h * 10 + i + 1)
                    ch.link(v.tensor_tensor(t1, t1, gn[:, r, :], ALU.mult))
                    dve.wait_ge(S("proj_evac"), b + gate[i] + 1)
                    if t not in seen:
                        seen.add(t)
                        v.tensor_tensor(yy[:, t, :], t1, sg[:, i % 2, :], ALU.mult).then_inc(S("ln_done"), 1)
                    else:
                        ch.link(v.tensor_tensor(t1, t1, sg[:, i % 2, :], ALU.mult))
                        v.tensor_tensor(yy[:, t, :], yy[:, t, :], t1, ALU.add).then_inc(S("ln_done"), 1)
                    dve.wait_ge(S("ln_done"), h * 10 + i + 1)

            dve.wait_ge(S("mask_tri"), 2)
            dve.wait_ge(S("decay_set"), 2)
            head(0)
            mod_rest(0, 16)
            dve.wait_ge(S("g1_in0"), 32)
            with dve.Fori(1, RH) as h:
                ch.c.enter(h, 1, 25)
                head(h)
            ch.c.leave(RH)
            mod_first(1, 48)
            mod_rest(1, 48)
            op_evac(RH)

            def moe(l):
                h2_evac(l, NT - 1)
                dve.wait_ge(S("misc_in"), 48)
                dve.wait_ge(S("sig_s"), l + 1)
                s, sbias, msk, chosen, oh1, oh2, tmp, tmp2 = rt[:8]
                grp = lambda ap: ap.rearrange("p t (g e) -> p (t g) e", g=NG)
                bc5 = lambda ap: ap.unsqueeze(1).to_broadcast([P, NT, NE])
                bce = lambda ap: ap.unsqueeze(2).to_broadcast([P, NT, NE])
                L = ch.link
                L(v.tensor_tensor(sbias, s, bc5(bias_row[:]), ALU.add))
                sgp = grp(sbias)
                L(v.tensor_tensor(pairs[:, :, 0:3], sgp[:, :, 0:3], sgp[:, :, 1:4], ALU.add))
                L(v.tensor_tensor(pairs[:, :, 3:5], sgp[:, :, 0:2], sgp[:, :, 2:4], ALU.add))
                L(v.tensor_tensor(pairs[:, :, 5:6], sgp[:, :, 0:1], sgp[:, :, 3:4], ALU.add))
                gsc, geq, gkey, gpen = rq[0], rq[1], rq[2], rq[3]
                gmx, gidx = rq[4][:, 0:NT], rq[5][:, 0:NT]
                t4 = lambda ap: ap.rearrange("p (t g) -> p t g", g=NG)
                b4 = lambda ap: ap.unsqueeze(2).to_broadcast([P, NT, NG])
                L(v.tensor_reduce(gsc, pairs, AX.X, ALU.max))
                L(v.tensor_reduce(gmx, t4(gsc), AX.X, ALU.max))
                L(v.tensor_tensor(t4(geq), t4(gsc), b4(gmx), ALU.is_equal))
                g5 = lambda ap: ap.unsqueeze(1).to_broadcast([P, NT, NG])
                L(v.scalar_tensor_tensor(out=t4(gkey), in0=t4(geq), scalar=-100.0, in1=g5(idx16p[:, 0:NG]),
                                         op0=ALU.mult, op1=ALU.add))
                L(v.tensor_reduce(gidx, t4(gkey), AX.X, ALU.min))
                L(v.tensor_tensor(t4(geq), g5(idx16[:, 0:NG]), b4(gidx), ALU.is_equal))
                L(v.tensor_scalar(gpen, geq, BIG, -BIG, ALU.mult, ALU.add))
                L(v.tensor_tensor(grp(msk), sgp, gpen.unsqueeze(2).to_broadcast([P, NT * NG, 4]), ALU.add))

                def top(src, oh):
                    mx, ix = rq[6][:, 0:NT], rq[7][:, 0:NT]
                    L(v.tensor_reduce(mx, src, AX.X, ALU.max))
                    L(v.tensor_tensor(tmp, src, bce(mx), ALU.is_equal))
                    L(v.scalar_tensor_tensor(out=tmp2, in0=tmp, scalar=-100.0, in1=bc5(idx16p[:]), op0=ALU.mult, op1=ALU.add))
                    L(v.tensor_reduce(ix, tmp2, AX.X, ALU.min))
                    L(v.tensor_tensor(oh, bc5(idx16[:]), bce(ix), ALU.is_equal))
                top(msk, oh1)
                L(v.scalar_tensor_tensor(out=msk, in0=oh1, scalar=-BIG, in1=msk, op0=ALU.mult, op1=ALU.add))
                top(msk, oh2)
                v.tensor_tensor(chosen, oh1, oh2, ALU.add).then_inc(S("sel"), 1)
                for j, oh in enumerate((oh1, oh2)):
                    L(v.tensor_tensor(tmp, s, oh, ALU.mult))
                    L(v.tensor_reduce(wts[:, j, :], tmp, AX.X, ALU.add))
                L(v.tensor_tensor(wts[:, 2, :], wts[:, 0, :], wts[:, 1, :], ALU.add))
                L(v.reciprocal(wts[:, 2, :], wts[:, 2, :]))
                for j, oh in enumerate((oh1, oh2)):
                    L(v.tensor_tensor(wts[:, j, :], wts[:, j, :], wts[:, 2, :], ALU.mult))
                    L(v.tensor_tensor(sent[:, NT * j:NT * j + NT, 0, :], bce(tok_f[:]), oh, ALU.mult))
                    L(v.tensor_tensor(sent[:, NT * j:NT * j + NT, 1, :], bce(wts[:, j, :]), oh, ALU.mult))
                rank, slot, blk = rq[8][:, 0:10], rq[9][:, 0:10], rq[10][:, 0:10]
                dve.wait_ge(S("rank_done"), l + 1)
                for j, oh in enumerate((oh1, oh2)):
                    L(v.tensor_tensor(tmp2, bank[5][:, 0:NT * NE].rearrange("p (t e) -> p t e", t=NT), oh, ALU.mult))
                    L(v.tensor_reduce(rank[:, 5 * j:5 * j + 5], tmp2, AX.X, ALU.add))
                v.tensor_tensor(onehot, row_no[:].unsqueeze(1).to_broadcast([P, 2 * NT, P]),
                                rank.unsqueeze(2).to_broadcast([P, 2 * NT, P]), ALU.is_equal).then_inc(S("onehot"), 1)
                L(v.tensor_reduce(tmp2[:, 0, :], bank[5][:, NT * NE:2 * NT * NE].rearrange("p (t e) -> p e t", t=NT), AX.X, ALU.add))
                L(v.tensor_reduce(cntf[:], tmp2[:, 0, :], AX.X, ALU.max))
                v.tensor_copy(cnt[:], cntf[:]).then_inc(S("cnt_ready"), 1)
                dve.wait_ge(S("ids_mm"), l + 1)
                v.tensor_copy(slot_w[:], bank[6][:, 16:32])
                v.tensor_copy(ids[:], bank[6][:, 0:16]).then_inc(S("ids_ready"), 1)
                dve.wait_ge(S("ids_ready"), l + 1)

                def slots_of_tokens():
                    for j, oh in enumerate((oh1, oh2)):
                        L(v.tensor_tensor(tmp2, bc5(ebase[:]), oh, ALU.mult))
                        L(v.tensor_reduce(slot[:, 5 * j:5 * j + 5], tmp2, AX.X, ALU.add))
                    L(v.tensor_tensor(slot, slot, rank, ALU.add))
                    L(v.tensor_scalar(blk, rank, float(BLK), None, ALU.is_ge))
                    for n_ in range(2, CAP // BLK):
                        L(v.scalar_tensor_tensor(out=blk, in0=rank, scalar=float(n_ * BLK), in1=blk, op0=ALU.is_ge, op1=ALU.add))
                    L(v.scalar_tensor_tensor(out=slot, in0=blk, scalar=float(NE * BLK - BLK), in1=slot,
                                             op0=ALU.mult, op1=ALU.add))
                    v.tensor_copy(slots[:].rearrange("p j t -> p (j t)"), slot).then_inc(S("slots_ready"), 1)
                slots_of_tokens()

                def x_evac(e):
                    dve.wait_ge(S("tr_done"), l * NE + e.n + 1)
                    if not (isinstance(e.n, int) and e.n < 2):
                        dve.wait_ge(S("gu_done"), l * NE + e.n - 1)
                    v.tensor_copy(xgT[:, e.par, 4:8, :].rearrange("p k n -> p (k n)"), bank[1]).then_inc(S("xd"), 1)

                def act_mul(e):
                    dve.wait_ge(S("silu"), l * NE + e.n + 1)
                    alone(dve)
                    w = slot_w[:, e.n:e.n + 1] if isinstance(e.n, int) else slot_w[:, bass.ds(e.n, 1)]
                    v.scalar_tensor_tensor(out=gact[:, e.par, :], in0=bank[2][:, FF:2 * FF], scalar=w, in1=gact[:, e.par, :],
                                           op0=ALU.mult, op1=ALU.mult).then_inc(S("act"), 1)

                def y_evac(e):
                    dve.wait_ge(S("down_done"), l * NE + e.n + 1)
                    if not (isinstance(e.n, int) and e.n < 2):
                        dve.wait_ge(S(f"y_out{e.par}"), l * 128 + e.half * 16)
                    v.tensor_copy(ysb[:, e.par, 512:1024], bank[5 + 2 * e.par]).then_inc(S("yd"), 1)

                def one(e):
                    static = isinstance(e.n, int)
                    act_mul(e)
                    if not (static and e.n == NE - 1):
                        x_evac(e.plus(1))
                    if not (static and e.n == 0):
                        y_evac(e.plus(-1))

                x_evac(fixed(0, 4))
                for u in range(3):
                    one(fixed(u, 4))
                with dve.Fori(0, 3) as i:
                    for u in range(3, 7):
                        one(Step(i, 4, u))
                one(fixed(NE - 1, 4))
                y_evac(fixed(NE - 1, 4))
                overflow(dve, l)
                for t in range(NT):
                    c = 1 if t == PT else 0
                    dve.wait_ge(S(f"pick{t}"), 32 * l + 32)
                    L(v.tensor_tensor(picked[t], picked[t], rows[:, 2, c, :], ALU.mult))
                    v.tensor_tensor(x[:, t, :], x[:, t, :], picked[t], ALU.add).then_inc(S("comb"), 1)
                    if l == 0 and 2 <= t < 4:
                        h_evac(2, 1, t - 2)
                    if l == 1 and t:
                        final(t - 1)

            def final(t):
                if t == 0:
                    dve.wait_ge(S("misc_in"), 64)
                dve.wait_ge(S("rstd"), 4 * NT + t + 1)
                dve.wait_ge(S("comb"), NT + t + 1)
                if t >= 2:
                    dve.wait_ge(S(f"fin_out{t % 2}"), 16 * (t // 2))
                v.scalar_tensor_tensor(out=fin[:, t % 2, :], in0=x[:, t, :], scalar=rs[:, t:t + 1], in1=fin_row,
                                       op0=ALU.mult, op1=ALU.mult).then_inc(S("fin_ready"), 1)

            moe(0)


            def latent(t):
                b0 = 4 + 2 * (t % 2)
                dve.wait_ge(S("lat_rstd"), 2 * t + 2)
                if t >= 2:
                    dve.wait_ge(S("lat_tr"), t - 1)
                v.tensor_scalar(cqn[:, t % 2, :], bank[b0], rv[:, 0:1], None, ALU.mult)
                kv = bank[b0 + 1]
                v.scalar_tensor_tensor(out=ckvn[:, t % 2, :], in0=kv[:, 0:KVR], scalar=rv[:, 1:2], in1=kv_row[:],
                                       op0=ALU.mult, op1=ALU.mult)
                ax = lambda ap: ap.rearrange("p (a o n) -> p a o n", a=2, o=2)
                kp, sn, m = ax(kv[:, KVR:KVR + 64]), ax(tab[:, 1, t, :]), ax(kro[:, 64:128])
                v.tensor_tensor(kro[:, 0:64], kv[:, KVR:KVR + 64], tab[:, 0, t, :], ALU.mult)
                for o in range(2):
                    ins = v.tensor_tensor(m[:, :, o, :], kp[:, :, 1 - o, :], sn[:, :, o, :], ALU.mult)
                ins.then_inc(S("lat_used"), 1)
                dve.wait_ge(S("lat_used"), t + 1)
                for o in range(2):
                    ins = v.tensor_tensor(kr[:, t % 2, o * 64:o * 64 + 64], kro[:, 0:64], kro[:, 64:128], ALU.add)
                ins.then_inc(S("kr_ready"), 1)
                dve.wait_ge(S("kr_ready"), t + 1)

            def lat_evac_d(t):
                b1 = 3
                cols = key_cols(t) if t < NT else slice(512, 640)
                dve.wait_ge(S("lat_tr"), t + 1)
                v.tensor_copy(ckT[:, :, cols], bank[b1][:, 0:256].rearrange("p (j n) -> p j n", j=2))
                v.tensor_copy(kpT[:, cols], bank[b1][:, 256:384]).then_inc(S("lat_Td"), 1)

            for t in range(NT):
                if t == 0:
                    h_evac(2, 1, 2)
                    dve.wait_ge(S("tab_in"), 80)
                    dve.wait_ge(S("misc_in"), 48)
                latent(t)
                if t:
                    lat_evac_d(t - 1)
                if t + 3 < NT:
                    h_evac(2, 1, t + 3)
            lat_evac_d(NT - 1)
            lat_evac_d(NT)
            for kt in range(6):
                dve.wait_ge(S("v_done"), 2 * kt + 2)
                v.tensor_copy(V[:, kt, 512:1024], bank[4 + (2 * kt + 1) % 4]).then_inc(S("vd"), 1)
            SCALE = (NOPE + ROPE) ** -0.5

            def head_evac(h):
                p = h.par
                dve.wait_ge(S("hp_done"), h.n * 4 + 2)
                v.tensor_tensor(qpT[:, p, 0:TS], bank[2], CS[:, 0:TS], ALU.mult).then_inc(S("hp_d"), 1)
                dve.wait_ge(S("hp_done"), h.n * 4 + 4)
                v.tensor_copy(qnT[:, p, TS:T], bank[7][:, 0:128])
                v.tensor_tensor(qpT[:, p, TS:T], bank[7][:, 128:256], CS[:, TS:T], ALU.mult)
                v.tensor_copy(knT[:, p, 512:768], bank[7][:, 256:512]).then_inc(S("hp_d"), 1)

            def row_max(h, t):
                g, gp = h.n * 5 + t, (h.par + t) % 2
                w = P if t == PT else 640
                dve.wait_ge(S("sc_done"), g + 1)
                ch.link(v.tensor_reduce(smx[:, gp:gp + 1], banks(2 * (t % 2), 2)[:, 0:w], AX.X, ALU.max))
                if not (isinstance(g, int) and g < 2):
                    dve.wait_ge(S("ex_done"), g - 1)
                v.tensor_scalar(nmx[:, gp:gp + 1], smx[:, gp:gp + 1], -SCALE, None, ALU.mult).then_inc(S("mx"), 1)

            def recip(h, t):
                dve.wait_ge(S("ex_done"), h.n * 5 + t + 1)
                ch.link(v.reciprocal(sm_inv[:, t:t + 1], sm_sum[:, t:t + 1]))

            def o_evac(h, t):
                dve.wait_ge(S("pv_done"), h.n * 5 + t + 1)
                dst = o_all[:, t, h.n * VD:h.n * VD + VD] if isinstance(h.n, int) else o_all[:, t, bass.ds(h.n * VD, VD)]
                v.tensor_scalar(dst, bank[6][:, 0:VD], sm_inv[:, t:t + 1], None, ALU.mult).then_inc(S("o_ev"), 1)

            def main(h):
                row_max(h, 0)
                row_max(h, 1)
                recip(h, 0)
                row_max(h, 2)
                recip(h, 1)
                o_evac(h, 0)
                row_max(h, 3)
                recip(h, 2)
                o_evac(h, 1)
                row_max(h, 4)
                recip(h, 3)
                o_evac(h, 2)

            def tail(h):
                recip(h, 4)
                o_evac(h, 3)
                o_evac(h, 4)

            head_evac(fixed(0, 2))
            main(fixed(0, 2))
            with dve.Fori(0, 3) as i:
                ch.c.enter(i, 0, 20)
                for u in (1, 2):
                    h = Step(i, 2, u)
                    head_evac(h)
                    tail(h.plus(-1))
                    main(h)
            ch.c.leave(3)
            head_evac(fixed(MH - 1, 2))
            tail(fixed(MH - 2, 2))
            main(fixed(MH - 1, 2))
            tail(fixed(MH - 1, 2))
            dve.wait_ge(S("g1_in1"), 32)

            def oT_evac(t):
                dve.wait_ge(S("o_tr"), t + 1)
                if t >= 2:
                    dve.wait_ge(S("mo_done"), 2 * t - 2)
                v.tensor_copy(oTb[:, t % 2, 4:8, :].rearrange("p k n -> p (k n)"), bank[3]).then_inc(S("oTd"), 1)
            oT_evac(0)
            for t in range(NT):
                c = 1 if t == PT else 0
                if t + 1 < NT:
                    oT_evac(t + 1)
                for hf in range(2):
                    n = 2 * t + hf
                    dve.wait_ge(S("mo_done"), n + 1)
                    dve.wait_ge(S("mx_add"), n)
                    v.tensor_tensor(mtmp, bank[4 + hf], g1[1][:, c, hf * 512:hf * 512 + 512], ALU.mult)\
                        .then_inc(S("mo_evac"), 1)
                    dve.wait_ge(S("mo_evac"), n + 1)
                    xs = x[:, t, hf * 512:hf * 512 + 512]
                    v.tensor_tensor(xs, xs, mtmp, ALU.add).then_inc(S("mx_add"), 1)
                if t:
                    h2_evac(1, t - 1)
                h2_rows(1, t)
            moe(1)
            final(NT - 1)


_INS = ["x_prompt", "x_sample", "state_ret_fwd", "state_ret_bwd", "cache_mla_ckv", "cache_mla_kpe", "c", "c_ctx",
        "w_ada", "b_ada", "norm1", "norm2", "norm_final", "ret_w_in", "ret_decay", "ret_gn", "ret_w_out",
        "mla_w_in", "mla_q_norm", "mla_kv_norm", "mla_w_uq", "mla_w_uk", "mla_w_uv", "mla_w_o",
        "w_router", "router_bias", "moe_w_gate", "moe_w_up", "moe_w_down"]
_OUTS = [(1, P, D), (1, TS, D), (1, 1, RH, DK, DV), (1, 1, RH, DK, DV), (1, 1, P, KVR), (1, 1, P, ROPE)]


def rope_tables():
    f = np.float32
    pos = np.arange(TS)
    row, col = (pos // 64).astype(f), (pos % 64).astype(f)
    half_w = ROPE // 2
    inv = (f(10000.0) ** (-np.arange(0, half_w, 2, dtype=f) / f(half_w))).astype(f)
    ang = np.stack([row[:, None] * inv, col[:, None] * inv], axis=1)
    cos = np.stack([np.cos(ang), np.cos(ang)], axis=2).reshape(TS, 64)
    sin = np.stack([-np.sin(ang), np.sin(ang)], axis=2).reshape(TS, 64)
    cos = np.concatenate([cos, np.ones((P, 64))]).astype(f)
    sin = np.concatenate([sin, np.zeros((P, 64))]).astype(f)
    cs = np.concatenate([cos, sin], axis=1).T
    tabs = np.stack([cos.reshape(NT, P, 64), sin.reshape(NT, P, 64)])
    return np.ascontiguousarray(cs), np.ascontiguousarray(tabs.transpose(2, 0, 1, 3).reshape(P, 2 * NT * 64))


def kernel(**inputs):
    import concourse.bacc as bacc
    from concourse.bass_utils import run_bass_kernel_spmd as run

    nc = bacc.Bacc("TRN2", target_bir_lowering=False, num_devices=1)
    arrays, a = {}, {}
    for name in _INS:
        arr = np.ascontiguousarray(inputs[name])
        arrays[f"in_{name}"] = arr
        a[name] = nc.dram_tensor(f"in_{name}", arr.shape, F32, kind="ExternalInput").ap()
    for name, arr in zip(("rope_cs", "rope_tab"), rope_tables()):
        arrays[f"in_{name}"] = arr
        a[name] = nc.dram_tensor(f"in_{name}", arr.shape, F32, kind="ExternalInput").ap()
    a["mod_rows_dram"] = nc.dram_tensor("mod_rows_dram", (2, 48, 2, P), F32, kind="Internal").ap()
    for key, shape, dt in (("h2_dram", (T, D), F32), ("slot_tok_dram", (NE * CAP, 1), I32), ("y_dram", (NE * CAP, D), F32),
                            ("gate_dram", (T, NE), F32)):
        a[key] = [nc.dram_tensor(f"{key}{l}", shape, dt, kind="Internal").ap() for l in range(2)]
    out = [nc.dram_tensor(f"out_{i}", s, F32, kind="ExternalOutput").ap() for i, s in enumerate(_OUTS)]
    build(nc, a, out)
    r = run(nc, [arrays], core_ids=[0])
    return tuple(r.results[0][f"out_{i}"] for i in range(len(_OUTS)))
```
